# Optimizing a Trainium2 kernel written in Bass

```python
import jax, jax.numpy as jnp
from jax import lax
import numpy as np

D_MODEL = 1024
BATCH = 1
SEQ = 1024
DEPTH = 1

GRID_W = 64
CTX_LEN = 256
N_HEADS = 8
N_KV_HEADS = 2
HEAD_DIM = 128
Q_PER_KV = N_HEADS // N_KV_HEADS
ATTN_WIDTH = N_HEADS * HEAD_DIM
KV_WIDTH = N_KV_HEADS * HEAD_DIM
WINDOW = 128
BLOCK = 128
ROPE_THETA = 10000.0
D_RNN = D_MODEL
N_LRU_BLOCKS = 16
LRU_BLOCK = D_RNN // N_LRU_BLOCKS
LRU_C = 8.0
LRU_CONV_W = 4
LRU_CONV_LEFT = 2
N_DIRS = 2
D_FF = 3 * D_MODEL
FFN_CONV_W = 3
N_MOD = 6
EPS = 1e-6
NEG_INF = -1e30
IN_SPLITS = (D_RNN, D_RNN, ATTN_WIDTH, KV_WIDTH, KV_WIDTH, D_MODEL, D_MODEL)
D_IN = sum(IN_SPLITS)

kernel_name = 'hybrid_rglru_swa_convffn_prefix_dit'

def rms_norm(x, w):
    xf = x.astype(jnp.float32)
    y = xf * lax.rsqrt(jnp.mean(xf * xf, axis=-1, keepdims=True) + EPS)
    return (y * w.astype(jnp.float32)).astype(x.dtype)

def modulate(h, shift, scale):
    return h * (1.0 + scale) + shift

def dwconv(x, w, b, left):
    k_w, ch = w.shape
    y = lax.conv_general_dilated(x, w[:, None, :], window_strides=(1,), padding=[(left, k_w - 1 - left)],
                                 dimension_numbers=('NWC', 'WIO', 'NWC'), feature_group_count=ch)
    return y + b

def split_cols(p):
    idx = np.cumsum(IN_SPLITS)[:-1].tolist()
    return jnp.split(p, idx, axis=-1)

def linear_scan(a, b, h0):
    b = b.at[:, 0].add(a[:, 0] * h0)
    def combine(l, r):
        return (l[0] * r[0], r[0] * l[1] + r[1])
    return lax.associative_scan(combine, (a, b), axis=1)[1]

def rglru_dir(xc, w_a, b_a, w_x, b_x, lam, h0):
    bsz, length, ch = xc.shape
    xf = xc.astype(jnp.float32)
    xg = xf.reshape(bsz, length, N_LRU_BLOCKS, LRU_BLOCK)
    r = jax.nn.sigmoid(jnp.einsum('blnc,ncd->blnd', xg, w_a.astype(jnp.float32)).reshape(bsz, length, ch)
                       + b_a.astype(jnp.float32))
    i = jax.nn.sigmoid(jnp.einsum('blnc,ncd->blnd', xg, w_x.astype(jnp.float32)).reshape(bsz, length, ch)
                       + b_x.astype(jnp.float32))
    log_a = -LRU_C * r * jax.nn.softplus(-lam.astype(jnp.float32))
    a = jnp.exp(log_a)
    b = jnp.sqrt(-jnp.expm1(2.0 * log_a)) * (i * xf)
    return linear_scan(a, b, h0)

def rglru_states(xr, conv_w, conv_b, w_a, b_a, w_x, b_x, lam, h0_f, h0_b):
    xc = dwconv(xr, conv_w, conv_b, LRU_CONV_LEFT)
    h_f = rglru_dir(xc, w_a[0], b_a[0], w_x[0], b_x[0], lam[0], h0_f)
    h_b = jnp.flip(rglru_dir(jnp.flip(xc, axis=1), w_a[1], b_a[1], w_x[1], b_x[1], lam[1], h0_b), axis=1)
    return h_f, h_b

def rglru_output(h_f, h_b, gate, dtype):
    return ((h_f + h_b) * jax.nn.gelu(gate.astype(jnp.float32))).astype(dtype)

def axial_rope_tables(length):
    rows = length // GRID_W
    row = jnp.repeat(jnp.arange(rows), GRID_W)
    col = jnp.tile(jnp.arange(GRID_W), rows)
    half = HEAD_DIM // 2
    inv = ROPE_THETA ** (-jnp.arange(0, half, 2, dtype=jnp.float32) / half)
    ang = jnp.stack([row[:, None] * inv, col[:, None] * inv], axis=1)
    return jnp.cos(ang), jnp.sin(ang)

def apply_rope(x, cos, sin):
    bsz, length, heads, _ = x.shape
    xr = x.astype(jnp.float32).reshape(bsz, length, heads, 2, 2, HEAD_DIM // 4)
    x1, x2 = xr[..., 0, :], xr[..., 1, :]
    cs, sn = cos[None, :, None], sin[None, :, None]
    out = jnp.stack([x1 * cs - x2 * sn, x2 * cs + x1 * sn], axis=-2)
    return out.reshape(bsz, length, heads, HEAD_DIM)

def windowed_attention(q, k, v, kc, vc, sink):
    bsz, length = q.shape[:2]
    nb = length // BLOCK
    qb = (q * HEAD_DIM ** -0.5).reshape(bsz, nb, BLOCK, N_KV_HEADS, Q_PER_KV, HEAD_DIM)

    def neighbours(t):
        tb = t.reshape(bsz, nb, BLOCK, N_KV_HEADS, HEAD_DIM)
        tp = jnp.pad(tb, ((0, 0), (1, 1), (0, 0), (0, 0), (0, 0)))
        return jnp.concatenate([tp[:, :-2], tp[:, 1:-1], tp[:, 2:]], axis=2)

    kw, vw = neighbours(k), neighbours(v)
    s_loc = jnp.einsum('bnqkgd,bnjkd->bnkgqj', qb, kw)
    blk = jnp.arange(nb)[:, None, None]
    qpos = blk * BLOCK + jnp.arange(BLOCK)[None, :, None]
    kpos = (blk - 1) * BLOCK + jnp.arange(3 * BLOCK)[None, None, :]
    valid = (jnp.abs(kpos - qpos) <= WINDOW) & (kpos >= 0) & (kpos < length)
    s_loc = jnp.where(valid[None, :, None, None], s_loc, NEG_INF)
    s_ctx = jnp.einsum('bnqkgd,bckd->bnkgqc', qb, kc)
    sink_l = sink.astype(jnp.float32).reshape(1, 1, N_KV_HEADS, Q_PER_KV, 1)
    m = jnp.maximum(jnp.maximum(s_loc.max(-1), s_ctx.max(-1)), sink_l)
    p_loc = jnp.exp(s_loc - m[..., None])
    p_ctx = jnp.exp(s_ctx - m[..., None])
    denom = p_loc.sum(-1) + p_ctx.sum(-1) + jnp.exp(sink_l - m)
    o = jnp.einsum('bnkgqj,bnjkd->bnkgqd', p_loc, vw) + jnp.einsum('bnkgqc,bckd->bnkgqd', p_ctx, vc)
    o = o / denom[..., None]
    return o.transpose(0, 1, 4, 2, 3, 5).reshape(bsz, length, ATTN_WIDTH)

def context_attention(qc, kc, vc, sink):
    bsz, clen = qc.shape[:2]
    q = (qc * HEAD_DIM ** -0.5).reshape(bsz, clen, N_KV_HEADS, Q_PER_KV, HEAD_DIM)
    s = jnp.einsum('bqkgd,bckd->bkgqc', q, kc)
    sink_l = sink.astype(jnp.float32).reshape(1, N_KV_HEADS, Q_PER_KV, 1)
    m = jnp.maximum(s.max(-1), sink_l)
    p = jnp.exp(s - m[..., None])
    denom = p.sum(-1) + jnp.exp(sink_l - m)
    o = jnp.einsum('bkgqc,bckd->bkgqd', p, vc) / denom[..., None]
    return o.transpose(0, 3, 1, 2, 4).reshape(bsz, clen, ATTN_WIDTH)

def merge_branches(y_rnn, y_attn, g_rnn, g_attn, w_o_rnn, w_o_attn, w_out):
    y = jax.nn.sigmoid(g_rnn) * (y_rnn @ w_o_rnn) + jax.nn.sigmoid(g_attn) * (y_attn @ w_o_attn)
    return y @ w_out

def conv_ffn(h, w_up, conv_w, conv_b, w_down):
    u = dwconv(h @ w_up, conv_w, conv_b, FFN_CONV_W // 2)
    a, v = jnp.split(u, 2, axis=-1)
    return (jax.nn.gelu(a) * v) @ w_down

def setup_inputs(seed: int = 0) -> dict:
    key = jax.random.key(seed)
    ks = jax.random.split(key, 32)

    def nrm(k, shape, scale):
        return jax.random.normal(k, shape, jnp.float32) * scale

    u = jax.random.uniform(ks[14], (DEPTH, N_DIRS, D_RNN), jnp.float32, 0.9, 0.999)
    a0 = u ** (1.0 / LRU_C)
    return {
        'x': nrm(ks[0], (BATCH, SEQ, D_MODEL), 1.0),
        'c': nrm(ks[1], (BATCH, D_MODEL), 1.0),
        'ctx': nrm(ks[2], (BATCH, CTX_LEN, D_MODEL), 1.0),
        'c_ctx': nrm(ks[3], (D_MODEL,), 1.0),
        'w_mod': nrm(ks[4], (DEPTH, D_MODEL, N_MOD * D_MODEL), 0.5 * D_MODEL ** -0.5),
        'b_mod': nrm(ks[5], (DEPTH, N_MOD * D_MODEL), 0.02),
        'norm1_w': 1.0 + nrm(ks[6], (DEPTH, D_MODEL), 0.02),
        'w_in': nrm(ks[7], (DEPTH, D_MODEL, D_IN), D_MODEL ** -0.5),
        'lru_conv_w': nrm(ks[8], (DEPTH, LRU_CONV_W, D_RNN), LRU_CONV_W ** -0.5),
        'lru_conv_b': nrm(ks[9], (DEPTH, D_RNN), 0.02),
        'gate_a_w': nrm(ks[10], (DEPTH, N_DIRS, N_LRU_BLOCKS, LRU_BLOCK, LRU_BLOCK), LRU_BLOCK ** -0.5),
        'gate_a_b': nrm(ks[11], (DEPTH, N_DIRS, D_RNN), 0.02),
        'gate_x_w': nrm(ks[12], (DEPTH, N_DIRS, N_LRU_BLOCKS, LRU_BLOCK, LRU_BLOCK), LRU_BLOCK ** -0.5),
        'gate_x_b': nrm(ks[13], (DEPTH, N_DIRS, D_RNN), 0.02),
        'lru_lambda': jnp.log(a0) - jnp.log1p(-a0),
        'sink_logit': nrm(ks[15], (DEPTH, N_HEADS), 0.5),
        'w_o_rnn': nrm(ks[16], (DEPTH, D_RNN, D_MODEL), D_RNN ** -0.5),
        'w_o_attn': nrm(ks[17], (DEPTH, ATTN_WIDTH, D_MODEL), ATTN_WIDTH ** -0.5),
        'w_out': nrm(ks[18], (DEPTH, D_MODEL, D_MODEL), D_MODEL ** -0.5),
        'norm2_w': 1.0 + nrm(ks[19], (DEPTH, D_MODEL), 0.02),
        'w_up': nrm(ks[20], (DEPTH, D_MODEL, 2 * D_FF), D_MODEL ** -0.5),
        'ffn_conv_w': nrm(ks[21], (DEPTH, FFN_CONV_W, 2 * D_FF), FFN_CONV_W ** -0.5),
        'ffn_conv_b': nrm(ks[22], (DEPTH, 2 * D_FF), 0.02),
        'w_down': nrm(ks[23], (DEPTH, D_FF, D_MODEL), D_FF ** -0.5),
        'final_norm_w': 1.0 + nrm(ks[24], (D_MODEL,), 0.02),
    }

def reference(x, c, ctx, c_ctx, w_mod, b_mod, norm1_w, w_in, lru_conv_w, lru_conv_b, gate_a_w, gate_a_b,
              gate_x_w, gate_x_b, lru_lambda, sink_logit, w_o_rnn, w_o_attn, w_out, norm2_w, w_up,
              ffn_conv_w, ffn_conv_b, w_down, final_norm_w):
    bsz, length, _ = x.shape
    cos, sin = axial_rope_tables(length)
    silu_c = jax.nn.silu(c)
    silu_cc = jax.nn.silu(c_ctx)
    for l in range(DEPTH):
        last = l == DEPTH - 1
        mod_x = (silu_c @ w_mod[l] + b_mod[l])[:, None, :]
        mod_c = (silu_cc @ w_mod[l] + b_mod[l])[None, None, :]
        sh1, sc1, g1, sh2, sc2, g2 = jnp.split(mod_x, N_MOD, axis=-1)
        csh1, csc1, cg1, csh2, csc2, cg2 = jnp.split(mod_c, N_MOD, axis=-1)

        hx = modulate(rms_norm(x, norm1_w[l]), sh1, sc1)
        hc = modulate(rms_norm(ctx, norm1_w[l]), csh1, csc1)
        rx, rgx, qx, kx, vx, gax, gbx = split_cols(hx @ w_in[l])
        rc, rgc, qc, kc, vc, gac, gbc = split_cols(hc @ w_in[l])

        lru = (lru_conv_w[l], lru_conv_b[l], gate_a_w[l], gate_a_b[l], gate_x_w[l], gate_x_b[l], lru_lambda[l])
        zeros = jnp.zeros((bsz, D_RNN), jnp.float32)
        hf_c, hb_c = rglru_states(rc, *lru, zeros, zeros)
        hf_x, hb_x = rglru_states(rx, *lru, hf_c[:, -1], hb_c[:, 0])
        y_rx = rglru_output(hf_x, hb_x, rgx, x.dtype)

        kc_h = kc.reshape(bsz, CTX_LEN, N_KV_HEADS, HEAD_DIM).astype(jnp.float32)
        vc_h = vc.reshape(bsz, CTX_LEN, N_KV_HEADS, HEAD_DIM).astype(jnp.float32)
        q_lat = apply_rope(qx.reshape(bsz, length, N_HEADS, HEAD_DIM), cos, sin)
        k_lat = apply_rope(kx.reshape(bsz, length, N_KV_HEADS, HEAD_DIM), cos, sin)
        v_lat = vx.reshape(bsz, length, N_KV_HEADS, HEAD_DIM).astype(jnp.float32)
        y_ax = windowed_attention(q_lat, k_lat, v_lat, kc_h, vc_h, sink_logit[l]).astype(x.dtype)

        x = x + g1 * merge_branches(y_rx, y_ax, gax, gbx, w_o_rnn[l], w_o_attn[l], w_out[l])
        hx2 = modulate(rms_norm(x, norm2_w[l]), sh2, sc2)
        x = x + g2 * conv_ffn(hx2, w_up[l], ffn_conv_w[l], ffn_conv_b[l], w_down[l])

        if not last:
            y_rc = rglru_output(hf_c, hb_c, rgc, ctx.dtype)
            qc_h = qc.reshape(bsz, CTX_LEN, N_HEADS, HEAD_DIM).astype(jnp.float32)
            y_ac = context_attention(qc_h, kc_h, vc_h, sink_logit[l]).astype(ctx.dtype)
            ctx = ctx + cg1 * merge_branches(y_rc, y_ac, gac, gbc, w_o_rnn[l], w_o_attn[l], w_out[l])
            hc2 = modulate(rms_norm(ctx, norm2_w[l]), csh2, csc2)
            ctx = ctx + cg2 * conv_ffn(hc2, w_up[l], ffn_conv_w[l], ffn_conv_b[l], w_down[l])
    return rms_norm(x, final_norm_w)


_drawn_inputs = setup_inputs


def setup_inputs(seed=0):
    import zlib

    import numpy as np

    out = dict(_drawn_inputs(seed))
    spreads = {}
    factors = {'ctx': 2.918,
     'norm1_w': 6.571,
     'gate_a_b': 21.744,
     'gate_x_b': 8.0,
     'sink_logit': 8.0,
     'norm2_w': 8.0,
     'ffn_conv_b': 8.0,
     'final_norm_w': 8.028}
    for name, (base, spread) in spreads.items():
        noise = np.random.default_rng([zlib.crc32(name.encode()), seed]).standard_normal(out[name].shape)
        drawn = base * np.exp(spread * noise) if base else spread * noise
        out[name] = __import__('jax').numpy.asarray(drawn.astype(out[name].dtype))
    for name, factor in factors.items():
        out[name] = (out[name] * factor).astype(out[name].dtype)
    return out
```

```python
import numpy as np
import concourse.bass as bass
from concourse import mybir
from contextlib import ExitStack

P = 128
D_MODEL, SEQ, CTX = 1024, 1024, 256
GRID_W, N_HEADS, HEAD_DIM, N_KV = 64, 8, 128, 2
Q_PER_KV = N_HEADS // N_KV
KV_WIDTH = N_KV * HEAD_DIM
D_FF = 3 * D_MODEL
LRU_BLOCK, LRU_C, N_MOD = 64, 8.0, 6
EPS, NEG = 1e-6, -1e30
ROPE_THETA = 10000.0
KC = D_MODEL // P
XT = SEQ // P
TT = XT + CTX // P
ALL = CTX + SEQ
HALF = 512
FC = D_FF // P
GRP = 3
NG = FC // GRP
REST = (N_MOD - 2) * D_MODEL
COL_R, COL_RG, COL_Q = 0, D_MODEL, 2 * D_MODEL
COL_K = 3 * D_MODEL
COL_V = COL_K + KV_WIDTH
COL_GA = COL_V + KV_WIDTH
COL_GB = COL_GA + D_MODEL

C_C, C_CCTX, C_N1, C_BMOD, C_LCW, C_LCB = 0, 8, 16, 24, 72, 104
C_GAB, C_GXB, C_LAM, C_N2, C_FN, C_FCB = 112, 128, 144, 160, 168, 176
C_FCW = 224
N_COL = C_FCW + 3 * 2 * FC

W_RC, W_K, W_V = 0, 8, 10
W_S1, W_S2, W_Q, W_S4, W_S5, W_S6 = 12, 28, 44, 52, 68, 76
A_RC, A_K, A_V = 0, 8, 12
A_S1, A_S2, A_Q, A_S4, A_S5, A_S6 = 15, 31, 47, 55, 71, 79
A_ST2, A_UP0 = 79, 80
PER_G = 2 * GRP + KC
PER_2 = 2 * PER_G
A_ST3 = A_UP0 + NG * PER_G


def rope_tables():
    half = HEAD_DIM // 2
    inv = (np.float32(ROPE_THETA) ** (-np.arange(0, half, 2, dtype=np.float32) / np.float32(half))).astype(np.float32)
    row = np.repeat(np.arange(SEQ // GRID_W), GRID_W).astype(np.float32)
    col = np.tile(np.arange(GRID_W), SEQ // GRID_W).astype(np.float32)
    cos, sin = np.zeros((P, SEQ), np.float32), np.zeros((P, SEQ), np.float32)
    for axis, pos in enumerate((row, col)):
        ang = (pos[None, :] * inv[:, None]).astype(np.float32)
        for h in range(2):
            at = axis * half + h * (half // 2)
            cos[at:at + half // 2] = np.cos(ang)
            sin[at:at + half // 2] = np.sin(ang) * (1 if h else -1)
    return cos, sin


def window_masks():
    q, k = np.arange(P)[:, None], np.arange(P)[None, :]
    before = np.where(k >= q, 0.0, NEG).astype(np.float32)
    after = np.where(k <= q, 0.0, NEG).astype(np.float32)
    return np.stack([before, after], 1)


def build(nc, D, out):
    f32, f32r, bf16 = mybir.dt.float32, mybir.dt.float32r, mybir.dt.bfloat16
    ALU, ACT, AX = mybir.AluOpType, mybir.ActivationFunctionType, mybir.AxisListType
    ds = bass.ds
    mult, add, sub = ALU.mult, ALU.add, ALU.subtract
    SCALE = float(HEAD_DIM) ** -0.5

    CONST = 16512
    RING = CONST + 6144
    HX = RING + 6 * 4096
    B = HX + 65536
    at = {}

    def sb(name, off, shape, dt=f32):
        at[name] = (off, off + (2 if dt == bf16 else 4) * int(np.prod(shape[1:])))
        assert at[name][1] <= 229368, name
        return nc.alloc_sbuf_tensor_at(name, shape, dt, offset=off)

    cursor = [CONST]

    def const(name, shape, dt=f32):
        off = cursor[0]
        cursor[0] += ((2 if dt == bf16 else 4) * int(np.prod(shape[1:])) + 31) // 32 * 32
        assert cursor[0] <= RING, cursor[0]
        return sb(name, off, shape, dt)

    ident = const("ident", [P, P])
    ones = const("ones", [P, P])
    masks = const("masks", [P, 2, P])
    pcol = const("pcol", [P, N_COL])
    silu2 = const("silu2", [P, KC, 2])
    sgm2 = const("sgm2", [P, 2 * KC])
    mod_x = const("mod_x", [P, 2, KC])
    mod_c = const("mod_c", [P, 2, KC])
    rest = const("rest", [P, 4, KC])
    a2col = const("a2col", [P, KC])
    lru = const("lru", [P, 8, 2 * KC])
    decay = const("decay", [P, 2, 2 * KC])
    ss = const("ss", [P, TT])
    rms = const("rms", [P, TT])
    rstd0 = const("rstd0", [P, TT])
    sink = const("sink", [P, N_HEADS])
    nsink = const("nsink", [P, N_HEADS])
    epsc = const("epsc", [P, 1])
    negm = const("negm", [P, 2, Q_PER_KV])
    smax = const("smax", [P, 2, Q_PER_KV])
    rsum = const("rsum", [P, 2, Q_PER_KV])
    esink = const("esink", [P, 2, Q_PER_KV])
    rden = const("rden", [P, 2, Q_PER_KV])
    ident_b = const("ident_b", [P, P], bf16)
    masks_b = const("masks_b", [P, 2, P], bf16)

    wst = [sb(f"wst{s}", RING + 4096 * s, [P, KC, P]) for s in range(2)]
    whi2 = sb("whi_both", RING + 8192, [P, 2, KC, P], f32r)
    wlo2 = sb("wlo_both", RING + 16384, [P, 2, KC, P], f32r)
    whi = [whi2[:, s, :, :] for s in range(2)]
    wlo = [wlo2[:, s, :, :] for s in range(2)]

    hx_hi = sb("hx_hi", HX, [P, KC, SEQ], f32r)
    hx_lo = sb("hx_lo", HX + 32768, [P, KC, SEQ], f32r)
    NXB = 6
    xtile = [sb(f"xtile{s}", HX + 4096 * s, [P, D_MODEL]) for s in range(NXB)]
    xn = [sb(f"xn{s}", HX + 24576 + 4096 * s, [P, D_MODEL]) for s in range(2)]
    xTs = [sb(f"xTs{s}", HX + 32768 + 4096 * s, [P, KC, P]) for s in range(2)]
    squares0 = sb("squares0", HX + 40960, [P, D_MODEL])
    prow = [sb(f"prow{s}", HX + 45056 + 512 * s, [P, P]) for s in range(3)]
    xnT = sb("xnT", B, [P, KC, ALL])
    hc_hi = sb("hc_hi", B + 40960, [P, KC, CTX], f32r)
    hc_lo = sb("hc_lo", B + 49152, [P, KC, CTX], f32r)
    NWM = 4
    wmod = [sb(f"wmod{s}", B + 57344 + 8192 * s, [P, 2 * D_MODEL]) for s in range(NWM)]
    mrow = sb("mrow", B + 90112, [P, 2 * D_MODEL])
    mtmp = [sb(f"mtmp{s}", B + 98304 + 4096 * s, [P, SEQ]) for s in range(2)]
    kf = sb("kf", B, [P, SEQ])
    ks = sb("ks", B + 4096, [P, SEQ])
    kout = [sb(f"kout{s}", B + 8192 + 5120 * s, [P, ALL]) for s in range(N_KV)]
    vout = sb("vout", B + 18432, [P, TT, KV_WIDTH])
    cosA = sb("cosA", B + 28672, [P, SEQ])
    sinA = sb("sinA", B + 32768, [P, SEQ])
    racc = sb("racc", B + 57344, [P, REST])
    wrest = [sb(f"wrest{s}", B + 73728 + 16384 * s, [P, REST]) for s in range(2)]
    xc_ctx = sb("xc_ctx", B + 108352, [P, KC, CTX])
    Y = sb("Y", B, [P, KC, SEQ])
    s1 = B + 32768
    sr = [sb(f"sr{d}", s1 + 5120 * d, [P, ALL]) for d in range(2)]
    si = [sb(f"si{d}", s1 + 10240 + 5120 * d, [P, ALL]) for d in range(2)]
    aa = [sb(f"aa{d}", s1 + 20480 + 5120 * d, [P, ALL]) for d in range(2)]
    qq = [sb(f"qq{d}", s1 + 30720 + 5120 * d, [P, ALL]) for d in range(2)]
    gst = sb("gst", s1 + 40960, [P, 4, P])
    ghi = sb("ghi", s1 + 43008, [P, 4, P], f32r)
    glo = sb("glo", s1 + 45056, [P, 4, P], f32r)
    xc = [sb("xc0", s1 + 47104, [P, ALL]), sb("xc1", s1 + 62464, [P, ALL])]
    xch = sb("xch", s1 + 52224, [P, ALL], f32r)
    xcl = sb("xcl", s1 + 57344, [P, ALL], f32r)
    y_hi = sb("y_hi", B + 32768, [P, KC, SEQ], f32r)
    y_lo = sb("y_lo", B + 65536, [P, KC, SEQ], f32r)
    sg = [sb(f"sg{s}", B + 98304 + 4096 * s, [P, SEQ]) for s in range(2)]
    t1 = [sb(f"t1_{s}", B + 106496 + 4096 * s, [P, SEQ]) for s in range(2)]
    yq = sb("yq", B, [P, N_HEADS, SEQ])
    khi = sb("khi", B + 32768, [P, N_KV, ALL], f32r)
    klo = sb("klo", B + 43008, [P, N_KV, ALL], f32r)
    vf = sb("vf", B + 53248, [P, TT, KV_WIDTH])
    vc_hi = sb("vc_hi", B + 63488, [P, CTX // P, KV_WIDTH], f32r)
    vc_lo = sb("vc_lo", B + 65536, [P, CTX // P, KV_WIDTH], f32r)
    vl_hi = sb("vl_hi", B + 67584, [P, 3, P], f32r)
    vl_lo = sb("vl_lo", B + 69120, [P, 3, P], f32r)
    kff = sb("kff", B + 70656, [P, N_KV, ALL])
    cosQ = sb("cosQ", B + 80896, [P, SEQ])
    sinQ = sb("sinQ", B + 84992, [P, SEQ])
    qf = sb("qf", B + 89088, [P, SEQ])
    qs = sb("qs", B + 93184, [P, SEQ])
    q_hi = sb("q_hi", B + 111616, [P, Q_PER_KV, P], f32r)
    q_lo = sb("q_lo", B + 113664, [P, Q_PER_KV, P], f32r)
    NKB = 5
    prob = [sb(f"prob{s}", B + 91136 + 10240 * s, [P, Q_PER_KV, NKB * P]) for s in range(2)]
    pt_hi = sb("pt_hi", B + 70656, [P, NKB, HALF], f32r)
    pt_lo = sb("pt_lo", B + 80896, [P, NKB, HALF], f32r)
    xres = [sb(f"xres{s}", B + 98304 + 4096 * s, [P, SEQ]) for s in range(2)]
    sqb = sb("sqb", B + 106496, [P, SEQ])
    ssum = sb("ssum", B + 110592, [P, SEQ])
    rstd = sb("rstd", B + 98304, [P, SEQ])
    nrm = [sb(f"nrm{s}", B + 102400 + 4096 * s, [P, SEQ]) for s in range(2)]
    g_hi = [sb(f"g_hi{p}", HX + 24576 * p, [P, GRP, SEQ], f32r) for p in range(2)]
    g_lo = [sb(f"g_lo{p}", HX + 24576 * p + 12288, [P, GRP, SEQ], f32r) for p in range(2)]
    ca = [sb(f"ca{s}", HX + 49152 + 4096 * s, [P, SEQ]) for s in range(GRP)]
    cv = [sb("cv0", HX + 61440, [P, SEQ]), sb("cv1", B + 98304, [P, SEQ]), sb("cv2", B + 102400, [P, SEQ])]
    rms3 = sb("rms3", HX + 49152, [P, SEQ])
    rstd3 = sb("rstd3", HX + 53248, [P, SEQ])
    otile = [sb(f"otile{s}", HX + 4096 * s, [P, D_MODEL]) for s in range(2)]

    xT_d = nc.dram_tensor("xT_scratch", [KC, P, SEQ], f32).ap()
    k_d = nc.dram_tensor("k_scratch", [N_KV, P, ALL], f32).ap()
    v_d = nc.dram_tensor("v_scratch", [P, TT, KV_WIDTH], f32).ap()
    t1_d = nc.dram_tensor("t1_scratch", [KC, P, SEQ], f32).ap()

    ctx = ExitStack()
    with ctx:
        acc = [ctx.enter_context(nc.psum_tensor(f"acc{s}", [P, SEQ], f32)) for s in range(2)]
        gp = ctx.enter_context(nc.psum_tensor("gp", [P, 4 * HALF], f32))

        names = """row_loaded par_loaded par_T par_col c_sig silu_ready lru_e lru_w consts_set sq_done rms_done
        rn_done xn_done raw_T xn_T xT_copied xnT_copied modrow_done modrow_copied modT_done
        modT_read hx_hi_c hx_lo_c hx_hi_x hx_lo_x mt_done mod_ready
        acc_full k_copied k_rope ksv_stored v_copied ctx_conv ctx_centre rest_acc rest_sum rest_ready
        w_hi w_ready g_loaded g_zero g_hi_s g_ready
        xc_centre xc_ready xc_hi xc_lo gate_full gate_read ix_done ex_done th_done sq2_done m_done root_done b_done
        scan_done gelu_done y_done y_hi_s y_lo_s sig_done t1_done q_copied q_swap q_cos q_sin q_rope
        kv_loaded rope_loaded k_hi_s k_lo_s vc_s qv_s s_full s_max s_neg s_exp s_es s_rden n_act n_pool n_dve mask_b
        pt_full pt_hi_s pt_lo_s o_full o_read m_prod m_done4 mg_hi mg_lo x1_done sqx_done ssx_done st_full st_root
        st_rstd n2_a n2_hi n2_tmp n2_lo z_hi_s z_lo_s merged q_s v_s
        f_centre f_conv f_gelu f_prod f_hi f_lo passed_sp passed_pool x2_done fin_done o_T o_copied dve_link kf_load""".split()
        S = {n: ctx.enter_context(nc.semaphore(n)) for n in names}
        x_loaded = [ctx.enter_context(nc.semaphore(f"x_loaded{s}")) for s in range(NXB)]
        wm_loaded = [ctx.enter_context(nc.semaphore(f"wm_loaded{s}")) for s in range(NWM)]
        wr_loaded = [ctx.enter_context(nc.semaphore(f"wr_loaded{s}")) for s in range(2)]
        w_loaded = [ctx.enter_context(nc.semaphore(f"w_loaded{s}")) for s in range(2)]
        xT_stored = [ctx.enter_context(nc.semaphore(f"xT_stored{s}")) for s in range(2)]
        acc_read = [ctx.enter_context(nc.semaphore(f"acc_read{s}")) for s in range(2)]
        k_swap = [ctx.enter_context(nc.semaphore(f"k_swap{s}")) for s in range(2)]
        t1_stored = [ctx.enter_context(nc.semaphore(f"t1_stored{s}")) for s in range(2)]
        t1_loaded = [ctx.enter_context(nc.semaphore(f"t1_loaded{s}")) for s in range(2)]
        xr_loaded = [ctx.enter_context(nc.semaphore(f"xr_loaded{s}")) for s in range(2)]
        out_stored = [ctx.enter_context(nc.semaphore(f"out_stored{s}")) for s in range(2)]

        def wait(eng, sem, value):
            eng.wait_ge(sem, value)
            if not isinstance(value, int):
                eng.sem_inc(S["passed_sp" if eng is nc.sync else "passed_pool"], 1)

        def full(eng, a0, per=0, i=0):
            w = wait if eng is nc.gpsimd else (lambda e, sem, v: e.wait_ge(sem, v))
            w(eng, S["acc_full"], a0 + 1 + per * i)

        def slot_read(eng, a0, per=0, i=0):
            w = wait if eng is nc.gpsimd else (lambda e, sem, v: e.wait_ge(sem, v))
            w(eng, acc_read[a0 % 2], a0 // 2 + 1 + per // 2 * i)

        def halves(tile, k, h):
            return tile[:, k, HALF * h:HALF * (h + 1)]

        def pairs(eng, step):
            step(1, 1)
            with eng.Fori(1, KC // 2) as j:
                step(2 * j, 0)
                step(2 * j + 1, 1)

        def units(eng, step, finish):
            step(0, 0, 0, None)
            step(0, 1, 1, (0, 0, 0))
            step(1, 0, 2, (0, 1, 1))
            step(1, 1, 3, (1, 0, 2))
            with eng.Fori(2, XT - 1) as n:
                step(n, 0, 2 * n, (n - 1, 1, 2 * n - 1))
                step(n, 1, 2 * n + 1, (n, 0, 2 * n))
            last = XT - 1
            step(last, 0, 2 * last, (last - 1, 1, 2 * last - 1))
            step(last, 1, 2 * last + 1, (last, 0, 2 * last))
            finish(last, 1, 2 * last + 1)

        def is_edge(n):
            return isinstance(n, int) and n in (0, XT - 1)

        def block_base(n, u):
            if not isinstance(n, int) or 0 < n < XT - 1:
                return 5 * u - 2
            return 4 * u if n == 0 else 5 * (2 * n) - 2 + 4 * (u - 2 * n)

        block = ctx.enter_context(nc.Block())

        @block.sync
        def _(sp):
            sp.dma_start(ident[:, :], D["ident"]).then_inc(S["par_loaded"], 16)
            rows = [
                (0, C_C, D["c"].rearrange("o (k p) -> (o k) p", p=P)),
                (0, C_CCTX, D["c_ctx"].rearrange("(k p) -> k p", p=P)),
                (0, C_N1, D["norm1_w"].rearrange("o (k p) -> (o k) p", p=P)),
                (0, C_BMOD, D["b_mod"].rearrange("o (k p) -> (o k) p", p=P)),
                (0, C_LCW, D["lru_conv_w"].rearrange("o t (k p) -> (o t k) p", p=P)),
                (0, C_LCB, D["lru_conv_b"].rearrange("o (k p) -> (o k) p", p=P)),
                (1, C_GAB - 112, D["gate_a_b"].rearrange("o d (k p) -> (o d k) p", p=P)),
                (1, C_GXB - 112, D["gate_x_b"].rearrange("o d (k p) -> (o d k) p", p=P)),
                (1, C_LAM - 112, D["lru_lambda"].rearrange("o d (k p) -> (o d k) p", p=P)),
                (1, C_N2 - 112, D["norm2_w"].rearrange("o (k p) -> (o k) p", p=P)),
                (1, C_FN - 112, D["final_norm_w"].rearrange("(k p) -> k p", p=P)),
                (1, C_FCB - 112, D["ffn_conv_b"].rearrange("o (k p) -> (o k) p", p=P)),
            ]
            for t, r, src in rows:
                sp.dma_start(prow[t][r:r + src.shape[0], :], src).then_inc(S["par_loaded"], 16)
            fcw = D["ffn_conv_w"].rearrange("o t (k p) -> (o t k) p", p=P)
            sp.dma_start(prow[2][:, :], fcw[0:P, :]).then_inc(S["par_loaded"], 16)
            sp.dma_start(prow[0][112:P, :], fcw[P:144, :]).then_inc(S["par_loaded"], 16)
            sp.dma_start(sink[:, :], D["sink_logit"].to_broadcast([P, N_HEADS])).then_inc(S["par_loaded"], 16)
            sp.dma_start(masks[:, :, :], D["masks"]).then_inc(S["par_loaded"], 16)
            for t in range(max(TT, KC)):
                if t < KC:
                    if t >= NWM:
                        sp.wait_ge(S["modrow_done"], t - NWM + 1)
                    sp.dma_start(wmod[t % NWM][:, :], D["w_mod"][0, P * t:P * (t + 1), 0:2 * D_MODEL])\
                        .then_inc(wm_loaded[t % NWM], 16)
                if t < TT:
                    if t >= NXB:
                        sp.wait_ge(S["xn_T"], t - NXB + 1)
                    src = D["ctx"][0, P * t:P * (t + 1), :] if t < 2 else D["x"][0, P * (t - 2):P * (t - 1), :]
                    sp.dma_start(xtile[t % NXB][:, :], src).then_inc(x_loaded[t % NXB], 16)

            def load_w(src, n0, kc=KC, per=0, i=0):
                if n0 >= 2:
                    wait(sp, S["w_ready"], n0 - 1 + per * i)
                sp.dma_start(wst[n0 % 2][:, 0:kc, :], src).then_inc(w_loaded[n0 % 2], 16)

            w_in = D["w_in"][0].rearrange("(k p) n -> p k n", p=P)
            w_or = D["w_o_rnn"][0].rearrange("(k p) n -> p k n", p=P)
            w_oa = D["w_o_attn"][0].rearrange("(k p) n -> p k n", p=P)
            w_out = D["w_out"][0].rearrange("(k p) n -> p k n", p=P)
            w_up = D["w_up"][0].rearrange("(k p) n -> p k n", p=P)
            w_dn = D["w_down"][0].rearrange("(k p) n -> p k n", p=P)

            def col(w, base, i):
                return w[:, :, ds(base + i * P, P)] if not isinstance(i, int) else w[:, :, base + i * P:base + i * P + P]

            def load_rest(k):
                if k >= 2:
                    sp.wait_ge(S["rest_acc"], k - 1)
                else:
                    sp.wait_ge(S["hx_lo_x"], KC)
                sp.dma_start(wrest[k % 2][:, :], D["w_mod"][0, P * k:P * (k + 1), 2 * D_MODEL:]).then_inc(wr_loaded[k % 2], 16)

            for n in range(2):
                load_w(col(w_in, COL_R, n), W_RC + n)
            sp.wait_ge(S["hx_lo_x"], KC)
            sp.dma_start(cosA[:, :], D["rope_cos"]).then_inc(S["rope_loaded"], 16)
            sp.dma_start(sinA[:, :], D["rope_sin"]).then_inc(S["rope_loaded"], 16)
            for k in range(2):
                load_rest(k)
            for n in range(2, KC):
                load_w(col(w_in, COL_R, n), W_RC + n)
            load_rest(2)
            load_w(col(w_in, COL_K, 0), W_K)
            load_rest(3)
            load_w(col(w_in, COL_K, 1), W_K + 1)
            load_rest(4)
            load_w(col(w_in, COL_V, 0), W_V)
            load_rest(5)
            load_w(col(w_in, COL_V, 1), W_V + 1)
            load_rest(6)
            load_rest(7)

            def swap(dst, src, sem):
                for q in range(4):
                    sp.dma_start(dst[32 * q:32 * q + 32, :], src[32 * (q ^ 1):32 * (q ^ 1) + 32, :]).then_inc(sem, 16)

            def load_gates(c, waits):
                if waits is not None:
                    wait(sp, S["g_ready"], waits)
                for b in range(2):
                    for q, name in ((0, "gate_a_w"), (2, "gate_x_w")):
                        src = D[name][0].rearrange("d n k m -> k n d m")
                        if isinstance(c, int):
                            blk = src[:, 2 * c + b, :, :]
                        else:
                            blk = src[:, ds(2 * c + b, 1), :, :].rearrange("k o d m -> k (o d) m")
                        sp.dma_start(gst[64 * b:64 * b + 64, q:q + 2, 64 * b:64 * b + 64], blk).then_inc(S["g_loaded"], 16)

            load_w(col(w_in, COL_R, 0), W_S1)
            load_w(col(w_in, COL_RG, 0), W_S1 + 1)
            sp.wait_ge(S["g_zero"], 1)
            load_gates(0, None)
            with sp.Fori(1, KC) as i:
                load_w(col(w_in, COL_R, i), W_S1, per=2, i=i)
                load_w(col(w_in, COL_RG, i), W_S1 + 1, per=2, i=i)
                load_gates(i, i)
            with sp.Fori(0, KC) as i:
                load_w(col(w_in, COL_GA, i), W_S2, per=2, i=i)
                load_w(col(w_or, 0, i), W_S2 + 1, per=2, i=i)
            load_w(col(w_in, COL_Q, 0), W_Q)
            load_w(col(w_in, COL_Q, 1), W_Q + 1)
            full(sp, A_S2 + 15)
            sp.dma_start(cosQ[:, :], D["rope_cos"]).then_inc(S["rope_loaded"], 16)
            sp.dma_start(sinQ[:, :], D["rope_sin"]).then_inc(S["rope_loaded"], 16)
            sp.wait_ge(S["ksv_stored"], 16 * 3)
            sp.dma_start(kff[:, :, :], k_d.rearrange("h p n -> p h n")).then_inc(S["kf_load"], 16)
            sp.dma_start(vf[:, :, :], v_d).then_inc(S["kv_loaded"], 16)
            with sp.Fori(1, KC // 2) as i:
                load_w(col(w_in, COL_Q, 2 * i), W_Q, per=2, i=i)
                load_w(col(w_in, COL_Q + P, 2 * i), W_Q + 1, per=2, i=i)
            def load_t1(m, s):
                sp.dma_start(t1[s][:, :], t1_d[m] if isinstance(m, int) else
                             t1_d.rearrange("k p n -> p k n")[:, ds(m, 1), :].rearrange("p o n -> p (o n)"))\
                    .then_inc(t1_loaded[s], 16)

            for s in range(2):
                load_w(col(w_in, COL_GB, s), W_S4 + 2 * s)
                load_w(col(w_oa, 0, s), W_S4 + 2 * s + 1)
                if s == 0:
                    sp.wait_ge(S["o_read"], N_KV * XT)
                    for e in range(2):
                        sp.wait_ge(t1_stored[e], 16 * KC // 2)
                load_t1(s, s)
            with sp.Fori(1, KC // 2) as i:
                for s in range(2):
                    load_w(col(w_in, COL_GB + P * s, 2 * i), W_S4 + 2 * s, per=4, i=i)
                    load_w(col(w_oa, P * s, 2 * i), W_S4 + 2 * s + 1, per=4, i=i)
                    wait(sp, S["merged"], 2 * i + s - 1)
                    load_t1(2 * i + s, s)

            def load_xres(m, s):
                sp.dma_start(xres[s][:, :], xT_d[m]).then_inc(xr_loaded[s], 16)

            for m in range(KC):
                load_w(col(w_out, 0, m), W_S5 + m)
                if m == 0:
                    sp.wait_ge(S["merged"], KC)
                if m >= 2:
                    slot_read(sp, A_S5 + m - 2)
                load_xres(m, m % 2)

            def load_up(g, n0, i=0):
                for j in range(GRP):
                    for h in range(2):
                        c0 = h * D_FF + j * P
                        src = w_up[:, :, c0 + GRP * P * g:c0 + GRP * P * g + P] if isinstance(g, int) else \
                            w_up[:, :, ds(c0 + g * (GRP * P), P)]
                        load_w(src, n0 + 2 * j + h, per=PER_2, i=i)

            def load_down(g, n0, i=0):
                for m in range(KC):
                    rows = w_dn[:, GRP * g:GRP * (g + 1), :] if isinstance(g, int) else w_dn[:, ds(GRP * g, GRP), :]
                    load_w(rows[:, :, P * m:P * (m + 1)], n0 + m, kc=GRP, per=PER_2, i=i)

            load_up(0, W_S6)
            with sp.Fori(0, NG // 2 - 1) as i:
                for e in range(2):
                    load_up(2 * i + 1 + e, W_S6 + 2 * GRP + e * PER_G, i)
                    load_down(2 * i + e, W_S6 + 4 * GRP + e * PER_G, i)
            tail = W_S6 + 2 * GRP + PER_2 * (NG // 2 - 1)
            load_up(NG - 1, tail)
            load_down(NG - 2, tail + 2 * GRP)
            load_down(NG - 1, tail + PER_G)
            for t in range(XT):
                slot_read(sp, A_ST3 + 1 + t)
                sp.dma_start(out[0, P * t:P * (t + 1), :], otile[t % 2][:, :]).then_inc(out_stored[t % 2], 16)
            for e in range(2):
                sp.wait_ge(out_stored[e], 16 * XT // 2)

        @block.gpsimd
        def _(pool):
            def ones_of(k):
                return ones[:, :].rearrange("p (o n) -> p o n", o=1).to_broadcast([P, k, P])

            def split_w(n0, kc=KC, last_use=None, per=0, i=0):
                s = n0 % 2
                wait(pool, w_loaded[s], 16 * (n0 // 2 + 1) + 16 * (per // 2) * i)
                if last_use is not None:
                    full(pool, last_use, per, i)
                nc.gpsimd.tensor_tensor(whi[s][:, 0:kc, :], wst[s][:, 0:kc, :], ones_of(kc), mult).then_inc(S["w_hi"], 1)
                pool.wait_ge(S["w_hi"], n0 + 1 + per * i)
                nc.gpsimd.tensor_tensor(wlo[s][:, 0:kc, :], wst[s][:, 0:kc, :], whi[s][:, 0:kc, :], sub)\
                    .then_inc(S["w_ready"], 1)

            nc.gpsimd.memset(ones[:, :], 1.0).then_inc(S["consts_set"], 1)
            nc.gpsimd.memset(epsc[:, :], EPS).then_inc(S["consts_set"], 1)
            for n in range(KC):
                split_w(W_RC + n, last_use=A_RC + n - 2 if n >= 2 else None)
            split_w(W_K, last_use=A_RC + 6)
            split_w(W_K + 1, last_use=A_RC + 7)
            split_w(W_V, last_use=A_K + 1)
            split_w(W_V + 1, last_use=A_K + 3)
            split_w(W_S1, last_use=A_V + 2)
            split_w(W_S1 + 1, last_use=A_V + 2)
            pool.wait_ge(S["rest_acc"], KC)
            nc.gpsimd.memset(gst[:, :, :], 0.0).then_inc(S["g_zero"], 1)

            def split_gates(c):
                wait(pool, S["g_loaded"], 64 * c + 64)
                if not isinstance(c, int) or c > 0:
                    wait(pool, S["gate_full"], 4 * c)
                nc.gpsimd.tensor_tensor(ghi[:, :, :], gst[:, :, :], ones_of(4), mult).then_inc(S["g_hi_s"], 1)
                pool.wait_ge(S["g_hi_s"], c + 1)
                nc.gpsimd.tensor_tensor(glo[:, :, :], gst[:, :, :], ghi[:, :, :], sub).then_inc(S["g_ready"], 1)

            def gated_input(c, d, e):
                pool.wait_ge(S["gate_read"], 4 * c + d + 3)
                nc.gpsimd.tensor_tensor(si[d][:, :], si[d][:, :], xc[e][:, :], mult).then_inc(S["ix_done"], 1)

            def decay_square(c, d):
                pool.wait_ge(S["ex_done"], 2 * c + d + 1)
                if not isinstance(c, int) or c > 0:
                    pool.wait_ge(S["scan_done"], 4 * c)
                nc.gpsimd.tensor_tensor(qq[d][:, :], aa[d][:, :], aa[d][:, :], mult).then_inc(S["sq2_done"], 1)

            split_gates(0)
            split_w(W_S1 + 2, last_use=A_S1)
            split_w(W_S1 + 3, last_use=A_S1 + 1)

            def chunk_step(i, e):
                split_w(W_S1 + 2, last_use=A_S1, per=2, i=i)
                decay_square(i - 1, 0)
                decay_square(i - 1, 1)
                gated_input(i - 1, 0, 1 - e)
                split_gates(i)
                gated_input(i - 1, 1, 1 - e)
                split_w(W_S1 + 3, last_use=A_S1 + 1, per=2, i=i)

            pairs(pool, chunk_step)
            decay_square(KC - 1, 0)
            decay_square(KC - 1, 1)
            gated_input(KC - 1, 0, 1)
            gated_input(KC - 1, 1, 1)
            with pool.Fori(0, KC) as i:
                split_w(W_S2 + 2, last_use=A_S2, per=2, i=i)
                split_w(W_S2 + 3, last_use=A_S2 + 1, per=2, i=i)
            with pool.Fori(1, KC // 2) as i:
                split_w(W_Q, last_use=A_Q - 2, per=2, i=i)
                split_w(W_Q + 1, last_use=A_Q - 1, per=2, i=i)
            split_w(W_S4, last_use=A_Q + 6)
            split_w(W_S4 + 1, last_use=A_Q + 7)

            pool.wait_ge(S["kv_loaded"], 16)
            nc.gpsimd.tensor_scalar(vc_hi[:, :, :], vf[:, 0:2, :], 1.0, None, mult).then_inc(S["vc_s"], 1)
            pool.wait_ge(S["vc_s"], 1)
            nc.gpsimd.tensor_tensor(vc_lo[:, :, :], vf[:, 0:2, :], vc_hi[:, :, :], sub).then_inc(S["vc_s"], 1)

            def split_queries(n, kh, u):
                if not isinstance(u, int) or u > 0:
                    wait(pool, S["s_full"], 4 * u)
                cols = slice(P * n, P * n + P) if isinstance(n, int) else ds(n * P, P)
                q = yq[:, Q_PER_KV * kh:Q_PER_KV * (kh + 1), cols]
                one = ones[:, :].rearrange("p (o n) -> p o n", o=1).to_broadcast([P, Q_PER_KV, P])
                nc.gpsimd.tensor_tensor(q_hi[:, :, :], q, one, mult).then_inc(S["q_s"], 1)
                wait(pool, S["q_s"], 2 * u + 1)
                nc.gpsimd.tensor_tensor(q_lo[:, :, :], q, q_hi[:, :, :], sub).then_inc(S["q_s"], 1)

            def split_values(n, kh, u):
                if not isinstance(u, int) or u > 0:
                    wait(pool, S["o_full"], u)
                edge = isinstance(n, int) and n in (0, XT - 1)
                t, lo, nl = (2 + (0 if n == 0 else n - 1), 1, 2) if edge else (n + 1, 0, 3)
                v = vf[:, t:t + nl, P * kh:P * (kh + 1)] if isinstance(t, int) else vf[:, ds(t, nl), P * kh:P * (kh + 1)]
                one = ones[:, :].rearrange("p (o n) -> p o n", o=1).to_broadcast([P, nl, P])
                nc.gpsimd.tensor_tensor(vl_hi[:, lo:3, :], v, one, mult).then_inc(S["v_s"], 1)
                wait(pool, S["v_s"], 2 * u + 1)
                nc.gpsimd.tensor_tensor(vl_lo[:, lo:3, :], v, vl_hi[:, lo:3, :], sub).then_inc(S["v_s"], 1)

            def norm_probs(n, kh, u):
                edge = isinstance(n, int) and n in (0, XT - 1)
                wait(pool, S["s_rden"], 2 * u + 2)
                pr = prob[kh][:, 2, P if edge else 0:]
                nc.gpsimd.tensor_tensor(pr, pr, rden[:, kh, 2:3].to_broadcast([P, pr.shape[-1]]), mult)\
                    .then_inc(S["n_pool"], 1)

            pool.wait_ge(S["q_rope"], N_HEADS)

            def finish(n, kh, u):
                norm_probs(n, kh, u)
                split_values(n, kh, u)

            def step(n, kh, u, before):
                split_queries(n, kh, u)
                if before:
                    finish(*before)

            units(pool, step, finish)

            with pool.Fori(0, KC) as i:
                split_w(W_S4 + 2, last_use=A_S4, per=2, i=i)
                split_w(W_S4 + 3, last_use=A_S4 + 1, per=2, i=i)

            def add_square(m, base):
                pool.wait_ge(S["sqx_done"], base + m + 1)
                if m == 0:
                    nc.gpsimd.tensor_scalar(ssum[:, :], sqb[:, :], 1.0, None, mult).then_inc(S["ssx_done"], 1)
                else:
                    pool.wait_ge(S["ssx_done"], base + m)
                    nc.gpsimd.tensor_tensor(ssum[:, :], ssum[:, :], sqb[:, :], add).then_inc(S["ssx_done"], 1)

            for m in range(KC):
                if m < KC - 2:
                    split_w(W_S5 + m + 2, last_use=A_S5 + m)
                else:
                    split_w(W_S6 + m - (KC - 2), last_use=A_S5 + m)
                add_square(m, 0)
            for j in range(2, 2 * GRP):
                split_w(W_S6 + j, last_use=A_UP0 + j - 2)

            def split_group(j0, ups, downs, i=0):
                for j in range(ups):
                    split_w(W_S6 + j0 + j, last_use=A_UP0 + j0 + j - 2, per=PER_2, i=i)
                for m in range(downs):
                    split_w(W_S6 + j0 + ups + m, kc=GRP, last_use=A_UP0 + j0 + ups + m - 2, per=PER_2, i=i)

            with pool.Fori(0, NG // 2 - 1) as i:
                split_group(2 * GRP, 2 * GRP, KC, i)
                split_group(2 * GRP + PER_G, 2 * GRP, KC, i)
            tail = 2 * GRP + PER_2 * (NG // 2 - 1)
            split_group(tail, 2 * GRP, KC)
            split_group(tail + PER_G, 0, 2)
            for m in range(KC):
                if m < KC - 2:
                    split_w(W_S6 + tail + PER_G + m + 2, kc=GRP, last_use=A_UP0 + tail + PER_G + m)
                add_square(m, KC)

        @block.tensor
        def _(pe):
            mm = nc.tensor.matmul

            def three(out_ap, w_h, w_l, x_h, x_l, first, last):
                mm(out_ap, w_h, x_h, start=first, stop=False)
                mm(out_ap, w_h, x_l, start=False, stop=False)
                return mm(out_ap, w_l, x_h, start=False, stop=last)

            def weights(n0, per=0, i=0):
                pe.wait_ge(S["w_ready"], n0 + 1 + per * i)

            def slot_free(a0, per=0, i=0):
                slot_read(pe, a0 - 2, per, i)

            def half(a0, n0, h, x_h, x_l, kc=KC, width=HALF, paced=None):
                s = n0 % 2
                o = acc[a0 % 2][:, HALF * h:HALF * h + width]
                for k in range(kc):
                    if paced is not None:
                        pe.wait_ge(S[paced], k + 1)
                    last = three(o, whi[s][:, k, :], wlo[s][:, k, :], x_h[:, k, HALF * h:HALF * h + width],
                                 x_l[:, k, HALF * h:HALF * h + width], k == 0, k == kc - 1)
                return last

            def product(a0, n0, x_h, x_l, kc=KC, per=0, i=0, paced=None):
                weights(n0, per, i)
                slot_free(a0, per, i)
                half(a0, n0, 0, x_h, x_l, kc, paced=paced)
                half(a0, n0, 1, x_h, x_l, kc).then_inc(S["acc_full"], 1)

            pe.wait_ge(S["par_loaded"], 16 * 17)
            nc.tensor.transpose(acc[0][:, 0:P], prow[0][:, :], ident[:, :])
            nc.tensor.transpose(acc[0][:, P:P + 112], prow[1][0:112, :], ident[0:112, 0:112])
            nc.tensor.transpose(acc[0][:, 256:384], prow[2][:, :], ident[:, :]).then_inc(S["par_T"], 1)
            pe.wait_ge(S["par_col"], 4)
            for t in range(TT):
                pe.wait_ge(x_loaded[t % NXB], 16 * (t // NXB + 1))
                if t >= 2:
                    if t >= 3:
                        pe.wait_ge(S["xT_copied"], t - 2)
                    for k in range(KC):
                        last = nc.tensor.transpose(acc[0][:, P * k:P * (k + 1)], xtile[t % NXB][:, P * k:P * (k + 1)],
                                                   ident[:, :])
                    last.then_inc(S["raw_T"], 1)
                if t < KC:
                    pe.wait_ge(wm_loaded[t % NWM], 16 * (t // NWM + 1))
                    pe.wait_ge(S["silu_ready"], 2)
                    for b in range(4):
                        last = mm(gp[0:2, HALF * b:HALF * (b + 1)], silu2[:, t, :], wmod[t % NWM][:, HALF * b:HALF * (b + 1)],
                                  start=t == 0, stop=t == KC - 1)
                    last.then_inc(S["modrow_done"], 1)
                pe.wait_ge(S["xn_done"], t + 1)
                if t >= 1:
                    pe.wait_ge(S["xnT_copied"], t)
                for k in range(KC):
                    last = nc.tensor.transpose(acc[1][:, P * k:P * (k + 1)], xn[t % 2][:, P * k:P * (k + 1)], ident[:, :])
                last.then_inc(S["xn_T"], 1)
            pe.wait_ge(S["modrow_copied"], 1)
            pe.wait_ge(S["xT_copied"], XT)
            for j in range(2 * KC):
                last = nc.tensor.transpose(acc[0][:, 2 * j:2 * j + 2], mrow[0:2, P * j:P * (j + 1)], ident[0:2, 0:2])
            last.then_inc(S["modT_done"], 1)

            pe.wait_ge(S["mod_ready"], 4)
            pe.wait_ge(S["xnT_copied"], TT)
            for n in range(KC):
                weights(W_RC + n)
                if n >= 2:
                    slot_free(A_RC + n)
                half(A_RC + n, W_RC + n, 0, hc_hi, hc_lo, width=CTX, paced="hx_lo_c" if n == 0 else None)\
                    .then_inc(S["acc_full"], 1)
            for kh in range(N_KV):
                product(A_K + 2 * kh, W_K + kh, hx_hi, hx_lo, paced="hx_lo_x" if kh == 0 else None)
                slot_free(A_K + 2 * kh + 1)
                half(A_K + 2 * kh + 1, W_K + kh, 0, hc_hi, hc_lo, width=CTX).then_inc(S["acc_full"], 1)
            weights(W_V + 1)
            for t in range(TT):
                a = A_V + t // 4
                if t % 4 == 0:
                    slot_free(a)
                x_h, x_l, c0 = (hc_hi, hc_lo, P * t) if t < 2 else (hx_hi, hx_lo, P * (t - 2))
                o = acc[a % 2][:, KV_WIDTH * (t % 4):KV_WIDTH * (t % 4 + 1)]
                for k in range(KC):
                    last = three(o, x_h[:, k, c0:c0 + P], x_l[:, k, c0:c0 + P], whi2[:, :, k, :], wlo2[:, :, k, :],
                                 k == 0, k == KC - 1)
                if t % 4 == 3 or t == TT - 1:
                    last.then_inc(S["acc_full"], 1)
            pe.wait_ge(S["rest_acc"], KC)
            pe.wait_ge(S["modrow_copied"], 1)
            pe.wait_ge(S["consts_set"], 2)
            for m in range(4 * KC):
                last = mm(gp[:, 2 * m:2 * m + 2], racc[:, P * m:P * (m + 1)], ones[:, 0:2], start=True, stop=True)
            last.then_inc(S["rest_sum"], 1)

            def gate(c, q):
                if q == 0:
                    pe.wait_ge(S["g_ready"], c + 1)
                    pe.wait_ge(S["xc_lo"], c + 1)
                if not (isinstance(c, int) and c == 0 and q == 0):
                    pe.wait_ge(S["gate_read"], 4 * c + q)
                for c0, c1 in ((0, 512), (512, 1024), (1024, ALL)):
                    last = three(gp[:, c0:c1], ghi[:, q, :], glo[:, q, :], xch[:, c0:c1], xcl[:, c0:c1], True, True)
                last.then_inc(S["gate_full"], 1)

            product(A_S1, W_S1, hx_hi, hx_lo)
            product(A_S1 + 1, W_S1 + 1, hx_hi, hx_lo)
            pe.wait_ge(S["rest_ready"], 1)

            def chunk_step(i, e):
                for j in range(2):
                    weights(W_S1 + j, 2, i)
                    slot_free(A_S1 + j, 2, i)
                    half(A_S1 + j, W_S1 + j, 0, hx_hi, hx_lo)
                    gate(i - 1, 2 * j)
                    half(A_S1 + j, W_S1 + j, 1, hx_hi, hx_lo).then_inc(S["acc_full"], 1)
                    gate(i - 1, 2 * j + 1)

            pairs(pe, chunk_step)
            for q in range(4):
                gate(KC - 1, q)
            product(A_S2, W_S2, hx_hi, hx_lo)
            product(A_S2 + 1, W_S2 + 1, y_hi, y_lo, paced="y_lo_s")
            with pe.Fori(1, KC) as i:
                product(A_S2, W_S2, hx_hi, hx_lo, per=2, i=i)
                product(A_S2 + 1, W_S2 + 1, y_hi, y_lo, per=2, i=i)
            with pe.Fori(0, KC // 2) as i:
                product(A_Q, W_Q, hx_hi, hx_lo, per=2, i=i)
                product(A_Q + 1, W_Q + 1, hx_hi, hx_lo, per=2, i=i)

            pe.wait_ge(S["mask_b"], 2)
            pe.wait_ge(S["k_lo_s"], 1)
            pe.wait_ge(S["vc_s"], 2)
            pe.wait_ge(S["q_rope"], N_HEADS)
            slot_read(pe, A_Q + 7)

            def score(n, kh, u, h):
                if h == 0:
                    pe.wait_ge(S["q_s"], 2 * u + 2)
                pair = gp[:, 1024 * (h % 2):1024 * (h % 2) + 1024]
                if not (isinstance(u, int) and u == 0 and h < 2):
                    pe.wait_ge(S["s_exp"], 4 * u + h - 1)
                if is_edge(n):
                    c0, o0, w = CTX + (0 if n == 0 else P * (n - 1)), 256, 256
                else:
                    c0, o0, w = (n - 1) * P + CTX, 128, 384
                def keys(t, c, width):
                    return t[:, kh, c:c + width] if isinstance(c, int) else t[:, kh, ds(c, width)]
                mm(pair[:, o0:512], q_hi[:, h, :], keys(khi, c0, w), start=True, stop=False)
                for e in range(2):
                    if not is_edge(n) or (n == 0) == (e == 1):
                        m0 = 384 if e else o0
                        mm(pair[:, m0:m0 + P], ident_b[:, :], masks_b[:, e, :], start=False, stop=False)
                mm(pair[:, o0:512], q_hi[:, h, :], keys(klo, c0, w), start=False, stop=False)
                mm(pair[:, o0:512], q_lo[:, h, :], keys(khi, c0, w), start=False, stop=True)
                three(pair[:, 512:768], q_hi[:, h, :], q_lo[:, h, :], keys(khi, 0, CTX), keys(klo, 0, CTX), True, True)\
                    .then_inc(S["s_full"], 1)

            def flip(n, kh, u, j):
                nb = 4 if is_edge(n) else 5
                if j >= nb:
                    return
                t = block_base(n, u) + j
                par = (4 * u + j) % 2 if isinstance(u, int) and is_edge(n) and n == 0 else (kh * 5 + j) % 2 if not is_edge(n) else j % 2
                if j == 0:
                    pe.wait_ge(S["n_act"], 2 * u + 2)
                    pe.wait_ge(S["n_pool"], u + 1)
                    pe.wait_ge(S["n_dve"], u + 1)
                if not (isinstance(t, int) and t < 2):
                    pe.wait_ge(S["pt_lo_s"], t - 1)
                kb = j + 1 if is_edge(n) else j
                for h in range(Q_PER_KV):
                    last = nc.tensor.transpose(acc[0][:, HALF * par + P * h:HALF * par + P * (h + 1)],
                                               prob[kh][:, h, P * kb:P * (kb + 1)], ident[:, :])
                last.then_inc(S["pt_full"], 1)

            def weigh(n, kh, u):
                nb = 4 if is_edge(n) else 5
                pe.wait_ge(S["v_s"], 2 * u + 2)
                if not (isinstance(u, int) and u < 2):
                    pe.wait_ge(S["o_read"], u - 1)
                o = acc[1][:, HALF * kh:HALF * (kh + 1)]
                base = block_base(n, u)
                for j in range(nb):
                    pe.wait_ge(S["pt_lo_s"], base + j + 1)
                    kb = j + 1 if is_edge(n) else j
                    if kb < 3:
                        v_h, v_l = vl_hi[:, kb, :], vl_lo[:, kb, :]
                    else:
                        v_h, v_l = (v[:, kb - 3, P * kh:P * (kh + 1)] for v in (vc_hi, vc_lo))
                    last = three(o, v_h, v_l, pt_hi[:, kb, :], pt_lo[:, kb, :], j == 0, j == nb - 1)
                last.then_inc(S["o_full"], 1)

            def attention(n, kh, u, before):
                score(n, kh, u, 0)
                score(n, kh, u, 1)
                if before:
                    flip(*before, 0)
                    flip(*before, 1)
                score(n, kh, u, 2)
                if before:
                    flip(*before, 2)
                    flip(*before, 3)
                score(n, kh, u, 3)
                if before:
                    flip(*before, 4)
                    weigh(*before)

            units(pe, attention, lambda n, kh, u: ([flip(n, kh, u, j) for j in range(NKB)], weigh(n, kh, u)))

            pe.wait_ge(S["o_read"], N_KV * XT)
            product(A_S4, W_S4, hx_hi, hx_lo)
            product(A_S4 + 1, W_S4 + 1, y_hi, y_lo, paced="z_lo_s")
            with pe.Fori(1, KC) as i:
                product(A_S4, W_S4, hx_hi, hx_lo, per=2, i=i)
                product(A_S4 + 1, W_S4 + 1, y_hi, y_lo, per=2, i=i)
            product(A_S5, W_S5, hx_hi, hx_lo, paced="mg_lo")
            product(A_S5 + 1, W_S5 + 1, hx_hi, hx_lo)
            with pe.Fori(1, KC // 2) as i:
                product(A_S5, W_S5, hx_hi, hx_lo, per=2, i=i)
                product(A_S5 + 1, W_S5 + 1, hx_hi, hx_lo, per=2, i=i)

            def statistics(a0, ready):
                slot_free(a0)
                pe.wait_ge(S["ssx_done"], ready)
                for h in range(2):
                    last = mm(acc[a0 % 2][:, HALF * h:HALF * (h + 1)], ones[:, :], ssum[:, HALF * h:HALF * (h + 1)],
                              start=True, stop=True)
                last.then_inc(S["acc_full"], 1)

            statistics(A_ST2, KC)
            def up(j0, i=0, paced=None):
                for j in range(2 * GRP):
                    product(A_UP0 + j0 + j, W_S6 + j0 + j, y_hi, y_lo, per=PER_2, i=i, paced=paced if j == 0 else None)

            def down(j0, p, prods, i=0):
                pe.wait_ge(S["f_lo"], prods)
                for m in range(KC):
                    product(A_UP0 + j0 + m, W_S6 + j0 + m, g_hi[p], g_lo[p], kc=GRP, per=PER_2, i=i)

            up(0, paced="n2_lo")
            with pe.Fori(0, NG // 2 - 1) as i:
                for e in range(2):
                    up(2 * GRP + e * PER_G, i)
                    down(4 * GRP + e * PER_G, e, GRP * (2 * i + e + 1), i)
            tail = 2 * GRP + PER_2 * (NG // 2 - 1)
            up(tail)
            down(tail + 2 * GRP, 0, GRP * (NG - 1))
            down(tail + PER_G, 1, GRP * NG)
            statistics(A_ST3, 2 * KC)
            for t in range(XT):
                a = A_ST3 + 1 + t
                slot_free(a)
                if t == 0:
                    pe.wait_ge(S["fin_done"], KC)
                for k in range(KC):
                    last = nc.tensor.transpose(acc[a % 2][:, P * k:P * (k + 1)], yq[:, k, P * t:P * (t + 1)], ident[:, :])
                last.then_inc(S["acc_full"], 1)

        @block.scalar
        def _(act):
            def act_of(o, x, f, **kw):
                return nc.scalar.activation(o, x, f, **kw)

            act.wait_ge(S["par_col"], 4)
            act_of(sgm2[:, :], pcol[:, 0:2 * KC], ACT.Sigmoid).then_inc(S["c_sig"], 1)
            act.wait_ge(S["lru_e"], 1)
            act_of(lru[:, 1, :], lru[:, 0, :], ACT.Exp, scale=-1.0).then_inc(S["lru_e"], 1)
            act.wait_ge(S["consts_set"], 2)

            def copy_raw(t):
                act.wait_ge(S["raw_T"], t - 1)
                if t >= 4:
                    act.wait_ge(xT_stored[t % 2], 16 * (t // 2 - 1))
                act_of(xTs[t % 2][:, :, :], acc[0][:, :].rearrange("p (k n) -> p k n", k=KC), ACT.Copy).then_inc(S["xT_copied"], 1)
                act.wait_ge(S["xT_copied"], t - 1)
                act.dma_start(xT_d.rearrange("k p n -> p k n")[:, :, P * (t - 2):P * (t - 1)], xTs[t % 2][:, :, :])\
                    .then_inc(xT_stored[t % 2], 16)

            for t in range(TT):
                act.wait_ge(x_loaded[t % NXB], 16 * (t // NXB + 1))
                if t >= 1:
                    act.wait_ge(S["sq_done"], t)
                act_of(squares0[:, :], xtile[t % NXB][:, :], ACT.Square, accum_out=ss[:, t:t + 1]).then_inc(S["sq_done"], 1)
                act.wait_ge(S["sq_done"], t + 1)
                act_of(rms[:, t:t + 1], ss[:, t:t + 1], ACT.Sqrt, scale=1.0 / D_MODEL, bias=epsc[:, 0:1]).then_inc(S["rms_done"], 1)
                if t >= 3:
                    copy_raw(t - 1)
            copy_raw(TT - 1)
            act.wait_ge(S["modrow_done"], KC)
            act_of(mrow[0:2, :], gp[0:2, :], ACT.Copy).then_inc(S["modrow_copied"], 1)
            act.wait_ge(S["xnT_copied"], TT)
            act.wait_ge(S["mod_ready"], 4)
            for k in range(KC):
                act_of(hc_hi[:, k, :], xnT[:, k, 0:CTX], ACT.Identity, scale=mod_c[:, 0, k:k + 1],
                       bias=mod_c[:, 1, k:k + 1]).then_inc(S["hx_hi_c"], 1)
            act.wait_ge(S["xn_T"], TT)
            for s in range(2):
                act.wait_ge(xT_stored[s], 16 * XT // 2)
            for k in range(KC):
                act_of(hx_hi[:, k, :], xnT[:, k, CTX:], ACT.Identity, scale=mod_x[:, 0, k:k + 1],
                       bias=mod_x[:, 1, k:k + 1]).then_inc(S["hx_hi_x"], 1)

            def lcw(t, c):
                return pcol[:, C_LCW + KC * t + c:C_LCW + KC * t + c + 1] if isinstance(c, int) else \
                    pcol[:, ds(c + (C_LCW + KC * t), 1)]

            def colat(tile, base, c):
                return tile[:, base + c:base + c + 1] if isinstance(c, int) else tile[:, ds(c + base, 1)]

            for n in range(KC):
                full(act, A_RC + n)
                act_of(xc_ctx[:, n, :], acc[n % 2][:, 0:CTX], ACT.Identity, scale=lcw(2, n),
                       bias=pcol[:, C_LCB + n:C_LCB + n + 1]).then_inc(S["ctx_centre"], 1)
            act.wait_ge(S["rope_loaded"], 32)
            for kh in range(N_KV):
                full(act, A_K + 2 * kh)
                if kh:
                    act.wait_ge(S["k_rope"], 3)
                act_of(kf[:, :], acc[0][:, :], ACT.Copy).then_inc(acc_read[0], 1)
                slot_read(act, A_K + 2 * kh)
                for q in range(4):
                    act.dma_start(ks[32 * q:32 * q + 32, :], kf[32 * (q ^ 1):32 * (q ^ 1) + 32, :]).then_inc(k_swap[kh], 16)
                full(act, A_K + 2 * kh + 1)
                act_of(kout[kh][:, 0:CTX], acc[1][:, 0:CTX], ACT.Copy).then_inc(acc_read[1], 1)
                act.wait_ge(S["k_rope"], 3 * kh + 3)
                slot_read(act, A_K + 2 * kh + 1)
                act.dma_start(k_d[kh], kout[kh][:, :]).then_inc(S["ksv_stored"], 16)
            for j in range(3):
                full(act, A_V + j)
                nt = min(4, TT - 4 * j)
                act_of(vout[:, 4 * j:4 * j + nt, :], acc[(A_V + j) % 2][:, 0:KV_WIDTH * nt].rearrange("p (t n) -> p t n", t=nt),
                       ACT.Copy).then_inc(acc_read[(A_V + j) % 2], 1)
            slot_read(act, A_V + 1)
            slot_read(act, A_V + 2)
            act.dma_start(v_d, vout[:, :, :]).then_inc(S["ksv_stored"], 16)

            def centre(c, e):
                if isinstance(c, int) and c == 0:
                    act.wait_ge(S["rest_acc"], KC)
                    act.wait_ge(acc_read[1], 7 + 0)
                    act.wait_ge(acc_read[0], 7 + 0)
                elif not isinstance(c, int):
                    act.wait_ge(S["ix_done"], 2 * c - 2)
                    act.wait_ge(S["xc_lo"], c - 1)
                if isinstance(c, int):
                    src = xc_ctx[:, c, :]
                else:
                    src = xc_ctx[:, ds(c, 1), :].rearrange("p o n -> p (o n)")
                act_of(xc[e][:, 0:CTX], src, ACT.Copy).then_inc(S["xc_centre"], 1)
                full(act, A_S1, 2, c)
                act_of(xc[e][:, CTX:], acc[1][:, :], ACT.Identity, scale=lcw(2, c), bias=colat(pcol, C_LCB, c))\
                    .then_inc(S["xc_centre"], 1)

            def gate_sigmoid(c, q):
                d, is_r = q % 2, q < 2
                act.wait_ge(S["gate_full"], 4 * c + q + 1)
                if not (isinstance(c, int) and c == 0):
                    act.wait_ge(S["m_done" if is_r else "b_done"], 2 * c - 1 + d)
                dst, base = (sr[d], C_GAB) if is_r else (si[d], C_GXB)
                act_of(dst[:, :], gp[:, 0:ALL], ACT.Sigmoid, bias=colat(pcol, base + KC * d, c)).then_inc(S["gate_read"], 1)

            def decays(c):
                if not (isinstance(c, int) and c == 0):
                    act.wait_ge(S["y_done"], 2 * c)
                for d in range(2):
                    act.wait_ge(S["gate_read"], 4 * c + 1 + d)
                    act_of(aa[d][:, :], sr[d][:, :], ACT.Exp, scale=colat(decay[:, 0, :], KC * d, c)).then_inc(S["ex_done"], 1)
                    act.wait_ge(S["ex_done"], 2 * c + d + 1)
                    act_of(sr[d][:, :], sr[d][:, :], ACT.Tanh, scale=colat(decay[:, 1, :], KC * d, c)).then_inc(S["th_done"], 1)

            def roots(c):
                for d in range(2):
                    act.wait_ge(S["m_done"], 2 * c + d + 1)
                    act_of(qq[d][:, :], qq[d][:, :], ACT.Sqrt).then_inc(S["root_done"], 1)

            def gelu(c):
                full(act, A_S1 + 1, 2, c)
                dst = Y[:, c, :] if isinstance(c, int) else Y[:, ds(c, 1), :].rearrange("p o n -> p (o n)")
                act_of(dst, acc[0][:, :], ACT.Gelu_apprx_tanh).then_inc(acc_read[0], 1)

            centre(0, 0)
            act.wait_ge(S["ksv_stored"], 48)
            act.wait_ge(S["rest_sum"], 1)
            gelu(0)

            def chunk_step(i, e):
                gate_sigmoid(i - 1, 0)
                centre(i, e)
                gate_sigmoid(i - 1, 1)
                decays(i - 1)
                gate_sigmoid(i - 1, 2)
                gate_sigmoid(i - 1, 3)
                gelu(i)
                roots(i - 1)

            pairs(act, chunk_step)
            gate_sigmoid(KC - 1, 0)
            gate_sigmoid(KC - 1, 1)
            decays(KC - 1)
            gate_sigmoid(KC - 1, 2)
            gate_sigmoid(KC - 1, 3)
            roots(KC - 1)

            def high(dst, src, sem, c):
                act_of(dst[:, c, :], src[:, c, :], ACT.Copy).then_inc(S[sem], 1)

            def merge_gate(a0, m, s, before):
                full(act, a0, 2, m)
                if before is not None:
                    act.wait_ge(*before)
                act_of(sg[s][:, :], acc[1][:, :], ACT.Sigmoid).then_inc(acc_read[1], 1)

            act.wait_ge(S["y_done"], 2 * KC)
            for c in range(KC):
                high(y_hi, Y, "y_hi_s", c)

            def store_t1(m, s):
                slot_read(act, A_S2 + 1, 2, m)
                act.dma_start(t1_d[m] if isinstance(m, int) else
                              t1_d.rearrange("k p n -> p k n")[:, ds(m, 1), :].rearrange("p o n -> p (o n)"),
                              t1[s][:, :]).then_inc(t1_stored[s], 16)

            for s in range(2):
                merge_gate(A_S2, s, s, None)
                store_t1(s, s)
            with act.Fori(1, KC // 2) as i:
                for s in range(2):
                    merge_gate(A_S2, 2 * i + s, s, (acc_read[0], (A_S2 + 1) // 2 + 2 * i + s - 1))
                    store_t1(2 * i + s, s)

            def query_pair(i):
                for s in range(2):
                    full(act, A_Q + s, 2, i)
                    if not (isinstance(i, int) and i == 0 and s == 0):
                        act.wait_ge(S["q_rope"], 2 * i + s)
                    e = (A_Q + s) % 2
                    act_of(qf[:, :], acc[e][:, :], ACT.Copy).then_inc(acc_read[e], 1)
                    slot_read(act, A_Q + s, 2, i)
                    for q in range(4):
                        act.dma_start(qs[32 * q:32 * q + 32, :], qf[32 * (q ^ 1):32 * (q ^ 1) + 32, :])\
                            .then_inc(S["q_swap"], 16)

            query_pair(0)
            with act.Fori(1, KC // 2) as i:
                query_pair(i)
            act.wait_ge(S["kf_load"], 16)
            act_of(khi[:, :, :], kff[:, :, :], ACT.Copy).then_inc(S["k_hi_s"], 1)

            def exp_head(n, kh, u, h):
                edge = is_edge(n)
                act.wait_ge(S["s_neg"], 4 * u + h + 1)
                if not (isinstance(u, int) and u < 2):
                    act.wait_ge(S["o_full"], u - 1)
                if isinstance(u, int) and u == 0 and h == 0:
                    act.wait_ge(S["q_rope"], N_HEADS)
                c0 = 1024 * (h % 2) + (256 if edge else 128)
                act_of(prob[kh][:, h, P if edge else 0:], gp[:, c0:1024 * (h % 2) + 768], ACT.Exp, scale=SCALE,
                       bias=negm[:, kh, h:h + 1], accum_out=rsum[:, kh, h:h + 1]).then_inc(S["s_exp"], 1)

            def high_block(n, kh, u, j):
                if j >= (4 if is_edge(n) else 5):
                    return
                par = j % 2 if is_edge(n) else (kh * 5 + j) % 2
                kb = j + 1 if is_edge(n) else j
                act.wait_ge(S["pt_full"], block_base(n, u) + j + 1)
                if not (isinstance(u, int) and u == 0):
                    act.wait_ge(S["o_full"], u)
                else:
                    act.wait_ge(S["k_lo_s"], 1)
                act_of(pt_hi[:, kb, :], acc[0][:, HALF * par:HALF * (par + 1)], ACT.Copy).then_inc(S["pt_hi_s"], 1)

            def sink_exp(n, kh, u):
                act.wait_ge(S["s_es"], 2 * u + 1)
                act_of(esink[:, kh, :], esink[:, kh, :], ACT.Exp).then_inc(S["s_es"], 1)

            def norm_heads(n, kh, u):
                act.wait_ge(S["s_rden"], 2 * u + 2)
                for h in range(2):
                    pr = prob[kh][:, h, P if is_edge(n) else 0:]
                    act_of(pr, pr, ACT.Identity, scale=rden[:, kh, h:h + 1]).then_inc(S["n_act"], 1)

            def out_block(n, kh, u):
                act.wait_ge(S["o_full"], u + 1)
                cols = slice(P * n, P * n + P) if isinstance(n, int) else ds(n * P, P)
                act_of(yq[:, Q_PER_KV * kh:Q_PER_KV * (kh + 1), cols],
                       acc[1][:, HALF * kh:HALF * (kh + 1)].rearrange("p (h n) -> p h n", h=Q_PER_KV), ACT.Copy)\
                    .then_inc(S["o_read"], 1)

            def attention(n, kh, u, before):
                exp_head(n, kh, u, 0)
                exp_head(n, kh, u, 1)
                if before:
                    high_block(*before, 0)
                    high_block(*before, 1)
                exp_head(n, kh, u, 2)
                if before:
                    high_block(*before, 2)
                    high_block(*before, 3)
                exp_head(n, kh, u, 3)
                if before:
                    high_block(*before, 4)
                sink_exp(n, kh, u)
                norm_heads(n, kh, u)
                if before:
                    out_block(*before)

            units(act, attention, lambda n, kh, u: ([high_block(n, kh, u, j) for j in range(NKB)], out_block(n, kh, u)))

            act.wait_ge(S["o_read"], N_KV * XT)
            for c in range(KC):
                high(y_hi, yq, "z_hi_s", c)
            for s in range(2):
                merge_gate(A_S4, s, s, None)
            with act.Fori(1, KC // 2) as i:
                for s in range(2):
                    merge_gate(A_S4, 2 * i + s, s, (S["merged"], 2 * i + s - 1))
            full(act, A_S4 + 14)
            for c in range(KC):
                act.wait_ge(S["merged"], c + 1)
                high(hx_hi, yq, "mg_hi", c)

            def square(m, a0, base):
                slot_read(act, a0 + m)
                if m or base:
                    act.wait_ge(S["ssx_done"], base + m)
                act_of(sqb[:, :], yq[:, m, :], ACT.Square).then_inc(S["sqx_done"], 1)

            for m in range(KC):
                square(m, A_S5, 0)
            full(act, A_ST2)
            act_of(nrm[1][:, :], acc[A_ST2 % 2][:, :], ACT.Sqrt, scale=1.0 / D_MODEL, bias=epsc[:, 0:1])\
                .then_inc(acc_read[A_ST2 % 2], 1)
            for c in range(KC):
                act.wait_ge(S["n2_a"], c + 1)
                act_of(y_hi[:, c, :], nrm[c % 2][:, :], ACT.Identity, bias=rest[:, 1, c:c + 1]).then_inc(S["n2_hi"], 1)

            def fcol(base, g, j):
                return colat(pcol, base + j, GRP * g)

            def gated(g, j, a0, i=0, after=None):
                p = GRP * g + j
                full(act, a0, PER_2, i)
                if not (isinstance(g, int) and g == 0):
                    act.wait_ge(S["f_lo"], p - GRP + 1)
                act_of(ca[j][:, :], acc[0][:, :], ACT.Identity, scale=fcol(C_FCW + 2 * FC, g, j), bias=fcol(C_FCB, g, j))\
                    .then_inc(S["f_centre"], 1)
                slot_read(act, a0, PER_2, i)
                act_of(ca[j][:, :], ca[j][:, :], ACT.Gelu_apprx_tanh).then_inc(S["f_gelu"], 1)
                full(act, a0 + 1, PER_2, i)
                act_of(cv[j][:, :], acc[1][:, :], ACT.Identity, scale=fcol(C_FCW + 2 * FC + FC, g, j),
                       bias=fcol(C_FCB + FC, g, j)).then_inc(S["f_centre"], 1)
                act.wait_ge(S["f_prod"], p + 1)
                if after is not None:
                    full(act, *after)
                act_of(g_hi[e_of(g)][:, j, :], ca[j][:, :], ACT.Copy).then_inc(S["f_hi"], 1)

            def e_of(g):
                return parity[0]

            parity = [0]

            def group(g, e, j0, i=0, after=None):
                parity[0] = e
                for j in range(GRP):
                    gated(g, j, A_UP0 + j0 + 2 * j, i, after)

            group(0, 0, 0)
            with act.Fori(0, NG // 2 - 1) as i:
                group(2 * i + 1, 1, 2 * GRP, i, (A_UP0 + 4 * GRP + KC - 1 - PER_G, PER_2, i))
                group(2 * i + 2, 0, 2 * GRP + PER_G, i, (A_UP0 + 4 * GRP + KC - 1, PER_2, i))
            tail = 2 * GRP + PER_2 * (NG // 2 - 1)
            group(NG - 1, 1, tail, 0, (A_UP0 + tail - 1, 0, 0))
            for m in range(KC):
                square(m, A_UP0 + tail + PER_G, KC)
            full(act, A_ST3)
            act_of(rms3[:, :], acc[A_ST3 % 2][:, :], ACT.Sqrt, scale=1.0 / D_MODEL, bias=epsc[:, 0:1])\
                .then_inc(acc_read[A_ST3 % 2], 1)
            for t in range(XT):
                a = A_ST3 + 1 + t
                full(act, a)
                if t >= 2:
                    act.wait_ge(out_stored[t % 2], 16 * (t // 2))
                act_of(otile[t % 2][:, :], acc[a % 2][:, :], ACT.Copy).then_inc(acc_read[a % 2], 1)

        @block.vector
        def _(dve):
            v = nc.vector
            links = [0]

            def link(ins):
                links[0] += 1
                ins.then_inc(S["dve_link"], 1)
                dve.wait_ge(S["dve_link"], links[0])

            def colat(tile, base, c):
                return tile[:, base + c:base + c + 1] if isinstance(c, int) else tile[:, ds(c + base, 1)]

            def chunk(tile, c, c0=0, c1=None):
                c1 = tile.shape[-1] if c1 is None else c1
                return tile[:, c, c0:c1] if isinstance(c, int) else tile[:, ds(c, 1), c0:c1].rearrange("p o n -> p (o n)")

            dve.wait_ge(S["par_T"], 1)
            v.tensor_copy(pcol[:, 0:112], acc[0][:, 0:112]).then_inc(S["par_col"], 1)
            v.tensor_copy(pcol[:, 352:368], acc[0][:, 112:128]).then_inc(S["par_col"], 1)
            v.tensor_copy(pcol[:, 112:224], acc[0][:, 128:240]).then_inc(S["par_col"], 1)
            v.tensor_copy(pcol[:, 224:352], acc[0][:, 256:384]).then_inc(S["par_col"], 1)
            dve.wait_ge(S["par_col"], 4)
            lam = pcol[:, C_LAM:C_LAM + 2 * KC]
            link(v.tensor_scalar(lru[:, 7, :], lam, -1.0, None, mult))
            v.tensor_tensor(lru[:, 0, :], lam, lru[:, 7, :], ALU.max).then_inc(S["lru_e"], 1)
            dve.wait_ge(S["c_sig"], 1)
            for j in range(2):
                v.tensor_tensor(silu2[:, :, j], pcol[:, KC * j:KC * (j + 1)], sgm2[:, KC * j:KC * (j + 1)], mult)\
                    .then_inc(S["silu_ready"], 1)
            v.tensor_scalar(nsink[:, :], sink[:, :], -1.0, None, mult).then_inc(S["lru_w"], 1)
            dve.wait_ge(S["lru_e"], 2)
            link(v.tensor_scalar(lru[:, 2, :], lru[:, 1, :], 2.0, None, add))
            link(v.reciprocal(lru[:, 3, :], lru[:, 2, :]))
            link(v.tensor_tensor(lru[:, 2, :], lru[:, 1, :], lru[:, 3, :], mult))
            link(v.tensor_tensor(lru[:, 3, :], lru[:, 2, :], lru[:, 2, :], mult))
            link(v.tensor_scalar(lru[:, 4, :], lru[:, 3, :], 1.0 / 19, None, mult))
            for o in (17, 15, 13, 11, 9, 7, 5, 3):
                link(v.scalar_tensor_tensor(out=lru[:, 4, :], in0=lru[:, 4, :], scalar=1.0 / o, in1=lru[:, 3, :],
                                            op0=add, op1=mult))
            link(v.scalar_tensor_tensor(out=lru[:, 5, :], in0=lru[:, 4, :], scalar=1.0, in1=lru[:, 2, :], op0=add, op1=mult))
            link(v.tensor_scalar(lru[:, 6, :], lru[:, 7, :], 0.0, None, ALU.max))
            link(v.scalar_tensor_tensor(out=lru[:, 4, :], in0=lru[:, 5, :], scalar=2.0, in1=lru[:, 6, :], op0=mult, op1=add))
            link(v.tensor_scalar(decay[:, 0, :], lru[:, 4, :], -LRU_C, None, mult))
            link(v.tensor_scalar(decay[:, 1, :], lru[:, 4, :], LRU_C, None, mult))

            def copy_normed(t):
                dve.wait_ge(S["xn_T"], t + 1)
                v.tensor_copy(xnT[:, :, P * t:P * (t + 1)], acc[1][:, :].rearrange("p (k n) -> p k n", k=KC))\
                    .then_inc(S["xnT_copied"], 1)

            for t in range(TT):
                dve.wait_ge(S["rms_done"], t + 1)
                link(v.reciprocal(rstd0[:, t:t + 1], rms[:, t:t + 1]))
                if t >= 2:
                    dve.wait_ge(S["xn_T"], t - 1)
                v.tensor_scalar(xn[t % 2][:, :], xtile[t % NXB][:, :], rstd0[:, t:t + 1], None, mult).then_inc(S["xn_done"], 1)
                if t >= 1:
                    copy_normed(t - 1)
            copy_normed(TT - 1)
            dve.wait_ge(S["modT_done"], 1)
            modT = acc[0][:, 0:4 * KC].rearrange("p (j e) -> p j e", e=2)
            for e, dst in ((0, mod_x), (1, mod_c)):
                v.tensor_tensor(dst[:, 1, :], modT[:, 0:KC, e], pcol[:, C_BMOD:C_BMOD + KC], add).then_inc(S["mod_ready"], 1)
                link(v.tensor_tensor(dst[:, 0, :], modT[:, KC:2 * KC, e], pcol[:, C_BMOD + KC:C_BMOD + 2 * KC], add))
            for dst in (mod_x, mod_c):
                v.scalar_tensor_tensor(out=dst[:, 0, :], in0=dst[:, 0, :], scalar=1.0, in1=pcol[:, C_N1:C_N1 + KC],
                                       op0=add, op1=mult).then_inc(S["mod_ready"], 1)
            dve.wait_ge(S["mod_ready"], 4)

            def modulated(mods, dst_lo, k, c0, w, hi, hi_sem, lo_sem, last_sem):
                link(v.tensor_scalar(mtmp[k % 2][:, 0:w], xnT[:, k, c0:c0 + w], mods[:, 0, k:k + 1], mods[:, 1, k:k + 1],
                                     mult, add))
                dve.wait_ge(S[hi_sem], k + 1)
                v.tensor_tensor(dst_lo[:, k, :], mtmp[k % 2][:, 0:w], hi[:, k, :], sub).then_inc(S[lo_sem], 1)
                dve.wait_ge(S[lo_sem], k + 1)

            for k in range(KC):
                modulated(mod_c, hc_lo, k, 0, CTX, hc_hi, "hx_hi_c", "hx_lo_c", None)
            for k in range(KC):
                modulated(mod_x, hx_lo, k, CTX, SEQ, hx_hi, "hx_hi_x", "hx_lo_x", None)

            def taps(dst, off, src, n, w_at, last_sem, lk):
                for j, sh in ((0, -2), (1, -1), (3, 1)):
                    a, b = max(0, -sh), n - max(0, sh)
                    ins = v.scalar_tensor_tensor(out=dst(off + a, off + b), in0=src[:, a + sh:b + sh], scalar=w_at(j),
                                                 in1=dst(off + a, off + b), op0=mult, op1=add)
                    if j == 3:
                        ins.then_inc(last_sem, 1)
                    else:
                        lk(ins, j)

            for n in range(KC):
                dve.wait_ge(S["ctx_centre"], n + 1)
                taps(lambda a, b: xc_ctx[:, n, a:b], 0, acc[n % 2][:, :], CTX,
                     lambda j: pcol[:, C_LCW + KC * j + n:C_LCW + KC * j + n + 1], acc_read[n % 2], lambda ins, j: link(ins))

            def add_rest(k):
                dve.wait_ge(wr_loaded[k % 2], 16 * (k // 2 + 1))
                if k == 0:
                    v.tensor_scalar(racc[:, :], wrest[0][:, :], silu2[:, 0, 0:1], None, mult).then_inc(S["rest_acc"], 1)
                else:
                    dve.wait_ge(S["rest_acc"], k)
                    v.scalar_tensor_tensor(out=racc[:, :], in0=wrest[k % 2][:, :], scalar=silu2[:, k, 0:1], in1=racc[:, :],
                                           op0=mult, op1=add).then_inc(S["rest_acc"], 1)

            def rotate_key(kh):
                slot_read(dve, A_K + 2 * kh)
                kx = kout[kh][:, CTX:]
                v.tensor_tensor(kx, kf[:, :], cosA[:, :], mult).then_inc(S["k_rope"], 1)
                dve.wait_ge(k_swap[kh], 64)
                v.tensor_tensor(ks[:, :], ks[:, :], sinA[:, :], mult).then_inc(S["k_rope"], 1)
                dve.wait_ge(S["k_rope"], 3 * kh + 2)
                v.tensor_tensor(kx, kx, ks[:, :], add).then_inc(S["k_rope"], 1)

            for k in range(3):
                add_rest(k)
            dve.wait_ge(S["rope_loaded"], 32)
            rotate_key(0)
            for k in range(3, 6):
                add_rest(k)
            rotate_key(1)
            for k in range(6, 8):
                add_rest(k)

            def convolve(c, e):
                dve.wait_ge(S["xc_centre"], 2 * c + 2)

                def in_order(ins, j):
                    ins.then_inc(S["xc_ready"], 1)
                    dve.wait_ge(S["xc_ready"], 2 * c + (1 if j == 0 else 2))
                taps(lambda a, b: xc[e][:, a:b], CTX, acc[1][:, :], SEQ,
                     lambda j: colat(pcol, C_LCW + KC * j, c), acc_read[1], in_order)

            def split_conv(c, e):
                slot_read(dve, A_S1, 2, c)
                if not (isinstance(c, int) and c == 0):
                    dve.wait_ge(S["gate_full"], 4 * c)
                v.tensor_copy(xch[:, :], xc[e][:, :]).then_inc(S["xc_hi"], 1)
                dve.wait_ge(S["xc_hi"], c + 1)
                v.tensor_tensor(xcl[:, :], xc[e][:, :], xch[:, :], sub).then_inc(S["xc_lo"], 1)

            def radicands(c):
                for d in range(2):
                    dve.wait_ge(S["sq2_done"], 2 * c + d + 1)
                    dve.wait_ge(S["th_done"], 2 * c + d + 1)
                    v.scalar_tensor_tensor(out=qq[d][:, :], in0=qq[d][:, :], scalar=1.0, in1=sr[d][:, :], op0=add, op1=mult)\
                        .then_inc(S["m_done"], 1)

            def recur(c):
                for d in range(2):
                    dve.wait_ge(S["root_done"], 2 * c + d + 1)
                    dve.wait_ge(S["ix_done"], 2 * c + d + 1)
                    v.tensor_tensor(qq[d][:, :], qq[d][:, :], si[d][:, :], mult).then_inc(S["b_done"], 1)
                    dve.wait_ge(S["b_done"], 2 * c + d + 1)
                    if d == 0:
                        part = (lambda t: t[:, 0:CTX]), (lambda t: t[:, CTX:ALL]), aa[0][:, CTX - 1:CTX]
                    else:
                        part = (lambda t: t[:, CTX - 1::-1]), (lambda t: t[:, ALL - 1:CTX - 1:-1]), aa[1][:, 0:1]
                    v.tensor_tensor_scan(part[0](aa[d]), part[0](aa[d]), part[0](qq[d]), 0.0, mult, add)\
                        .then_inc(S["scan_done"], 1)
                    dve.wait_ge(S["scan_done"], 4 * c + 2 * d + 1)
                    v.tensor_tensor_scan(part[1](aa[d]), part[1](aa[d]), part[1](qq[d]), part[2], mult, add)\
                        .then_inc(S["scan_done"], 1)
                dve.wait_ge(S["scan_done"], 4 * c + 4)
                v.tensor_tensor(aa[0][:, CTX:], aa[0][:, CTX:], aa[1][:, CTX:], add).then_inc(S["y_done"], 1)
                dve.wait_ge(S["y_done"], 2 * c + 1)
                slot_read(dve, A_S1 + 1, 2, c)
                v.tensor_tensor(chunk(Y, c), aa[0][:, CTX:], chunk(Y, c), mult).then_inc(S["y_done"], 1)

            convolve(0, 0)
            dve.wait_ge(S["rest_sum"], 1)
            v.tensor_tensor(rest[:, :, :], gp[:, 0:8 * KC].rearrange("p (j e) -> p j e", e=2)[:, :, 0].rearrange("p (a k) -> p a k", a=4),
                            pcol[:, C_BMOD + 2 * KC:C_BMOD + 6 * KC].rearrange("p (a k) -> p a k", a=4), add).then_inc(S["rest_ready"], 1)
            dve.wait_ge(S["rest_ready"], 1)
            link(v.scalar_tensor_tensor(out=a2col[:, :], in0=rest[:, 2, :], scalar=1.0, in1=pcol[:, C_N2:C_N2 + KC],
                                        op0=add, op1=mult))

            def chunk_step(i, e):
                split_conv(i - 1, 1 - e)
                if not isinstance(i, int):
                    recur(i - 2)
                convolve(i, e)
                radicands(i - 1)

            pairs(dve, chunk_step)
            split_conv(KC - 1, 1)
            recur(KC - 2)
            radicands(KC - 1)
            recur(KC - 1)

            def low(dst, src, hi, hi_sem, lo_sem, c):
                dve.wait_ge(S[hi_sem], c + 1)
                v.tensor_tensor(dst[:, c, :], src[:, c, :], hi[:, c, :], sub).then_inc(S[lo_sem], 1)

            dve.wait_ge(S["y_done"], 2 * KC)
            for c in range(KC):
                low(y_lo, Y, y_hi, "y_hi_s", "y_lo_s", c)

            def gated_branch(m, s, i=0):
                slot_read(dve, A_S2 + 2 * s, 4, i)
                full(dve, A_S2 + 2 * s + 1, 4, i)
                if not (isinstance(i, int) and i == 0):
                    dve.wait_ge(t1_stored[s], 16 * i)
                v.tensor_tensor(t1[s][:, :], acc[0][:, :], sg[s][:, :], mult).then_inc(acc_read[0], 1)

            for s in range(2):
                gated_branch(s, s)
            with dve.Fori(1, KC // 2) as i:
                for s in range(2):
                    gated_branch(2 * i + s, s, i)

            def rotate_queries(i):
                for s in range(2):
                    h = 2 * i + s
                    slot_read(dve, A_Q + s, 2, i)
                    yh = chunk(yq, h)
                    v.tensor_tensor(yh, qf[:, :], cosQ[:, :], mult).then_inc(S["q_cos"], 1)
                    dve.wait_ge(S["q_swap"], 64 * h + 64)
                    v.tensor_tensor(qs[:, :], qs[:, :], sinQ[:, :], mult).then_inc(S["q_sin"], 1)
                    dve.wait_ge(S["q_cos"], h + 1)
                    dve.wait_ge(S["q_sin"], h + 1)
                    v.tensor_tensor(yh, yh, qs[:, :], add).then_inc(S["q_rope"], 1)

            dve.wait_ge(S["rope_loaded"], 64)
            dve.wait_ge(S["y_lo_s"], KC)
            rotate_queries(0)
            with dve.Fori(1, KC // 2) as i:
                rotate_queries(i)
            v.tensor_copy(ident_b[:, :], ident[:, :]).then_inc(S["mask_b"], 1)
            v.tensor_copy(masks_b[:, :, :], masks[:, :, :]).then_inc(S["mask_b"], 1)
            dve.wait_ge(S["k_hi_s"], 1)
            v.tensor_tensor(klo[:, :, :], kff[:, :, :], khi[:, :, :], sub).then_inc(S["k_lo_s"], 1)

            def maxima(n, kh, u, h):
                pair = gp[:, 1024 * (h % 2):1024 * (h % 2) + 1024]
                dve.wait_ge(S["s_full"], 4 * u + h + 1)
                lo = 256 if is_edge(n) else 128
                v.reduce_max(smax[:, kh, h:h + 1], pair[:, lo:768], AX.X).then_inc(S["s_max"], 1)
                dve.wait_ge(S["s_max"], 4 * u + h + 1)
                hd = Q_PER_KV * kh + h
                v.tensor_scalar(negm[:, kh, h:h + 1], smax[:, kh, h:h + 1], -SCALE, nsink[:, hd:hd + 1], mult, ALU.min)\
                    .then_inc(S["s_neg"], 1)

            def denominators(n, kh, u):
                dve.wait_ge(S["s_neg"], 4 * u + 4)
                if not (isinstance(u, int) and u < 2):
                    dve.wait_ge(S["n_act"], 2 * u - 2)
                    dve.wait_ge(S["n_pool"], u - 1)
                v.tensor_tensor(esink[:, kh, :], negm[:, kh, :], sink[:, Q_PER_KV * kh:Q_PER_KV * (kh + 1)], add)\
                    .then_inc(S["s_es"], 1)
                dve.wait_ge(S["s_es"], 2 * u + 2)
                dve.wait_ge(S["s_exp"], 4 * u + 4)
                v.tensor_tensor(rden[:, kh, :], rsum[:, kh, :], esink[:, kh, :], add).then_inc(S["s_rden"], 1)
                dve.wait_ge(S["s_rden"], 2 * u + 1)
                v.reciprocal(rden[:, kh, :], rden[:, kh, :]).then_inc(S["s_rden"], 1)
                dve.wait_ge(S["s_rden"], 2 * u + 2)
                pr = prob[kh][:, 3, P if is_edge(n) else 0:]
                v.tensor_scalar(pr, pr, rden[:, kh, 3:4], None, mult).then_inc(S["n_dve"], 1)

            def low_block(n, kh, u, j):
                if j >= (4 if is_edge(n) else 5):
                    return
                par = j % 2 if is_edge(n) else (kh * 5 + j) % 2
                kb = j + 1 if is_edge(n) else j
                dve.wait_ge(S["pt_hi_s"], block_base(n, u) + j + 1)
                v.tensor_tensor(pt_lo[:, kb, :], acc[0][:, HALF * par:HALF * (par + 1)], pt_hi[:, kb, :], sub)\
                    .then_inc(S["pt_lo_s"], 1)

            def attention(n, kh, u, before):
                maxima(n, kh, u, 0)
                maxima(n, kh, u, 1)
                if before:
                    low_block(*before, 0)
                    low_block(*before, 1)
                maxima(n, kh, u, 2)
                if before:
                    low_block(*before, 2)
                    low_block(*before, 3)
                maxima(n, kh, u, 3)
                if before:
                    low_block(*before, 4)
                denominators(n, kh, u)

            units(dve, attention, lambda n, kh, u: [low_block(n, kh, u, j) for j in range(NKB)])

            for c in range(KC):
                low(y_lo, yq, y_hi, "z_hi_s", "z_lo_s", c)

            def merge(m, s, i=0):
                slot_read(dve, A_S4 + 2 * s, 4, i)
                full(dve, A_S4 + 2 * s + 1, 4, i)
                v.tensor_tensor(sg[s][:, :], acc[0][:, :], sg[s][:, :], mult).then_inc(acc_read[0], 1)
                slot_read(dve, A_S4 + 2 * s + 1, 4, i)
                dve.wait_ge(t1_loaded[s], 16 * i + 16)
                v.tensor_tensor(chunk(yq, m), sg[s][:, :], t1[s][:, :], add).then_inc(S["merged"], 1)

            dve.wait_ge(S["z_lo_s"], KC)
            for s in range(2):
                merge(s, s)
            with dve.Fori(1, KC // 2) as i:
                for s in range(2):
                    merge(2 * i + s, s, i)
            for c in range(KC):
                low(hx_lo, yq, hx_hi, "mg_hi", "mg_lo", c)
            dve.wait_ge(S["mg_lo"], KC)
            for m in range(KC):
                full(dve, A_S5 + m)
                dve.wait_ge(xr_loaded[m % 2], 16 * (m // 2 + 1))
                v.scalar_tensor_tensor(out=yq[:, m, :], in0=acc[(A_S5 + m) % 2][:, :], scalar=rest[:, 0, m:m + 1],
                                       in1=xres[m % 2][:, :], op0=mult, op1=add).then_inc(acc_read[(A_S5 + m) % 2], 1)
            slot_read(dve, A_ST2)
            v.reciprocal(rstd[:, :], nrm[1][:, :]).then_inc(S["st_rstd"], 1)
            dve.wait_ge(S["st_rstd"], 1)

            def normed(c):
                if c >= 2:
                    dve.wait_ge(S["n2_lo"], c - 1)
                v.scalar_tensor_tensor(out=nrm[c % 2][:, :], in0=yq[:, c, :], scalar=a2col[:, c:c + 1], in1=rstd[:, :],
                                       op0=mult, op1=mult).then_inc(S["n2_a"], 1)

            def normed_low(c):
                dve.wait_ge(S["n2_hi"], c + 1)
                v.tensor_scalar(nrm[c % 2][:, :], nrm[c % 2][:, :], rest[:, 1, c:c + 1], None, add).then_inc(S["n2_tmp"], 1)
                dve.wait_ge(S["n2_tmp"], c + 1)
                v.tensor_tensor(y_lo[:, c, :], nrm[c % 2][:, :], y_hi[:, c, :], sub).then_inc(S["n2_lo"], 1)

            normed(0)
            for c in range(1, KC):
                normed(c)
                normed_low(c - 1)
            normed_low(KC - 1)

            def ffn_taps(buf, slot, base, g, j, ct, last):
                dve.wait_ge(S["f_centre"], ct)
                v.scalar_tensor_tensor(out=buf[:, 1:SEQ], in0=acc[slot][:, 0:SEQ - 1], scalar=colat(pcol, base + j, GRP * g),
                                       in1=buf[:, 1:SEQ], op0=mult, op1=add).then_inc(S["f_conv"], 1)
                dve.wait_ge(S["f_conv"], ct)
                v.scalar_tensor_tensor(out=buf[:, 0:SEQ - 1], in0=acc[slot][:, 1:SEQ],
                                       scalar=colat(pcol, base + 4 * FC + j, GRP * g),
                                       in1=buf[:, 0:SEQ - 1], op0=mult, op1=add).then_inc(acc_read[slot], 1)

            def group(g, e, j0, i=0):
                for j in range(GRP):
                    p = GRP * g + j
                    ffn_taps(ca[j], 0, C_FCW, g, j, 2 * p + 1, None)
                    ffn_taps(cv[j], 1, C_FCW + FC, g, j, 2 * p + 2, None)
                    slot_read(dve, A_UP0 + j0 + 2 * j + 1, PER_2, i)
                    dve.wait_ge(S["f_gelu"], p + 1)
                    v.tensor_tensor(ca[j][:, :], ca[j][:, :], cv[j][:, :], mult).then_inc(S["f_prod"], 1)
                    dve.wait_ge(S["f_hi"], p + 1)
                    v.tensor_tensor(g_lo[e][:, j, :], ca[j][:, :], g_hi[e][:, j, :], sub).then_inc(S["f_lo"], 1)

            def add_down(j0, i=0):
                for m in range(KC):
                    full(dve, A_UP0 + j0 + m, PER_2, i)
                    s = (A_UP0 + j0 + m) % 2
                    if not (isinstance(i, int) and j0 == 4 * GRP and i == 0):
                        slot_read(dve, A_UP0 + j0 + m - 2, PER_2, i)
                    v.scalar_tensor_tensor(out=yq[:, m, :], in0=acc[s][:, :], scalar=rest[:, 3, m:m + 1], in1=yq[:, m, :],
                                           op0=mult, op1=add).then_inc(acc_read[s], 1)

            group(0, 0, 0)
            with dve.Fori(0, NG // 2 - 1) as i:
                for e in range(2):
                    group(2 * i + 1 + e, 1 - e, 2 * GRP + e * PER_G, i)
                    add_down(4 * GRP + e * PER_G, i)
            tail = 2 * GRP + PER_2 * (NG // 2 - 1)
            group(NG - 1, 1, tail)
            add_down(tail + 2 * GRP)
            add_down(tail + PER_G)
            slot_read(dve, A_ST3)
            v.reciprocal(rstd3[:, :], rms3[:, :]).then_inc(S["st_rstd"], 1)
            dve.wait_ge(S["st_rstd"], 2)
            for c in range(KC):
                v.scalar_tensor_tensor(out=yq[:, c, :], in0=yq[:, c, :], scalar=pcol[:, C_FN + c:C_FN + c + 1], in1=rstd3[:, :],
                                       op0=mult, op1=mult).then_inc(S["fin_done"], 1)


_INS = ["x", "c", "ctx", "c_ctx", "w_mod", "b_mod", "norm1_w", "w_in", "lru_conv_w", "lru_conv_b", "gate_a_w", "gate_a_b",
        "gate_x_w", "gate_x_b", "lru_lambda", "sink_logit", "w_o_rnn", "w_o_attn", "w_out", "norm2_w", "w_up", "ffn_conv_w",
        "ffn_conv_b", "w_down", "final_norm_w"]


def kernel(**inputs):
    import concourse.bacc as bacc
    from concourse.bass_utils import run_bass_kernel_spmd

    nc = bacc.Bacc("TRN2", target_bir_lowering=False, num_devices=1)
    arrays = {name: np.ascontiguousarray(inputs[name]) for name in _INS}
    cos, sin = rope_tables()
    arrays.update(ident=np.eye(P, dtype=np.float32), masks=window_masks(), rope_cos=cos, rope_sin=sin)
    dram = {n: nc.dram_tensor(f"in_{n}", a.shape, mybir.dt.from_np(a.dtype), kind="ExternalInput").ap() for n, a in arrays.items()}
    out = nc.dram_tensor("out_x", (1, SEQ, D_MODEL), mybir.dt.float32, kind="ExternalOutput").ap()
    build(nc, dram, out)
    r = run_bass_kernel_spmd(nc, [{f"in_{n}": a for n, a in arrays.items()}], core_ids=[0])
    return r.results[0]["out_x"]
```

```python
import numpy as np
import concourse.bass as bass
from concourse import mybir
from contextlib import ExitStack

P = 128
D_MODEL, SEQ, CTX = 1024, 1024, 256
GRID_W, N_HEADS, HEAD_DIM, N_KV = 64, 8, 128, 2
Q_PER_KV = N_HEADS // N_KV
KV_WIDTH = N_KV * HEAD_DIM
D_FF = 3 * D_MODEL
LRU_C, N_MOD = 8.0, 6
EPS, NEG = 1e-6, -1e30
ROPE_THETA = 10000.0
KC = D_MODEL // P
XT = SEQ // P
TT = XT + CTX // P
ALL = CTX + SEQ
HALF = 512
FC = D_FF // P
GRP = 3
NG = FC // GRP
REST = (N_MOD - 2) * D_MODEL
COL_R, COL_RG, COL_Q = 0, D_MODEL, 2 * D_MODEL
COL_K = 3 * D_MODEL
COL_V = COL_K + KV_WIDTH
COL_GA = COL_V + KV_WIDTH
COL_GB = COL_GA + D_MODEL

C_LAM, C_N1, C_BMOD, C_LCW, C_LCB = 0, 16, 24, 72, 104
C_GAB, C_GXB, C_N2, C_FCB, C_C, C_CCTX = 112, 128, 144, 152, 200, 208
C_FCW = 224
N_COL = C_FCW + 3 * 2 * FC

NORM_ON_POOL = (2, 5, 7)

W_RC, W_V, W_K = 0, 8, 10
W_S1, W_S2, W_Q, W_S4, W_S5, W_S6 = 12, 28, 44, 52, 68, 76
A_RC, A_V, A_K = 0, 8, 11
A_S1, A_S2, A_Q, A_S4, A_S5 = 15, 31, 47, 55, 71
A_ST2, A_UP0 = 79, 80
PER_G = 2 * GRP + KC
PER_2 = 2 * PER_G


def rope_tables():
    half = HEAD_DIM // 2
    inv = (np.float32(ROPE_THETA) ** (-np.arange(0, half, 2, dtype=np.float32) / np.float32(half))).astype(np.float32)
    row = np.repeat(np.arange(SEQ // GRID_W), GRID_W).astype(np.float32)
    col = np.tile(np.arange(GRID_W), SEQ // GRID_W).astype(np.float32)
    cos, sin = np.zeros((P, SEQ), np.float32), np.zeros((P, SEQ), np.float32)
    for axis, pos in enumerate((row, col)):
        ang = (pos[None, :] * inv[:, None]).astype(np.float32)
        for h in range(2):
            at = axis * half + h * (half // 2)
            cos[at:at + half // 2] = np.cos(ang)
            sin[at:at + half // 2] = np.sin(ang) * (1 if h else -1)
    return cos, sin


def window_masks():
    q, k = np.arange(P)[:, None], np.arange(P)[None, :]
    before = np.where(k >= q, 0.0, NEG).astype(np.float32)
    after = np.where(k <= q, 0.0, NEG).astype(np.float32)
    return np.stack([before, after], 1)


def build(nc, D, out):
    f32, f32r, bf16 = mybir.dt.float32, mybir.dt.float32r, mybir.dt.bfloat16
    ALU, ACT, AX = mybir.AluOpType, mybir.ActivationFunctionType, mybir.AxisListType
    ds = bass.ds
    mult, add, sub = ALU.mult, ALU.add, ALU.subtract
    SCALE = float(HEAD_DIM) ** -0.5

    CONST = 16512
    RING = CONST + 6144
    HX = RING + 6 * 4096
    B = HX + 65536
    at = {}

    def sb(name, off, shape, dt=f32):
        at[name] = (off, off + (2 if dt == bf16 else 4) * int(np.prod(shape[1:])))
        assert at[name][1] <= 229368, name
        return nc.alloc_sbuf_tensor_at(name, shape, dt, offset=off)

    cursor = [CONST]

    def const(name, shape, dt=f32):
        off = cursor[0]
        cursor[0] += ((2 if dt == bf16 else 4) * int(np.prod(shape[1:])) + 31) // 32 * 32
        assert cursor[0] <= RING, cursor[0]
        return sb(name, off, shape, dt)

    ident = const("ident", [P, P])
    ones = const("ones", [P, P])
    masks = const("masks", [P, 2, P])
    pcol = const("pcol", [P, N_COL])
    silu2 = const("silu2", [P, KC, 2])
    sgm2 = const("sgm2", [P, 2 * KC])
    mod_x = const("mod_x", [P, 2, KC])
    mod_c = const("mod_c", [P, 2, KC])
    rest = const("rest", [P, 4, KC])
    a2col = const("a2col", [P, KC])
    lru = const("lru", [P, 8, 2 * KC])
    decay = const("decay", [P, 2, 2 * KC])
    ss = const("ss", [P, TT])
    rms = const("rms", [P, TT])
    rstd0 = const("rstd0", [P, TT])
    sink = const("sink", [P, N_HEADS])
    nsink = const("nsink", [P, N_HEADS])
    epsc = const("epsc", [P, 1])
    negm = const("negm", [P, 2, Q_PER_KV])
    smax = const("smax", [P, 2, Q_PER_KV])
    rsum = const("rsum", [P, 2, Q_PER_KV])
    esink = const("esink", [P, 2, Q_PER_KV])
    rden = const("rden", [P, 2, Q_PER_KV])
    ident_b = const("ident_b", [P, P], bf16)
    masks_b = const("masks_b", [P, 2, P], bf16)

    wst = [sb(f"wst{s}", RING + 4096 * s, [P, KC, P]) for s in range(2)]
    whi2 = sb("whi_both", RING + 8192, [P, 2, KC, P], f32r)
    wlo2 = sb("wlo_both", RING + 16384, [P, 2, KC, P], f32r)
    whi = [whi2[:, s, :, :] for s in range(2)]
    wlo = [wlo2[:, s, :, :] for s in range(2)]

    hx_hi = sb("hx_hi", HX, [P, KC, SEQ], f32r)
    hx_lo = sb("hx_lo", HX + 32768, [P, KC, SEQ], f32r)
    NXB = 6
    xnTc = sb("xnTc", B, [P, KC, CTX])
    xtile = [sb(f"xtile{s}", B + 8192 + 4096 * s, [P, D_MODEL]) for s in range(NXB)]
    xn = [sb(f"xn{s}", B + 32768 + 4096 * s, [P, D_MODEL]) for s in range(2)]
    hc_hi = sb("hc_hi", B + 40960, [P, KC, CTX], f32r)
    hc_lo = sb("hc_lo", B + 49152, [P, KC, CTX], f32r)
    wmod = [sb(f"wmod{t}", (B + 57344 if t < 4 else HX - 32768) + 8192 * t, [P, 2 * D_MODEL]) for t in range(KC)]
    mrow = sb("mrow", B + 57344, [P, 2 * D_MODEL])
    xTs = [sb(f"xTs{s}", B + 65536 + 4096 * s, [P, KC, P]) for s in range(2)]
    prow = [sb(f"prow{s}", B + 90112 + 512 * s, [P, P]) for s in range(3)]
    crow = sb("crow", B + 91648, [2 * KC, P])
    mtmp = [sb(f"mtmp{s}", B + 98304 + 4096 * s, [P, KC, P]) for s in range(2)]
    kf = sb("kf", B, [P, SEQ])
    ks = sb("ks", B + 4096, [P, SEQ])
    kout = [sb(f"kout{s}", B + 8192 + 5120 * s, [P, ALL]) for s in range(N_KV)]
    vout = sb("vout", B + 18432, [P, TT, KV_WIDTH])
    cosA = sb("cosA", B + 28672, [P, SEQ])
    sinA = sb("sinA", B + 32768, [P, SEQ])
    racc = sb("racc", B + 57344, [P, REST])
    wrest = [sb(f"wrest{s}", B + 73728 + 16384 * s, [P, REST]) for s in range(2)]
    xc_ctx = sb("xc_ctx", B + 108352, [P, KC, CTX])
    Y = sb("Y", B, [P, KC, SEQ])
    s1 = B + 32768
    sr = [sb(f"sr{d}", s1 + 5120 * d, [P, ALL]) for d in range(2)]
    si = [sb(f"si{d}", s1 + 10240 + 5120 * d, [P, ALL]) for d in range(2)]
    aa = [sb(f"aa{d}", s1 + 20480 + 5120 * d, [P, ALL]) for d in range(2)]
    qq = [sb(f"qq{d}", s1 + 30720 + 5120 * d, [P, ALL]) for d in range(2)]
    gst = sb("gst", s1 + 40960, [P, 4, P])
    ghi = sb("ghi", s1 + 43008, [P, 4, P], f32r)
    glo = sb("glo", s1 + 45056, [P, 4, P], f32r)
    xc = [sb("xc0", s1 + 47104, [P, ALL]), sb("xc1", s1 + 62464, [P, ALL])]
    xch = sb("xch", s1 + 52224, [P, ALL], f32r)
    xcl = sb("xcl", s1 + 57344, [P, ALL], f32r)
    y_hi = sb("y_hi", B + 32768, [P, KC, SEQ], f32r)
    y_lo = sb("y_lo", B + 65536, [P, KC, SEQ], f32r)
    sg = [sb(f"sg{s}", B + 98304 + 4096 * s, [P, SEQ]) for s in range(2)]
    t1 = [sb(f"t1_{s}", B + 106496 + 4096 * s, [P, SEQ]) for s in range(2)]
    yq = sb("yq", B, [P, N_HEADS, SEQ])
    khi = sb("khi", B + 32768, [P, N_KV, ALL], f32r)
    klo = sb("klo", B + 43008, [P, N_KV, ALL], f32r)
    vf = sb("vf", B + 53248, [P, TT, KV_WIDTH])
    vc_hi = sb("vc_hi", B + 63488, [P, CTX // P, KV_WIDTH], f32r)
    vc_lo = sb("vc_lo", B + 65536, [P, CTX // P, KV_WIDTH], f32r)
    vl_hi = sb("vl_hi", B + 67584, [P, 3, P], f32r)
    vl_lo = sb("vl_lo", B + 69120, [P, 3, P], f32r)
    kff = sb("kff", B + 70656, [P, N_KV, ALL])
    cosQ = sb("cosQ", B + 80896, [P, SEQ])
    sinQ = sb("sinQ", B + 84992, [P, SEQ])
    qf = sb("qf", B + 101376, [P, SEQ])
    qs = sb("qs", B + 105472, [P, SEQ])
    q_hi = sb("q_hi", B + 111616, [P, Q_PER_KV, P], f32r)
    q_lo = sb("q_lo", B + 113664, [P, Q_PER_KV, P], f32r)
    NKB = 5
    prob = [sb(f"prob{s}", B + 91136 + 10240 * s, [P, Q_PER_KV, NKB * P]) for s in range(2)]
    pt_hi = sb("pt_hi", B + 70656, [P, NKB, HALF], f32r)
    pt_lo = sb("pt_lo", B + 80896, [P, NKB, HALF], f32r)
    xres = [sb(f"xres{s}", B + 98304 + 4096 * s, [P, SEQ]) for s in range(2)]
    sqb = sb("sqb", B + 106496, [P, SEQ])
    ssum = sb("ssum", B + 110592, [P, SEQ])
    rstd = sb("rstd", B + 98304, [P, SEQ])
    nrm = sb("nrm", HX + 32768, [P, KC, SEQ])
    g_hi = [sb(f"g_hi{p}", HX + 24576 * p, [P, GRP, SEQ], f32r) for p in range(2)]
    g_lo = [sb(f"g_lo{p}", HX + 24576 * p + 12288, [P, GRP, SEQ], f32r) for p in range(2)]
    ca = [sb(f"ca{s}", HX + 49152 + 4096 * s, [P, SEQ]) for s in range(GRP)]
    cv = [sb("cv0", HX + 61440, [P, SEQ]), sb("cv1", B + 98304, [P, SEQ]), sb("cv2", B + 102400, [P, SEQ])]
    otile = [sb(f"otile{t}", HX + 4096 * t, [P, D_MODEL]) for t in range(XT)]
    fnrow = sb("fnrow", B + 110592, [P, D_MODEL])

    xT_d = nc.dram_tensor("xT_scratch", [KC, P, SEQ], f32).ap()
    k_d = nc.dram_tensor("k_scratch", [N_KV, P, ALL], f32).ap()
    v_d = nc.dram_tensor("v_scratch", [P, TT, KV_WIDTH], f32).ap()
    t1_d = nc.dram_tensor("t1_scratch", [KC, P, SEQ], f32).ap()

    ctx = ExitStack()
    with ctx:
        acc = [ctx.enter_context(nc.psum_tensor(f"acc{s}", [P, SEQ], f32)) for s in range(2)]
        gp = ctx.enter_context(nc.psum_tensor("gp", [P, 4 * HALF], f32))

        names = """c_loaded c_T c_col par_loaded par_T par_col c_sig silu_ready lru_e lru_w consts_set sq_done rms_done
        xn_done raw_T xn_T xT_copied xnT_copied x_scaled x_shifted modrow_done modrow_copied modT_done
        hx_hi_c hx_lo_c hx_hi_x hx_lo_x mod_ready acc_full k_rope ksv_stored ctx_centre rest_acc rest_sum
        rest_ready w_hi w_ready g_loaded g_zero g_hi_s g_ready xc_centre xc_ready xc_hi xc_lo gate_full
        gate_read ix_done ex_done th_done sq2_done m_done root_done b_done scan_done y_done y_hi_s y_lo_s
        y_lo_pool q_swap q_cos q_sin q_rope kv_loaded rope_loaded k_hi_s k_lo_s vc_s s_full s_max s_neg
        s_exp s_es s_rden n_act n_pool n_dve mask_b pt_full pt_hi_s pt_lo_s o_full o_read mg_hi mg_lo
        sqx_done ssx_done st_full st_root st_rstd x1_half x1_part sq_last n2_a n2_a_pool n2_full n2_hi n2_lo
        n2_lo_pool z_hi_s z_lo_s merged q_s v_s f_centre f_conv f_gelu f_prod f_hi f_lo passed_sp
        passed_pool fn_loaded o_T o_sq o_rms o_done dve_link kf_load""".split()
        S = {n: ctx.enter_context(nc.semaphore(n)) for n in names}
        x_loaded = [ctx.enter_context(nc.semaphore(f"x_loaded{s}")) for s in range(NXB)]
        wm_loaded = [ctx.enter_context(nc.semaphore(f"wm_loaded{s}")) for s in range(KC)]
        wr_loaded = [ctx.enter_context(nc.semaphore(f"wr_loaded{s}")) for s in range(2)]
        w_loaded = [ctx.enter_context(nc.semaphore(f"w_loaded{s}")) for s in range(2)]
        xT_stored = [ctx.enter_context(nc.semaphore(f"xT_stored{s}")) for s in range(2)]
        acc_read = [ctx.enter_context(nc.semaphore(f"acc_read{s}")) for s in range(2)]
        k_swap = [ctx.enter_context(nc.semaphore(f"k_swap{s}")) for s in range(2)]
        t1_stored = [ctx.enter_context(nc.semaphore(f"t1_stored{s}")) for s in range(2)]
        t1_loaded = [ctx.enter_context(nc.semaphore(f"t1_loaded{s}")) for s in range(2)]
        xr_loaded = [ctx.enter_context(nc.semaphore(f"xr_loaded{s}")) for s in range(2)]
        out_stored = [ctx.enter_context(nc.semaphore(f"out_stored{s}")) for s in range(2)]

        def wait(eng, sem, value):
            eng.wait_ge(sem, value)
            if not isinstance(value, int) and (eng is nc.sync or eng is nc.gpsimd):
                eng.sem_inc(S["passed_sp" if eng is nc.sync else "passed_pool"], 1)

        def o_bank(t):
            return (gp[:, 0:SEQ], gp[:, SEQ:2 * SEQ], acc[0][:, :], acc[1][:, :])[t % 4]

        def per_channel(v):
            return v.rearrange("p (k o) -> p k o", o=1).to_broadcast([P, KC, P])

        def full(eng, a0, per=0, i=0):
            wait(eng, S["acc_full"], a0 + 1 + per * i)

        def slot_read(eng, a0, per=0, i=0):
            wait(eng, acc_read[a0 % 2], a0 // 2 + 1 + per // 2 * i)

        def pairs(eng, step):
            step(1, 1)
            with eng.Fori(1, KC // 2) as j:
                step(2 * j, 0)
                step(2 * j + 1, 1)

        def units(eng, step, finish):
            step(0, 0, 0, None)
            step(0, 1, 1, (0, 0, 0))
            step(1, 0, 2, (0, 1, 1))
            step(1, 1, 3, (1, 0, 2))
            with eng.Fori(2, XT - 1) as n:
                step(n, 0, 2 * n, (n - 1, 1, 2 * n - 1))
                step(n, 1, 2 * n + 1, (n, 0, 2 * n))
            last = XT - 1
            step(last, 0, 2 * last, (last - 1, 1, 2 * last - 1))
            step(last, 1, 2 * last + 1, (last, 0, 2 * last))
            finish(last, 1, 2 * last + 1)

        def is_edge(n):
            return isinstance(n, int) and n in (0, XT - 1)

        def pt_bank(j):
            b = j % 3
            return acc[b // 2][:, HALF * (b % 2):HALF * (b % 2 + 1)]

        att_out = acc[1][:, HALF:SEQ]

        def block_base(n, u):
            if not isinstance(n, int) or 0 < n < XT - 1:
                return 5 * u - 2
            return 4 * u if n == 0 else 5 * (2 * n) - 2 + 4 * (u - 2 * n)

        block = ctx.enter_context(nc.Block())

        @block.sync
        def _(sp):
            sp.dma_start(ident[:, :], D["ident"]).then_inc(S["c_loaded"], 16)
            sp.dma_start(crow[0:KC, :], D["c"].rearrange("o (k p) -> (o k) p", p=P)).then_inc(S["c_loaded"], 16)
            sp.dma_start(crow[KC:2 * KC, :], D["c_ctx"].rearrange("(k p) -> k p", p=P)).then_inc(S["c_loaded"], 16)
            rows = [
                (0, C_N1, D["norm1_w"].rearrange("o (k p) -> (o k) p", p=P)),
                (0, C_BMOD, D["b_mod"].rearrange("o (k p) -> (o k) p", p=P)),
                (0, C_LCW, D["lru_conv_w"].rearrange("o t (k p) -> (o t k) p", p=P)),
                (0, C_LCB, D["lru_conv_b"].rearrange("o (k p) -> (o k) p", p=P)),
                (1, C_GAB - 112, D["gate_a_b"].rearrange("o d (k p) -> (o d k) p", p=P)),
                (1, C_GXB - 112, D["gate_x_b"].rearrange("o d (k p) -> (o d k) p", p=P)),
                (0, C_LAM, D["lru_lambda"].rearrange("o d (k p) -> (o d k) p", p=P)),
                (1, C_N2 - 112, D["norm2_w"].rearrange("o (k p) -> (o k) p", p=P)),
                (1, C_FCB - 112, D["ffn_conv_b"].rearrange("o (k p) -> (o k) p", p=P)),
            ]
            small = [(prow[t][r:r + src.shape[0], :], src) for t, r, src in rows]
            fcw = D["ffn_conv_w"].rearrange("o t (k p) -> (o t k) p", p=P)
            small += [(prow[2][:, :], fcw[0:P, :]), (prow[0][112:P, :], fcw[P:144, :]),
                      (sink[:, :], D["sink_logit"].to_broadcast([P, N_HEADS])), (masks[:, :, :], D["masks"])]

            def load_small(n):
                for dst, src in small[:n]:
                    sp.dma_start(dst, src).then_inc(S["par_loaded"], 16)
                del small[:n]

            def load_tile(t):
                if t >= NXB:
                    sp.wait_ge(S["xn_T"], t - NXB + 1)
                src = D["ctx"][0, P * t:P * (t + 1), :] if t < 2 else D["x"][0, P * (t - 2):P * (t - 1), :]
                sp.dma_start(xtile[t % NXB][:, :], src).then_inc(x_loaded[t % NXB], 16)

            for t in range(KC):
                if t < 2:
                    load_tile(t)
                    load_small(5)
                sp.dma_start(wmod[t][:, :], D["w_mod"][0, P * t:P * (t + 1), 0:2 * D_MODEL])\
                    .then_inc(wm_loaded[t], 16)
                load_small(5)

            def load_w(src, n0, kc=KC, per=0, i=0):
                if n0 >= 2:
                    wait(sp, S["w_ready"], n0 - 1 + per * i)
                sp.dma_start(wst[n0 % 2][:, 0:kc, :], src).then_inc(w_loaded[n0 % 2], 16)

            w_in = D["w_in"][0].rearrange("(k p) n -> p k n", p=P)
            w_or = D["w_o_rnn"][0].rearrange("(k p) n -> p k n", p=P)
            w_oa = D["w_o_attn"][0].rearrange("(k p) n -> p k n", p=P)
            w_out = D["w_out"][0].rearrange("(k p) n -> p k n", p=P)
            w_up = D["w_up"][0].rearrange("(k p) n -> p k n", p=P)
            w_dn = D["w_down"][0].rearrange("(k p) n -> p k n", p=P)

            def col(w, base, i):
                return w[:, :, ds(base + i * P, P)] if not isinstance(i, int) else w[:, :, base + i * P:base + i * P + P]

            def load_rest(k):
                if k >= 2:
                    sp.wait_ge(S["rest_acc"], k - 1)
                elif k == 1:
                    sp.wait_ge(S["hx_lo_x"], KC)
                sp.dma_start(wrest[k % 2][:, :], D["w_mod"][0, P * k:P * (k + 1), 2 * D_MODEL:]).then_inc(wr_loaded[k % 2], 16)

            for n in range(2):
                load_w(col(w_in, COL_R, n), W_RC + n)
            for t in range(2, NXB):
                load_tile(t)
            for n in range(KC):
                load_w(col(w_in, COL_R, n + 2) if n + 2 < KC else col(w_in, COL_V, n + 2 - KC), n + 2)
                if n + NXB < TT:
                    load_tile(n + NXB)
            load_rest(0)
            load_rest(1)
            for n in range(2):
                load_w(col(w_in, COL_K, n), W_K + n)
            sp.dma_start(cosA[:, :], D["rope_cos"]).then_inc(S["rope_loaded"], 16)
            sp.dma_start(sinA[:, :], D["rope_sin"]).then_inc(S["rope_loaded"], 16)
            load_rest(2)
            load_rest(3)
            load_rest(4)
            load_w(col(w_in, COL_R, 0), W_S1)
            load_rest(5)
            load_w(col(w_in, COL_RG, 0), W_S1 + 1)
            load_rest(6)
            load_rest(7)

            def load_gates(c, waits):
                if waits is not None:
                    wait(sp, S["g_ready"], waits)
                for b in range(2):
                    for q, name in ((0, "gate_a_w"), (2, "gate_x_w")):
                        src = D[name][0].rearrange("d n k m -> k n d m")
                        if isinstance(c, int):
                            blk = src[:, 2 * c + b, :, :]
                        else:
                            blk = src[:, ds(2 * c + b, 1), :, :].rearrange("k o d m -> k (o d) m")
                        sp.dma_start(gst[64 * b:64 * b + 64, q:q + 2, 64 * b:64 * b + 64], blk).then_inc(S["g_loaded"], 16)

            sp.wait_ge(S["g_zero"], 1)
            load_gates(0, None)
            with sp.Fori(1, KC) as i:
                load_w(col(w_in, COL_R, i), W_S1, per=2, i=i)
                load_w(col(w_in, COL_RG, i), W_S1 + 1, per=2, i=i)
                load_gates(i, i)
            for m in range(2):
                load_w(col(w_in, COL_GA, m), W_S2 + m)
            with sp.Fori(0, KC - 2) as i:
                load_w(col(w_or, 0, i), W_S2 + 2, per=2, i=i)
                load_w(col(w_in, COL_GA + 2 * P, i), W_S2 + 3, per=2, i=i)
            for m in range(KC - 2, KC):
                load_w(col(w_or, 0, m), W_S2 + KC + m)
            load_w(col(w_in, COL_Q, 0), W_Q)
            load_w(col(w_in, COL_Q, 1), W_Q + 1)
            full(sp, A_S2 + 15)
            sp.dma_start(cosQ[:, :], D["rope_cos"]).then_inc(S["rope_loaded"], 16)
            sp.dma_start(sinQ[:, :], D["rope_sin"]).then_inc(S["rope_loaded"], 16)
            sp.wait_ge(S["ksv_stored"], 16 * 3)
            sp.dma_start(kff[:, :, :], k_d.rearrange("h p n -> p h n")).then_inc(S["kf_load"], 16)
            sp.dma_start(vf[:, :, :], v_d).then_inc(S["kv_loaded"], 16)
            with sp.Fori(1, KC // 2) as i:
                load_w(col(w_in, COL_Q, 2 * i), W_Q, per=2, i=i)
                load_w(col(w_in, COL_Q + P, 2 * i), W_Q + 1, per=2, i=i)
            def load_t1(m, s):
                sp.dma_start(t1[s][:, :], t1_d[m] if isinstance(m, int) else
                             t1_d.rearrange("k p n -> p k n")[:, ds(m, 1), :].rearrange("p o n -> p (o n)"))\
                    .then_inc(t1_loaded[s], 16)

            for s in range(2):
                load_w(col(w_in, COL_GB, s), W_S4 + 2 * s)
                load_w(col(w_oa, 0, s), W_S4 + 2 * s + 1)
                if s == 0:
                    sp.wait_ge(S["o_read"], N_KV * XT)
                    for e in range(2):
                        sp.wait_ge(t1_stored[e], 16 * KC // 2)
                load_t1(s, s)
            with sp.Fori(1, KC // 2) as i:
                for s in range(2):
                    load_w(col(w_in, COL_GB + P * s, 2 * i), W_S4 + 2 * s, per=4, i=i)
                    load_w(col(w_oa, P * s, 2 * i), W_S4 + 2 * s + 1, per=4, i=i)
                    wait(sp, S["merged"], 2 * i + s - 1)
                    load_t1(2 * i + s, s)

            def load_xres(m, s):
                sp.dma_start(xres[s][:, :], xT_d[m]).then_inc(xr_loaded[s], 16)

            for m in range(KC):
                load_w(col(w_out, 0, m), W_S5 + m)
                if m == 0:
                    sp.wait_ge(S["merged"], KC)
                if m >= 2:
                    slot_read(sp, A_S5 + m - 2)
                load_xres(m, m % 2)

            def load_up(g, n0, i=0):
                for j in range(GRP):
                    for h in range(2):
                        c0 = h * D_FF + j * P
                        src = w_up[:, :, c0 + GRP * P * g:c0 + GRP * P * g + P] if isinstance(g, int) else \
                            w_up[:, :, ds(c0 + g * (GRP * P), P)]
                        load_w(src, n0 + 2 * j + h, per=PER_2, i=i)

            def load_down(g, n0, i=0):
                for m in range(KC):
                    rows = w_dn[:, GRP * g:GRP * (g + 1), :] if isinstance(g, int) else w_dn[:, ds(GRP * g, GRP), :]
                    load_w(rows[:, :, P * m:P * (m + 1)], n0 + m, kc=GRP, per=PER_2, i=i)

            load_up(0, W_S6)
            sp.wait_ge(S["st_rstd"], 2)
            sp.dma_start(fnrow[:, :], D["final_norm_w"].rearrange("(o n) -> o n", o=1).to_broadcast([P, D_MODEL]))\
                .then_inc(S["fn_loaded"], 16)
            with sp.Fori(0, NG // 2 - 1) as i:
                for e in range(2):
                    load_up(2 * i + 1 + e, W_S6 + 2 * GRP + e * PER_G, i)
                    load_down(2 * i + e, W_S6 + 4 * GRP + e * PER_G, i)
            tail = W_S6 + 2 * GRP + PER_2 * (NG // 2 - 1)
            load_up(NG - 1, tail)
            load_down(NG - 2, tail + 2 * GRP)
            load_down(NG - 1, tail + PER_G)
            for t in range(XT):
                sp.wait_ge(S["o_done"], t + 1)
                sp.dma_start(out[0, P * t:P * (t + 1), :], otile[t][:, :]).then_inc(out_stored[t % 2], 16)
            for e in range(2):
                sp.wait_ge(out_stored[e], 16 * XT // 2)

        @block.gpsimd
        def _(pool):
            def ones_of(k):
                return ones[:, :].rearrange("p (o n) -> p o n", o=1).to_broadcast([P, k, P])

            def split_w(n0, kc=KC, last_use=None, per=0, i=0):
                s = n0 % 2
                wait(pool, w_loaded[s], 16 * (n0 // 2 + 1) + 16 * (per // 2) * i)
                if last_use is not None:
                    full(pool, last_use, per, i)
                nc.gpsimd.tensor_tensor(whi[s][:, 0:kc, :], wst[s][:, 0:kc, :], ones_of(kc), mult).then_inc(S["w_hi"], 1)
                pool.wait_ge(S["w_hi"], n0 + 1 + per * i)
                nc.gpsimd.tensor_tensor(wlo[s][:, 0:kc, :], wst[s][:, 0:kc, :], whi[s][:, 0:kc, :], sub)\
                    .then_inc(S["w_ready"], 1)

            nc.gpsimd.memset(ones[:, :], 1.0).then_inc(S["consts_set"], 1)
            nc.gpsimd.memset(epsc[:, :], EPS).then_inc(S["consts_set"], 1)
            def low_w(n):
                pool.wait_ge(S["w_hi"], n + 1)
                nc.gpsimd.tensor_tensor(wlo[n % 2][:, :, :], wst[n % 2][:, :, :], whi[n % 2][:, :, :], sub)\
                    .then_inc(S["w_ready"], 1)

            low_w(0)
            low_w(1)
            for n in range(XT):
                if n == XT - 1:
                    low_w(n + 2)
                pool.wait_ge(S["x_scaled"], n + 1)
                nc.gpsimd.tensor_tensor(mtmp[n % 2][:, :, :], mtmp[n % 2][:, :, :], per_channel(mod_x[:, 1, :]), add)\
                    .then_inc(S["x_shifted"], 1)
                if n < XT - 1:
                    low_w(n + 2)
            for n in range(XT + 2, W_S1):
                low_w(n)
            split_w(W_S1, last_use=A_K + 1)
            split_w(W_S1 + 1, last_use=A_K + 3)
            pool.wait_ge(S["rest_acc"], KC)
            nc.gpsimd.memset(gst[:, :, :], 0.0).then_inc(S["g_zero"], 1)

            def split_gates(c):
                wait(pool, S["g_loaded"], 64 * c + 64)
                if not isinstance(c, int) or c > 0:
                    wait(pool, S["gate_full"], 4 * c)
                nc.gpsimd.tensor_tensor(ghi[:, :, :], gst[:, :, :], ones_of(4), mult).then_inc(S["g_hi_s"], 1)
                pool.wait_ge(S["g_hi_s"], c + 1)
                nc.gpsimd.tensor_tensor(glo[:, :, :], gst[:, :, :], ghi[:, :, :], sub).then_inc(S["g_ready"], 1)

            def gated_input(c, d, e):
                pool.wait_ge(S["gate_read"], 4 * c + d + 3)
                nc.gpsimd.tensor_tensor(si[d][:, :], si[d][:, :], xc[e][:, :], mult).then_inc(S["ix_done"], 1)

            def decay_square(c, d):
                pool.wait_ge(S["ex_done"], 2 * c + d + 1)
                if not isinstance(c, int) or c > 0:
                    pool.wait_ge(S["scan_done"], 4 * c)
                nc.gpsimd.tensor_tensor(qq[d][:, :], aa[d][:, :], aa[d][:, :], mult).then_inc(S["sq2_done"], 1)

            split_gates(0)
            split_w(W_S1 + 2, last_use=A_S1)
            split_w(W_S1 + 3, last_use=A_S1 + 1)

            def chunk_step(i, e):
                split_w(W_S1 + 2, last_use=A_S1, per=2, i=i)
                decay_square(i - 1, 0)
                decay_square(i - 1, 1)
                gated_input(i - 1, 0, 1 - e)
                split_gates(i)
                gated_input(i - 1, 1, 1 - e)
                split_w(W_S1 + 3, last_use=A_S1 + 1, per=2, i=i)

            pairs(pool, chunk_step)
            decay_square(KC - 1, 0)
            decay_square(KC - 1, 1)
            gated_input(KC - 1, 0, 1)
            gated_input(KC - 1, 1, 1)
            split_w(W_S2 + 2, last_use=A_S2)
            for k in NORM_ON_POOL:
                pool.wait_ge(S["y_hi_s"], k + 1)
                nc.gpsimd.tensor_tensor(y_lo[:, k, :], Y[:, k, :], y_hi[:, k, :], sub).then_inc(S["y_lo_pool"], 1)
            split_w(W_S2 + 3, last_use=A_S2 + 1)
            with pool.Fori(1, KC) as i:
                split_w(W_S2 + 2, last_use=A_S2, per=2, i=i)
                split_w(W_S2 + 3, last_use=A_S2 + 1, per=2, i=i)
            with pool.Fori(1, KC // 2) as i:
                split_w(W_Q, last_use=A_Q - 2, per=2, i=i)
                split_w(W_Q + 1, last_use=A_Q - 1, per=2, i=i)
            pool.wait_ge(S["kv_loaded"], 16)
            nc.gpsimd.tensor_scalar(vc_hi[:, :, :], vf[:, 0:2, :], 1.0, None, mult).then_inc(S["vc_s"], 1)
            pool.wait_ge(S["vc_s"], 1)
            nc.gpsimd.tensor_tensor(vc_lo[:, :, :], vf[:, 0:2, :], vc_hi[:, :, :], sub).then_inc(S["vc_s"], 1)

            def split_queries(n, kh, u):
                if not isinstance(u, int) or u > 0:
                    wait(pool, S["s_full"], 4 * u)
                cols = slice(P * n, P * n + P) if isinstance(n, int) else ds(n * P, P)
                q = yq[:, Q_PER_KV * kh:Q_PER_KV * (kh + 1), cols]
                one = ones[:, :].rearrange("p (o n) -> p o n", o=1).to_broadcast([P, Q_PER_KV, P])
                nc.gpsimd.tensor_tensor(q_hi[:, :, :], q, one, mult).then_inc(S["q_s"], 1)
                wait(pool, S["q_s"], 2 * u + 1)
                nc.gpsimd.tensor_tensor(q_lo[:, :, :], q, q_hi[:, :, :], sub).then_inc(S["q_s"], 1)

            def split_values(n, kh, u):
                if not isinstance(u, int) or u > 0:
                    wait(pool, S["o_full"], u)
                edge = isinstance(n, int) and n in (0, XT - 1)
                t, lo, nl = (2 + (0 if n == 0 else n - 1), 1, 2) if edge else (n + 1, 0, 3)
                v = vf[:, t:t + nl, P * kh:P * (kh + 1)] if isinstance(t, int) else vf[:, ds(t, nl), P * kh:P * (kh + 1)]
                one = ones[:, :].rearrange("p (o n) -> p o n", o=1).to_broadcast([P, nl, P])
                nc.gpsimd.tensor_tensor(vl_hi[:, lo:3, :], v, one, mult).then_inc(S["v_s"], 1)
                wait(pool, S["v_s"], 2 * u + 1)
                nc.gpsimd.tensor_tensor(vl_lo[:, lo:3, :], v, vl_hi[:, lo:3, :], sub).then_inc(S["v_s"], 1)

            def norm_probs(n, kh, u):
                edge = isinstance(n, int) and n in (0, XT - 1)
                wait(pool, S["s_rden"], 2 * u + 2)
                pr = prob[kh][:, 2, P if edge else 0:]
                nc.gpsimd.tensor_tensor(pr, pr, rden[:, kh, 2:3].to_broadcast([P, pr.shape[-1]]), mult)\
                    .then_inc(S["n_pool"], 1)

            def finish(n, kh, u):
                norm_probs(n, kh, u)
                split_values(n, kh, u)

            def step(n, kh, u, before):
                if isinstance(u, int) and u < N_KV:
                    pool.wait_ge(S["q_rope"], Q_PER_KV * (u + 1))
                split_queries(n, kh, u)
                if isinstance(u, int) and u == 0:
                    split_w(W_S4, last_use=A_Q + 6)
                    split_w(W_S4 + 1, last_use=A_Q + 7)
                if before:
                    finish(*before)

            units(pool, step, finish)

            with pool.Fori(0, KC) as i:
                split_w(W_S4 + 2, last_use=A_S4, per=2, i=i)
                split_w(W_S4 + 3, last_use=A_S4 + 1, per=2, i=i)

            def add_square(m):
                pool.wait_ge(S["sqx_done"], m + 1)
                if m == 0:
                    nc.gpsimd.tensor_scalar(ssum[:, :], sqb[:, :], 1.0, None, mult).then_inc(S["ssx_done"], 1)
                else:
                    pool.wait_ge(S["ssx_done"], m)
                    nc.gpsimd.tensor_tensor(ssum[:, :], ssum[:, :], sqb[:, :], add).then_inc(S["ssx_done"], 1)

            for m in range(KC):
                if m < KC - 2:
                    split_w(W_S5 + m + 2, last_use=A_S5 + m)
                else:
                    split_w(W_S6 + m - (KC - 2), last_use=A_S5 + m)
                if m < KC - 1:
                    add_square(m)

            def norm_chunk(h, k):
                part, count = slice(HALF * h, HALF * (h + 1)), len(NORM_ON_POOL) * h + NORM_ON_POOL.index(k) + 1
                nc.gpsimd.tensor_tensor(nrm[:, k, part], yq[:, k, part], rstd[:, part], mult).then_inc(S["n2_a_pool"], 1)
                return part, count

            for h in range(2):
                pool.wait_ge(S["st_rstd"], h + 1)
                full(pool, A_S5 + KC - 1)
                todo = None
                for k in NORM_ON_POOL + (None,):
                    now = norm_chunk(h, k) + (k,) if k is not None else None
                    if todo:
                        part, count, kk = todo
                        pool.wait_ge(S["n2_hi"], KC * h + kk + 1)
                        nc.gpsimd.tensor_tensor(y_lo[:, kk, part], nrm[:, kk, part], y_hi[:, kk, part], sub)\
                            .then_inc(S["n2_lo_pool"], 1)
                    todo = now
            for j in range(2, 2 * GRP):
                split_w(W_S6 + j, last_use=A_UP0 + j - 2)

            def split_group(j0, ups, downs, i=0):
                for j in range(ups):
                    split_w(W_S6 + j0 + j, last_use=A_UP0 + j0 + j - 2, per=PER_2, i=i)
                for m in range(downs):
                    split_w(W_S6 + j0 + ups + m, kc=GRP, last_use=A_UP0 + j0 + ups + m - 2, per=PER_2, i=i)

            with pool.Fori(0, NG // 2 - 1) as i:
                split_group(2 * GRP, 2 * GRP, KC, i)
                split_group(2 * GRP + PER_G, 2 * GRP, KC, i)
            tail = 2 * GRP + PER_2 * (NG // 2 - 1)
            split_group(tail, 2 * GRP, KC)
            split_group(tail + PER_G, 0, 2)
            for m in range(KC):
                if m < KC - 2:
                    split_w(W_S6 + tail + PER_G + m + 2, kc=GRP, last_use=A_UP0 + tail + PER_G + m)

        @block.tensor
        def _(pe):
            mm = nc.tensor.matmul

            def three(out_ap, w_h, w_l, x_h, x_l, first, last):
                mm(out_ap, w_h, x_h, start=first, stop=False)
                mm(out_ap, w_h, x_l, start=False, stop=False)
                return mm(out_ap, w_l, x_h, start=False, stop=last)

            def weights(n0, per=0, i=0):
                pe.wait_ge(S["w_ready"], n0 + 1 + per * i)

            def slot_free(a0, per=0, i=0):
                slot_read(pe, a0 - 2, per, i)

            def split_by_two(by_pool, by_vector, k, h=0):
                if k in NORM_ON_POOL:
                    pe.wait_ge(S[by_pool], len(NORM_ON_POOL) * h + NORM_ON_POOL.index(k) + 1)
                else:
                    pe.wait_ge(S[by_vector], (KC - len(NORM_ON_POOL)) * h + k + 1 - sum(q < k for q in NORM_ON_POOL))

            def half(a0, n0, h, x_h, x_l, kc=KC, width=HALF, paced=None):
                s = n0 % 2
                o = acc[a0 % 2][:, HALF * h:HALF * h + width]
                for k in range(kc):
                    if callable(paced):
                        paced(k)
                    elif paced is not None:
                        pe.wait_ge(S[paced], k + 1)
                    last = three(o, whi[s][:, k, :], wlo[s][:, k, :], x_h[:, k, HALF * h:HALF * h + width],
                                 x_l[:, k, HALF * h:HALF * h + width], k == 0, k == kc - 1)
                return last

            def product(a0, n0, x_h, x_l, kc=KC, per=0, i=0, paced=None):
                weights(n0, per, i)
                slot_free(a0, per, i)
                half(a0, n0, 0, x_h, x_l, kc, paced=paced)
                half(a0, n0, 1, x_h, x_l, kc).then_inc(S["acc_full"], 1)

            pe.wait_ge(S["c_loaded"], 16 * 3)
            nc.tensor.transpose(acc[0][:, HALF:HALF + 2 * KC], crow[:, :], ident[0:2 * KC, 0:2 * KC]).then_inc(S["c_T"], 1)
            for t in range(KC):
                pe.wait_ge(wm_loaded[t], 16)
                pe.wait_ge(S["silu_ready"], 2)
                for b in range(4):
                    last = mm(gp[0:2, HALF * b:HALF * (b + 1)], silu2[:, t, :], wmod[t][:, HALF * b:HALF * (b + 1)],
                              start=t == 0, stop=t == KC - 1)
                last.then_inc(S["modrow_done"], 1)
                if t < 2:
                    pe.wait_ge(S["xn_done"], t + 1)
                    if t:
                        pe.wait_ge(S["xnT_copied"], t)
                    for k in range(KC):
                        last = nc.tensor.transpose(acc[1][:, P * k:P * (k + 1)], xn[t % 2][:, P * k:P * (k + 1)], ident[:, :])
                    last.then_inc(S["xn_T"], 1)
                if t == 2:
                    pe.wait_ge(S["par_loaded"], 16 * 13)
                    nc.tensor.transpose(acc[0][:, 0:P], prow[0][:, :], ident[:, :])
                    nc.tensor.transpose(acc[0][:, P:P + 88], prow[1][0:88, :], ident[0:88, 0:88])
                    nc.tensor.transpose(acc[0][:, 256:384], prow[2][:, :], ident[:, :]).then_inc(S["par_T"], 1)
            pe.wait_ge(S["modrow_copied"], 1)
            pe.wait_ge(S["par_col"], 4)
            for j in range(2 * KC):
                last = nc.tensor.transpose(acc[0][:, 2 * j:2 * j + 2], mrow[0:2, P * j:P * (j + 1)], ident[0:2, 0:2])
            last.then_inc(S["modT_done"], 1)

            def transpose_tile(n):
                t = n + 2
                pe.wait_ge(x_loaded[t % NXB], 16 * (t // NXB + 1))
                if n:
                    pe.wait_ge(S["xT_copied"], n)
                for k in range(KC):
                    last = nc.tensor.transpose(gp[:, SEQ + P * k:SEQ + P * (k + 1)], xtile[t % NXB][:, P * k:P * (k + 1)],
                                               ident[:, :])
                last.then_inc(S["raw_T"], 1)
                pe.wait_ge(S["xn_done"], t + 1)
                if n:
                    pe.wait_ge(S["x_scaled"], n)
                for k in range(KC):
                    last = nc.tensor.transpose(gp[:, P * k:P * (k + 1)], xn[t % 2][:, P * k:P * (k + 1)], ident[:, :])
                last.then_inc(S["xn_T"], 1)

            transpose_tile(0)
            pe.wait_ge(S["mod_ready"], 4)
            pe.wait_ge(S["xnT_copied"], 2)
            for n in range(KC):
                weights(W_RC + n)
                if n >= 2:
                    slot_free(A_RC + n)
                half(A_RC + n, W_RC + n, 0, hc_hi, hc_lo, width=CTX, paced="hx_lo_c" if n == 0 else None)\
                    .then_inc(S["acc_full"], 1)
                if n + 1 < XT:
                    transpose_tile(n + 1)
            weights(W_V + 1)
            for t in range(TT):
                a = A_V + t // 4
                if t % 4 == 0:
                    slot_free(a)
                if t >= 2:
                    pe.wait_ge(S["hx_lo_x"], t - 1)
                x_h, x_l, c0 = (hc_hi, hc_lo, P * t) if t < 2 else (hx_hi, hx_lo, P * (t - 2))
                o = acc[a % 2][:, KV_WIDTH * (t % 4):KV_WIDTH * (t % 4 + 1)]
                for k in range(KC):
                    last = three(o, x_h[:, k, c0:c0 + P], x_l[:, k, c0:c0 + P], whi2[:, :, k, :], wlo2[:, :, k, :],
                                 k == 0, k == KC - 1)
                if t % 4 == 3 or t == TT - 1:
                    last.then_inc(S["acc_full"], 1)
            for kh in range(N_KV):
                product(A_K + 2 * kh, W_K + kh, hx_hi, hx_lo)
                slot_free(A_K + 2 * kh + 1)
                half(A_K + 2 * kh + 1, W_K + kh, 0, hc_hi, hc_lo, width=CTX).then_inc(S["acc_full"], 1)
            def gate(c, q):
                if q == 0:
                    pe.wait_ge(S["g_ready"], c + 1)
                    pe.wait_ge(S["xc_lo"], c + 1)
                if not (isinstance(c, int) and c == 0 and q == 0):
                    pe.wait_ge(S["gate_read"], 4 * c + q)
                for c0, c1 in ((0, 512), (512, 1024), (1024, ALL)):
                    last = three(gp[:, c0:c1], ghi[:, q, :], glo[:, q, :], xch[:, c0:c1], xcl[:, c0:c1], True, True)
                last.then_inc(S["gate_full"], 1)

            product(A_S1, W_S1, hx_hi, hx_lo)
            product(A_S1 + 1, W_S1 + 1, hx_hi, hx_lo)
            pe.wait_ge(S["rest_acc"], KC)
            pe.wait_ge(S["modrow_copied"], 1)
            pe.wait_ge(S["consts_set"], 2)
            for m in range(4 * KC):
                last = mm(gp[:, 2 * m:2 * m + 2], racc[:, P * m:P * (m + 1)], ones[:, 0:2], start=True, stop=True)
            last.then_inc(S["rest_sum"], 1)

            pe.wait_ge(S["rest_ready"], 1)

            def chunk_step(i, e):
                for j in range(2):
                    weights(W_S1 + j, 2, i)
                    slot_free(A_S1 + j, 2, i)
                    half(A_S1 + j, W_S1 + j, 0, hx_hi, hx_lo)
                    gate(i - 1, 2 * j)
                    half(A_S1 + j, W_S1 + j, 1, hx_hi, hx_lo).then_inc(S["acc_full"], 1)
                    gate(i - 1, 2 * j + 1)

            pairs(pe, chunk_step)
            for j in range(2):
                weights(W_S2 + j)
                slot_free(A_S2 + j)
                half(A_S2 + j, W_S2 + j, 0, hx_hi, hx_lo)
                gate(KC - 1, 3 * j)
                half(A_S2 + j, W_S2 + j, 1, hx_hi, hx_lo).then_inc(S["acc_full"], 1)
                if j == 0:
                    gate(KC - 1, 1)
                    gate(KC - 1, 2)
            product(A_S2 + 2, W_S2 + 2, y_hi, y_lo, paced=lambda k: split_by_two("y_lo_pool", "y_lo_s", k))
            product(A_S2 + 3, W_S2 + 3, hx_hi, hx_lo)
            with pe.Fori(1, KC - 2) as i:
                product(A_S2 + 2, W_S2 + 2, y_hi, y_lo, per=2, i=i)
                product(A_S2 + 3, W_S2 + 3, hx_hi, hx_lo, per=2, i=i)
            product(A_S2 + 14, W_S2 + 14, y_hi, y_lo)
            product(A_S2 + 15, W_S2 + 15, y_hi, y_lo)
            with pe.Fori(0, KC // 2) as i:
                product(A_Q, W_Q, hx_hi, hx_lo, per=2, i=i)
                product(A_Q + 1, W_Q + 1, hx_hi, hx_lo, per=2, i=i)

            pe.wait_ge(S["mask_b"], 2)
            pe.wait_ge(S["k_lo_s"], 1)
            pe.wait_ge(S["vc_s"], 2)

            def score(n, kh, u, h):
                if h == 0:
                    pe.wait_ge(S["q_s"], 2 * u + 2)
                pair = gp[:, 1024 * (h % 2):1024 * (h % 2) + 1024]
                if not (isinstance(u, int) and u == 0 and h < 2):
                    pe.wait_ge(S["s_exp"], 4 * u + h - 1)
                if is_edge(n):
                    c0, o0, w = CTX + (0 if n == 0 else P * (n - 1)), 256, 256
                else:
                    c0, o0, w = (n - 1) * P + CTX, 128, 384
                def keys(t, c, width):
                    return t[:, kh, c:c + width] if isinstance(c, int) else t[:, kh, ds(c, width)]
                mm(pair[:, o0:512], q_hi[:, h, :], keys(khi, c0, w), start=True, stop=False)
                for e in range(2):
                    if not is_edge(n) or (n == 0) == (e == 1):
                        m0 = 384 if e else o0
                        mm(pair[:, m0:m0 + P], ident_b[:, :], masks_b[:, e, :], start=False, stop=False)
                mm(pair[:, o0:512], q_hi[:, h, :], keys(klo, c0, w), start=False, stop=False)
                mm(pair[:, o0:512], q_lo[:, h, :], keys(khi, c0, w), start=False, stop=True)
                three(pair[:, 512:768], q_hi[:, h, :], q_lo[:, h, :], keys(khi, 0, CTX), keys(klo, 0, CTX), True, True)\
                    .then_inc(S["s_full"], 1)

            def flip(n, kh, u, j):
                nb = 4 if is_edge(n) else 5
                if j >= nb:
                    return
                t = block_base(n, u) + j
                if j == 0 and isinstance(u, int) and u == 0:
                    slot_read(pe, A_Q + 6)
                    slot_read(pe, A_Q + 7)
                elif j == 0:
                    pe.wait_ge(S["pt_lo_s"], t)
                if j == 0:
                    pe.wait_ge(S["n_act"], 2 * u + 2)
                    pe.wait_ge(S["n_pool"], u + 1)
                    pe.wait_ge(S["n_dve"], u + 1)
                if j >= 3:
                    pe.wait_ge(S["pt_lo_s"], t - 2)
                kb = j + 1 if is_edge(n) else j
                for h in range(Q_PER_KV):
                    last = nc.tensor.transpose(pt_bank(j)[:, P * h:P * (h + 1)],
                                               prob[kh][:, h, P * kb:P * (kb + 1)], ident[:, :])
                last.then_inc(S["pt_full"], 1)

            def weigh(n, kh, u):
                nb = 4 if is_edge(n) else 5
                pe.wait_ge(S["v_s"], 2 * u + 2)
                if not (isinstance(u, int) and u == 0):
                    pe.wait_ge(S["o_read"], u)
                o = att_out
                base = block_base(n, u)
                for j in range(nb):
                    pe.wait_ge(S["pt_lo_s"], base + j + 1)
                    kb = j + 1 if is_edge(n) else j
                    if kb < 3:
                        v_h, v_l = vl_hi[:, kb, :], vl_lo[:, kb, :]
                    else:
                        v_h, v_l = (v[:, kb - 3, P * kh:P * (kh + 1)] for v in (vc_hi, vc_lo))
                    last = three(o, v_h, v_l, pt_hi[:, kb, :], pt_lo[:, kb, :], j == 0, j == nb - 1)
                last.then_inc(S["o_full"], 1)

            def attention(n, kh, u, before):
                score(n, kh, u, 0)
                score(n, kh, u, 1)
                if before:
                    for j in range(3):
                        flip(*before, j)
                score(n, kh, u, 2)
                score(n, kh, u, 3)
                if before:
                    flip(*before, 3)
                    flip(*before, 4)
                    weigh(*before)

            units(pe, attention, lambda n, kh, u: ([flip(n, kh, u, j) for j in range(NKB)], weigh(n, kh, u)))

            pe.wait_ge(S["o_read"], N_KV * XT)
            product(A_S4, W_S4, hx_hi, hx_lo)
            product(A_S4 + 1, W_S4 + 1, y_hi, y_lo, paced="z_lo_s")
            with pe.Fori(1, KC) as i:
                product(A_S4, W_S4, hx_hi, hx_lo, per=2, i=i)
                product(A_S4 + 1, W_S4 + 1, y_hi, y_lo, per=2, i=i)
            product(A_S5, W_S5, hx_hi, hx_lo, paced="mg_lo")
            product(A_S5 + 1, W_S5 + 1, hx_hi, hx_lo)
            with pe.Fori(1, KC // 2 - 1) as i:
                product(A_S5, W_S5, hx_hi, hx_lo, per=2, i=i)
                product(A_S5 + 1, W_S5 + 1, hx_hi, hx_lo, per=2, i=i)
            product(A_S5 + 6, W_S5 + 6, hx_hi, hx_lo)
            weights(W_S5 + 7)
            slot_free(A_S5 + 7)
            half(A_S5 + 7, W_S5 + 7, 0, hx_hi, hx_lo).then_inc(S["x1_half"], 1)
            half(A_S5 + 7, W_S5 + 7, 1, hx_hi, hx_lo).then_inc(S["acc_full"], 1)
            slot_free(A_ST2)
            pe.wait_ge(S["ssx_done"], KC - 1)
            stat = [acc[A_ST2 % 2][:, HALF * h:HALF * (h + 1)] for h in range(2)]
            for h in range(2):
                mm(stat[h], ones[:, :], ssum[:, HALF * h:HALF * (h + 1)], start=True, stop=False)
            for h in range(2):
                pe.wait_ge(S["sq_last"], h + 1)
                mm(stat[h], ones[:, :], sqb[:, HALF * h:HALF * (h + 1)], start=False, stop=True)\
                    .then_inc(S["acc_full" if h else "st_full"], 1)
            def up(j0, i=0, first=0):
                for j in range(first, 2 * GRP):
                    product(A_UP0 + j0 + j, W_S6 + j0 + j, y_hi, y_lo, per=PER_2, i=i)

            def down(j0, p, prods, i=0):
                pe.wait_ge(S["f_lo"], prods)
                for m in range(KC):
                    product(A_UP0 + j0 + m, W_S6 + j0 + m, g_hi[p], g_lo[p], kc=GRP, per=PER_2, i=i)

            for h in range(2):
                for j in range(2):
                    if h == 0:
                        weights(W_S6 + j)
                        slot_free(A_UP0 + j)
                    last = half(A_UP0 + j, W_S6 + j, h, y_hi, y_lo, paced=(lambda k: split_by_two("n2_lo_pool", "n2_lo", k, h)) if j == 0 else None)
                    if h == 1:
                        last.then_inc(S["acc_full"], 1)
            up(0, first=2)
            with pe.Fori(0, NG // 2 - 1) as i:
                for e in range(2):
                    up(2 * GRP + e * PER_G, i)
                    down(4 * GRP + e * PER_G, e, GRP * (2 * i + e + 1), i)
            tail = 2 * GRP + PER_2 * (NG // 2 - 1)
            up(tail)
            down(tail + 2 * GRP, 0, GRP * (NG - 1))
            down(tail + PER_G, 1, GRP * NG)
            last_down = A_UP0 + tail + PER_G + KC - 1
            for t in range(XT):
                if t == 2:
                    slot_read(pe, last_down)
                if t >= 4:
                    pe.wait_ge(S["o_done"], t - 3)
                for k in range(KC):
                    if t == 0 and k >= KC - 2:
                        slot_read(pe, last_down - (KC - 1) + k)
                    last = nc.tensor.transpose(o_bank(t)[:, P * k:P * (k + 1)], yq[:, k, P * t:P * (t + 1)], ident[:, :])
                last.then_inc(S["o_T"], 1)

        @block.scalar
        def _(act):
            def act_of(o, x, f, **kw):
                return nc.scalar.activation(o, x, f, **kw)

            act.wait_ge(S["c_col"], 1)
            act_of(sgm2[:, :], pcol[:, C_C:C_C + 2 * KC], ACT.Sigmoid).then_inc(S["c_sig"], 1)
            act.wait_ge(S["consts_set"], 2)

            def copy_raw(t):
                act.wait_ge(S["raw_T"], t - 1)
                if t >= 4:
                    act.wait_ge(xT_stored[t % 2], 16 * (t // 2 - 1))
                act_of(xTs[t % 2][:, :, :], gp[:, SEQ:2 * SEQ].rearrange("p (k n) -> p k n", k=KC), ACT.Copy).then_inc(S["xT_copied"], 1)
                act.wait_ge(S["xT_copied"], t - 1)
                act.dma_start(xT_d.rearrange("k p n -> p k n")[:, :, P * (t - 2):P * (t - 1)], xTs[t % 2][:, :, :])\
                    .then_inc(xT_stored[t % 2], 16)

            def square_sum(t):
                act.wait_ge(x_loaded[t % NXB], 16 * (t // NXB + 1))
                if t >= 2:
                    act.wait_ge(S["xn_T"], t - 1)
                act_of(xn[t % 2][:, :], xtile[t % NXB][:, :], ACT.Square, accum_out=ss[:, t:t + 1]).then_inc(S["sq_done"], 1)
                act.wait_ge(S["sq_done"], t + 1)
                act_of(rms[:, t:t + 1], ss[:, t:t + 1], ACT.Sqrt, scale=1.0 / D_MODEL, bias=epsc[:, 0:1]).then_inc(S["rms_done"], 1)

            for t in range(2):
                square_sum(t)
            act.wait_ge(S["lru_e"], 1)
            act_of(lru[:, 1, :], lru[:, 0, :], ACT.Exp, scale=-1.0).then_inc(S["lru_e"], 1)
            for t in range(2, 4):
                square_sum(t)
            act.wait_ge(S["modrow_done"], KC)
            act_of(mrow[0:2, :], gp[0:2, :], ACT.Copy).then_inc(S["modrow_copied"], 1)
            def high_w(n0, last_use=None):
                act.wait_ge(w_loaded[n0 % 2], 16 * (n0 // 2 + 1))
                if last_use is not None:
                    full(act, last_use)
                act_of(whi[n0 % 2][:, :, :], wst[n0 % 2][:, :, :], ACT.Copy).then_inc(S["w_hi"], 1)

            high_w(W_RC)
            high_w(W_RC + 1)
            act.wait_ge(S["xnT_copied"], 2)
            act.wait_ge(S["mod_ready"], 4)
            for k in range(KC):
                act_of(hc_hi[:, k, :], xnTc[:, k, :], ACT.Identity, scale=mod_c[:, 0, k:k + 1],
                       bias=mod_c[:, 1, k:k + 1]).then_inc(S["hx_hi_c"], 1)

            def lcw(t, c):
                return pcol[:, C_LCW + KC * t + c:C_LCW + KC * t + c + 1] if isinstance(c, int) else \
                    pcol[:, ds(c + (C_LCW + KC * t), 1)]

            def colat(tile, base, c):
                return tile[:, base + c:base + c + 1] if isinstance(c, int) else tile[:, ds(c + base, 1)]

            for n in range(KC):
                copy_raw(n + 2)
                if n + 4 < TT:
                    square_sum(n + 4)
                full(act, A_RC + n)
                if n == KC - 1:
                    high_w(n + 2, A_RC + n)
                act_of(xc_ctx[:, n, :], acc[n % 2][:, 0:CTX], ACT.Identity, scale=lcw(2, n),
                       bias=pcol[:, C_LCB + n:C_LCB + n + 1]).then_inc(S["ctx_centre"], 1)
                if n < KC - 1:
                    high_w(n + 2, A_RC + n)
                act.wait_ge(S["x_shifted"], n + 1)
                act_of(hx_hi[:, :, P * n:P * (n + 1)], mtmp[n % 2][:, :, :], ACT.Copy).then_inc(S["hx_hi_x"], 1)
            act.wait_ge(S["hx_lo_x"], KC)
            for j in range(3):
                full(act, A_V + j)
                nt = min(4, TT - 4 * j)
                act_of(vout[:, 4 * j:4 * j + nt, :], acc[(A_V + j) % 2][:, 0:KV_WIDTH * nt].rearrange("p (t n) -> p t n", t=nt),
                       ACT.Copy).then_inc(acc_read[(A_V + j) % 2], 1)
            high_w(W_K, A_V + 2)
            high_w(W_K + 1, A_V + 2)
            slot_read(act, A_V + 1)
            slot_read(act, A_V + 2)
            act.dma_start(v_d, vout[:, :, :]).then_inc(S["ksv_stored"], 16)

            for kh in range(N_KV):
                full(act, A_K + 2 * kh)
                if kh:
                    act.wait_ge(S["k_rope"], 3)
                act_of(kf[:, :], acc[A_K % 2][:, :], ACT.Copy).then_inc(acc_read[A_K % 2], 1)
                slot_read(act, A_K + 2 * kh)
                for q in range(4):
                    act.dma_start(ks[32 * q:32 * q + 32, :], kf[32 * (q ^ 1):32 * (q ^ 1) + 32, :]).then_inc(k_swap[kh], 16)
                full(act, A_K + 2 * kh + 1)
                act_of(kout[kh][:, 0:CTX], acc[1 - A_K % 2][:, 0:CTX], ACT.Copy).then_inc(acc_read[1 - A_K % 2], 1)
                act.wait_ge(S["k_rope"], 3 * kh + 3)
                slot_read(act, A_K + 2 * kh + 1)
                act.dma_start(k_d[kh], kout[kh][:, :]).then_inc(S["ksv_stored"], 16)
            def centre(c, e):
                if isinstance(c, int) and c == 0:
                    act.wait_ge(S["rest_acc"], KC)
                    slot_read(act, A_RC + 6)
                    slot_read(act, A_RC + 7)
                elif not isinstance(c, int):
                    act.wait_ge(S["ix_done"], 2 * c - 2)
                    act.wait_ge(S["xc_lo"], c - 1)
                if isinstance(c, int):
                    src = xc_ctx[:, c, :]
                else:
                    src = xc_ctx[:, ds(c, 1), :].rearrange("p o n -> p (o n)")
                act_of(xc[e][:, 0:CTX], src, ACT.Copy).then_inc(S["xc_centre"], 1)
                full(act, A_S1, 2, c)
                act_of(xc[e][:, CTX:], acc[1][:, :], ACT.Identity, scale=lcw(2, c), bias=colat(pcol, C_LCB, c))\
                    .then_inc(S["xc_centre"], 1)

            def gate_sigmoid(c, q):
                d, is_r = q % 2, q < 2
                act.wait_ge(S["gate_full"], 4 * c + q + 1)
                if not (isinstance(c, int) and c == 0):
                    act.wait_ge(S["m_done" if is_r else "b_done"], 2 * c - 1 + d)
                dst, base = (sr[d], C_GAB) if is_r else (si[d], C_GXB)
                act_of(dst[:, :], gp[:, 0:ALL], ACT.Sigmoid, bias=colat(pcol, base + KC * d, c)).then_inc(S["gate_read"], 1)

            def decays(c):
                if not (isinstance(c, int) and c == 0):
                    act.wait_ge(S["y_done"], 2 * c)
                for d in range(2):
                    act.wait_ge(S["gate_read"], 4 * c + 1 + d)
                    act_of(aa[d][:, :], sr[d][:, :], ACT.Exp, scale=colat(decay[:, 0, :], KC * d, c)).then_inc(S["ex_done"], 1)
                    act.wait_ge(S["ex_done"], 2 * c + d + 1)
                    act_of(sr[d][:, :], sr[d][:, :], ACT.Tanh, scale=colat(decay[:, 1, :], KC * d, c)).then_inc(S["th_done"], 1)

            def roots(c):
                for d in range(2):
                    act.wait_ge(S["m_done"], 2 * c + d + 1)
                    act_of(qq[d][:, :], qq[d][:, :], ACT.Sqrt).then_inc(S["root_done"], 1)

            def gelu(c):
                full(act, A_S1 + 1, 2, c)
                dst = Y[:, c, :] if isinstance(c, int) else Y[:, ds(c, 1), :].rearrange("p o n -> p (o n)")
                act_of(dst, acc[0][:, :], ACT.Gelu_apprx_tanh).then_inc(acc_read[0], 1)

            centre(0, 0)
            act.wait_ge(S["ksv_stored"], 48)
            gelu(0)
            act.wait_ge(S["rest_sum"], 1)

            def chunk_step(i, e):
                gate_sigmoid(i - 1, 0)
                centre(i, e)
                gate_sigmoid(i - 1, 1)
                decays(i - 1)
                gate_sigmoid(i - 1, 2)
                gate_sigmoid(i - 1, 3)
                gelu(i)
                roots(i - 1)

            pairs(act, chunk_step)
            gate_sigmoid(KC - 1, 0)
            gate_sigmoid(KC - 1, 1)
            decays(KC - 1)
            gate_sigmoid(KC - 1, 2)
            gate_sigmoid(KC - 1, 3)
            roots(KC - 1)

            def high(dst, src, sem, c):
                act_of(dst[:, c, :], src[:, c, :], ACT.Copy).then_inc(S[sem], 1)

            def merge_gate(a0, m, s, before):
                full(act, a0, 2, m)
                if before is not None:
                    act.wait_ge(*before)
                act_of(sg[s][:, :], acc[1][:, :], ACT.Sigmoid).then_inc(acc_read[1], 1)

            act.wait_ge(S["ix_done"], 2 * KC)
            for m in range(2):
                full(act, A_S2 + m)
                e = (A_S2 + m) % 2
                act_of(sg[m][:, :], acc[e][:, :], ACT.Sigmoid).then_inc(acc_read[e], 1)
            act.wait_ge(S["y_done"], 2 * KC - 2)
            act.wait_ge(S["m_done"], 2 * KC)
            for c in range(2):
                high(y_hi, Y, "y_hi_s", c)
            act.wait_ge(S["b_done"], 2 * KC)
            for c in range(2, 5):
                high(y_hi, Y, "y_hi_s", c)
            act.wait_ge(S["y_done"], 2 * KC)
            for c in range(5, KC):
                high(y_hi, Y, "y_hi_s", c)

            def store_t1(m, s, a0, per=0, i=0):
                slot_read(act, a0, per, i)
                act.dma_start(t1_d[m] if isinstance(m, int) else
                              t1_d.rearrange("k p n -> p k n")[:, ds(m, 1), :].rearrange("p o n -> p (o n)"),
                              t1[s][:, :]).then_inc(t1_stored[s], 16)

            with act.Fori(0, KC // 2 - 1) as i:
                for s in range(2):
                    store_t1(2 * i + s, s, A_S2 + 2 + 2 * s, 4, i)
                    full(act, A_S2 + 3 + 2 * s, 4, i)
                    act_of(sg[s][:, :], acc[0][:, :], ACT.Sigmoid).then_inc(acc_read[0], 1)
            store_t1(KC - 2, 0, A_S2 + 14)
            store_t1(KC - 1, 1, A_S2 + 15)

            def query_pair(i):
                for s in range(2):
                    full(act, A_Q + s, 2, i)
                    if not (isinstance(i, int) and i == 0 and s == 0):
                        act.wait_ge(S["q_rope"], 2 * i + s)
                    e = (A_Q + s) % 2
                    act_of(qf[:, :], acc[e][:, :], ACT.Copy).then_inc(acc_read[e], 1)
                    slot_read(act, A_Q + s, 2, i)
                    for q in range(4):
                        act.dma_start(qs[32 * q:32 * q + 32, :], qf[32 * (q ^ 1):32 * (q ^ 1) + 32, :])\
                            .then_inc(S["q_swap"], 16)

            for e in range(2):
                act.wait_ge(t1_stored[e], 16 * KC // 2)
            query_pair(0)
            with act.Fori(1, KC // 2 - 1) as i:
                query_pair(i)
            act.wait_ge(S["kf_load"], 16)
            act_of(khi[:, :, :], kff[:, :, :], ACT.Copy).then_inc(S["k_hi_s"], 1)
            query_pair(KC // 2 - 1)

            def exp_head(n, kh, u, h):
                edge = is_edge(n)
                act.wait_ge(S["s_neg"], 4 * u + h + 1)
                if not (isinstance(u, int) and u < 2):
                    act.wait_ge(S["o_full"], u - 1)
                if isinstance(u, int) and u == 1 and h == 0:
                    act.wait_ge(S["q_rope"], N_HEADS)
                c0 = 1024 * (h % 2) + (256 if edge else 128)
                act_of(prob[kh][:, h, P if edge else 0:], gp[:, c0:1024 * (h % 2) + 768], ACT.Exp, scale=SCALE,
                       bias=negm[:, kh, h:h + 1], accum_out=rsum[:, kh, h:h + 1]).then_inc(S["s_exp"], 1)

            def high_block(n, kh, u, j):
                if j >= (4 if is_edge(n) else 5):
                    return
                kb = j + 1 if is_edge(n) else j
                act.wait_ge(S["pt_full"], block_base(n, u) + j + 1)
                if not (isinstance(u, int) and u == 0):
                    act.wait_ge(S["o_full"], u)
                else:
                    act.wait_ge(S["k_lo_s"], 1)
                act_of(pt_hi[:, kb, :], pt_bank(j), ACT.Copy).then_inc(S["pt_hi_s"], 1)

            def sink_exp(n, kh, u):
                act.wait_ge(S["s_es"], 2 * u + 1)
                act_of(esink[:, kh, :], esink[:, kh, :], ACT.Exp).then_inc(S["s_es"], 1)

            def norm_heads(n, kh, u):
                act.wait_ge(S["s_rden"], 2 * u + 2)
                for h in range(2):
                    pr = prob[kh][:, h, P if is_edge(n) else 0:]
                    act_of(pr, pr, ACT.Identity, scale=rden[:, kh, h:h + 1]).then_inc(S["n_act"], 1)

            def out_block(n, kh, u):
                act.wait_ge(S["o_full"], u + 1)
                cols = slice(P * n, P * n + P) if isinstance(n, int) else ds(n * P, P)
                act_of(yq[:, Q_PER_KV * kh:Q_PER_KV * (kh + 1), cols],
                       att_out.rearrange("p (h n) -> p h n", h=Q_PER_KV), ACT.Copy)\
                    .then_inc(S["o_read"], 1)

            def attention(n, kh, u, before):
                exp_head(n, kh, u, 0)
                exp_head(n, kh, u, 1)
                if before:
                    for j in range(4):
                        high_block(*before, j)
                exp_head(n, kh, u, 2)
                if before:
                    high_block(*before, 4)
                exp_head(n, kh, u, 3)
                sink_exp(n, kh, u)
                norm_heads(n, kh, u)
                if before:
                    out_block(*before)

            units(act, attention, lambda n, kh, u: ([high_block(n, kh, u, j) for j in range(NKB)], out_block(n, kh, u)))

            act.wait_ge(S["o_read"], N_KV * XT)
            for c in range(KC):
                high(y_hi, yq, "z_hi_s", c)
            for s in range(2):
                merge_gate(A_S4, s, s, None)
            with act.Fori(1, KC // 2) as i:
                for s in range(2):
                    merge_gate(A_S4, 2 * i + s, s, (S["merged"], 2 * i + s - 1))
            full(act, A_S4 + 14)
            for c in range(KC):
                act.wait_ge(S["merged"], c + 1)
                high(hx_hi, yq, "mg_hi", c)

            for m in range(KC - 1):
                slot_read(act, A_S5 + m)
                if m:
                    act.wait_ge(S["ssx_done"], m)
                act_of(sqb[:, :], yq[:, m, :], ACT.Square).then_inc(S["sqx_done"], 1)
            act.wait_ge(S["ssx_done"], KC - 1)
            for h in range(2):
                if h == 0:
                    act.wait_ge(S["x1_part"], 1)
                else:
                    slot_read(act, A_S5 + KC - 1)
                part = slice(HALF * h, HALF * (h + 1))
                act_of(sqb[:, part], yq[:, KC - 1, part], ACT.Square).then_inc(S["sq_last"], 1)
            for h in range(2):
                part = slice(HALF * h, HALF * (h + 1))
                if h == 0:
                    act.wait_ge(S["st_full"], 1)
                else:
                    full(act, A_ST2)
                act_of(rstd[:, part], acc[A_ST2 % 2][:, part], ACT.Sqrt, scale=1.0 / D_MODEL, bias=epsc[:, 0:1])\
                    .then_inc(acc_read[A_ST2 % 2] if h else S["st_root"], 1)
            for h in range(2):
                part = slice(HALF * h, HALF * (h + 1))
                for k in range(KC):
                    if k in NORM_ON_POOL:
                        q = NORM_ON_POOL.index(k) + 1 + len(NORM_ON_POOL) * h
                        act.wait_ge(S["n2_a_pool"], q)
                        act_of(nrm[:, k, part], nrm[:, k, part], ACT.Identity, scale=a2col[:, k:k + 1],
                               bias=rest[:, 1, k:k + 1]).then_inc(S["n2_full"], 1)
                        act.wait_ge(S["n2_full"], q)
                        act_of(y_hi[:, k, part], nrm[:, k, part], ACT.Copy).then_inc(S["n2_hi"], 1)
                    else:
                        act.wait_ge(S["n2_a"], (KC - len(NORM_ON_POOL)) * h + k + 1 - sum(q < k for q in NORM_ON_POOL))
                        act_of(y_hi[:, k, part], nrm[:, k, part], ACT.Identity, bias=rest[:, 1, k:k + 1])\
                            .then_inc(S["n2_hi"], 1)

            def fcol(base, g, j):
                return colat(pcol, base + j, GRP * g)

            def gated(g, e, j, a0, i=0, after=None):
                p = GRP * g + j
                full(act, a0, PER_2, i)
                if not (isinstance(g, int) and g == 0):
                    act.wait_ge(S["f_lo"], p - GRP + 1)
                act_of(ca[j][:, :], acc[0][:, :], ACT.Identity, scale=fcol(C_FCW + 2 * FC, g, j), bias=fcol(C_FCB, g, j))\
                    .then_inc(S["f_centre"], 1)
                slot_read(act, a0, PER_2, i)
                act_of(ca[j][:, :], ca[j][:, :], ACT.Gelu_apprx_tanh).then_inc(S["f_gelu"], 1)
                full(act, a0 + 1, PER_2, i)
                act_of(cv[j][:, :], acc[1][:, :], ACT.Identity, scale=fcol(C_FCW + 2 * FC + FC, g, j),
                       bias=fcol(C_FCB + FC, g, j)).then_inc(S["f_centre"], 1)
                act.wait_ge(S["f_prod"], p + 1)
                if after is not None:
                    full(act, *after)
                act_of(g_hi[e][:, j, :], ca[j][:, :], ACT.Copy).then_inc(S["f_hi"], 1)

            def group(g, e, j0, i=0, after=None):
                for j in range(GRP):
                    gated(g, e, j, A_UP0 + j0 + 2 * j, i, after)

            group(0, 0, 0)
            with act.Fori(0, NG // 2 - 1) as i:
                group(2 * i + 1, 1, 2 * GRP, i, (A_UP0 + 4 * GRP + KC - 1 - PER_G, PER_2, i))
                group(2 * i + 2, 0, 2 * GRP + PER_G, i, (A_UP0 + 4 * GRP + KC - 1, PER_2, i))
            tail = 2 * GRP + PER_2 * (NG // 2 - 1)
            group(NG - 1, 1, tail, 0, (A_UP0 + tail - 1, 0, 0))
            for t in range(XT):
                act.wait_ge(S["o_T"], t + 1)
                if t:
                    act.wait_ge(S["o_sq"], t)
                act_of(sqb[:, :], o_bank(t), ACT.Square, accum_out=ss[:, t:t + 1]).then_inc(S["o_sq"], 1)
                act.wait_ge(S["o_sq"], t + 1)
                act_of(rms[:, t:t + 1], ss[:, t:t + 1], ACT.Sqrt, scale=1.0 / D_MODEL, bias=epsc[:, 0:1]).then_inc(S["o_rms"], 1)

        @block.vector
        def _(dve):
            v = nc.vector
            links = [0]

            def link(ins):
                links[0] += 1
                ins.then_inc(S["dve_link"], 1)
                dve.wait_ge(S["dve_link"], links[0])

            def colat(tile, base, c):
                return tile[:, base + c:base + c + 1] if isinstance(c, int) else tile[:, ds(c + base, 1)]

            def chunk(tile, c, c0=0, c1=None):
                c1 = tile.shape[-1] if c1 is None else c1
                return tile[:, c, c0:c1] if isinstance(c, int) else tile[:, ds(c, 1), c0:c1].rearrange("p o n -> p (o n)")

            dve.wait_ge(S["c_T"], 1)
            v.tensor_copy(pcol[:, C_C:C_C + 2 * KC], acc[0][:, HALF:HALF + 2 * KC]).then_inc(S["c_col"], 1)
            dve.wait_ge(S["c_sig"], 1)
            for j in range(2):
                v.tensor_tensor(silu2[:, :, j], pcol[:, C_C + KC * j:C_C + KC * (j + 1)], sgm2[:, KC * j:KC * (j + 1)], mult)\
                    .then_inc(S["silu_ready"], 1)

            def normalise(t):
                dve.wait_ge(S["rms_done"], t + 1)
                link(v.reciprocal(rstd0[:, t:t + 1], rms[:, t:t + 1]))
                v.tensor_scalar(xn[t % 2][:, :], xtile[t % NXB][:, :], rstd0[:, t:t + 1], None, mult).then_inc(S["xn_done"], 1)

            for t in range(2):
                normalise(t)
                dve.wait_ge(S["xn_T"], t + 1)
                v.tensor_copy(xnTc[:, :, P * t:P * (t + 1)], acc[1][:, :].rearrange("p (k n) -> p k n", k=KC))\
                    .then_inc(S["xnT_copied"], 1)
            dve.wait_ge(S["par_T"], 1)
            v.tensor_copy(pcol[:, 0:112], acc[0][:, 0:112]).then_inc(S["par_col"], 1)
            v.tensor_copy(pcol[:, 352:368], acc[0][:, 112:128]).then_inc(S["par_col"], 1)
            v.tensor_copy(pcol[:, 112:200], acc[0][:, 128:216]).then_inc(S["par_col"], 1)
            v.tensor_copy(pcol[:, 224:352], acc[0][:, 256:384]).then_inc(S["par_col"], 1)
            dve.wait_ge(S["par_col"], 4)
            lam = pcol[:, C_LAM:C_LAM + 2 * KC]
            link(v.tensor_scalar(lru[:, 7, :], lam, -1.0, None, mult))
            v.tensor_tensor(lru[:, 0, :], lam, lru[:, 7, :], ALU.max).then_inc(S["lru_e"], 1)
            v.tensor_scalar(nsink[:, :], sink[:, :], -1.0, None, mult).then_inc(S["lru_w"], 1)
            dve.wait_ge(S["lru_e"], 2)
            link(v.tensor_scalar(lru[:, 2, :], lru[:, 1, :], 2.0, None, add))
            link(v.reciprocal(lru[:, 3, :], lru[:, 2, :]))
            link(v.tensor_tensor(lru[:, 2, :], lru[:, 1, :], lru[:, 3, :], mult))
            link(v.tensor_tensor(lru[:, 3, :], lru[:, 2, :], lru[:, 2, :], mult))
            link(v.tensor_scalar(lru[:, 4, :], lru[:, 3, :], 1.0 / 19, None, mult))
            for o in (17, 15, 13, 11, 9, 7, 5, 3):
                link(v.scalar_tensor_tensor(out=lru[:, 4, :], in0=lru[:, 4, :], scalar=1.0 / o, in1=lru[:, 3, :],
                                            op0=add, op1=mult))
            link(v.scalar_tensor_tensor(out=lru[:, 5, :], in0=lru[:, 4, :], scalar=1.0, in1=lru[:, 2, :], op0=add, op1=mult))
            link(v.tensor_scalar(lru[:, 6, :], lru[:, 7, :], 0.0, None, ALU.max))
            link(v.scalar_tensor_tensor(out=lru[:, 4, :], in0=lru[:, 5, :], scalar=2.0, in1=lru[:, 6, :], op0=mult, op1=add))
            link(v.tensor_scalar(decay[:, 0, :], lru[:, 4, :], -LRU_C, None, mult))
            link(v.tensor_scalar(decay[:, 1, :], lru[:, 4, :], LRU_C, None, mult))

            normalise(2)
            normalise(3)
            dve.wait_ge(S["modT_done"], 1)
            modT = acc[0][:, 0:4 * KC].rearrange("p (j e) -> p j e", e=2)
            for e, dst in ((0, mod_x), (1, mod_c)):
                v.tensor_tensor(dst[:, 1, :], modT[:, 0:KC, e], pcol[:, C_BMOD:C_BMOD + KC], add).then_inc(S["mod_ready"], 1)
                link(v.tensor_tensor(dst[:, 0, :], modT[:, KC:2 * KC, e], pcol[:, C_BMOD + KC:C_BMOD + 2 * KC], add))
            for dst in (mod_x, mod_c):
                v.scalar_tensor_tensor(out=dst[:, 0, :], in0=dst[:, 0, :], scalar=1.0, in1=pcol[:, C_N1:C_N1 + KC],
                                       op0=add, op1=mult).then_inc(S["mod_ready"], 1)
            dve.wait_ge(S["mod_ready"], 4)

            dve.wait_ge(S["xnT_copied"], 2)
            for k in range(KC):
                m = mtmp[k % 2][:, 0:2, :].rearrange("p a n -> p (a n)")
                link(v.tensor_scalar(m, xnTc[:, k, :], mod_c[:, 0, k:k + 1], mod_c[:, 1, k:k + 1], mult, add))
                dve.wait_ge(S["hx_hi_c"], k + 1)
                v.tensor_tensor(hc_lo[:, k, :], m, hc_hi[:, k, :], sub).then_inc(S["hx_lo_c"], 1)
                dve.wait_ge(S["hx_lo_c"], k + 1)

            def taps(dst, src, n, w_at, last_sem, lk):
                for j, sh in ((0, -2), (1, -1), (3, 1)):
                    a, b = max(0, -sh), n - max(0, sh)
                    ins = v.scalar_tensor_tensor(out=dst(a, b), in0=src[:, a + sh:b + sh], scalar=w_at(j),
                                                 in1=dst(a, b), op0=mult, op1=add)
                    if j == 3:
                        ins.then_inc(last_sem, 1)
                    else:
                        lk(ins, j)

            for n in range(KC):
                dve.wait_ge(S["xn_T"], n + 3)
                if n >= 2:
                    dve.wait_ge(S["hx_lo_x"], n - 1)
                v.tensor_tensor(mtmp[n % 2][:, :, :], gp[:, 0:SEQ].rearrange("p (k n) -> p k n", k=KC),
                                per_channel(mod_x[:, 0, :]), mult).then_inc(S["x_scaled"], 1)
                dve.wait_ge(S["ctx_centre"], n + 1)
                taps(lambda a, b: xc_ctx[:, n, a:b], acc[n % 2][:, :], CTX,
                     lambda j: pcol[:, C_LCW + KC * j + n:C_LCW + KC * j + n + 1], acc_read[n % 2], lambda ins, j: link(ins))
                if n + 4 < TT:
                    normalise(n + 4)
                dve.wait_ge(S["hx_hi_x"], n + 1)
                v.tensor_tensor(hx_lo[:, :, P * n:P * (n + 1)], mtmp[n % 2][:, :, :], hx_hi[:, :, P * n:P * (n + 1)], sub)\
                    .then_inc(S["hx_lo_x"], 1)

            def add_rest(k):
                dve.wait_ge(wr_loaded[k % 2], 16 * (k // 2 + 1))
                if k == 0:
                    v.tensor_scalar(racc[:, :], wrest[0][:, :], silu2[:, 0, 0:1], None, mult).then_inc(S["rest_acc"], 1)
                else:
                    dve.wait_ge(S["rest_acc"], k)
                    v.scalar_tensor_tensor(out=racc[:, :], in0=wrest[k % 2][:, :], scalar=silu2[:, k, 0:1], in1=racc[:, :],
                                           op0=mult, op1=add).then_inc(S["rest_acc"], 1)

            def rotate_key(kh):
                slot_read(dve, A_K + 2 * kh)
                kx = kout[kh][:, CTX:]
                v.tensor_tensor(kx, kf[:, :], cosA[:, :], mult).then_inc(S["k_rope"], 1)
                dve.wait_ge(k_swap[kh], 64)
                v.tensor_tensor(ks[:, :], ks[:, :], sinA[:, :], mult).then_inc(S["k_rope"], 1)
                dve.wait_ge(S["k_rope"], 3 * kh + 2)
                v.tensor_tensor(kx, kx, ks[:, :], add).then_inc(S["k_rope"], 1)

            for e in range(2):
                dve.wait_ge(xT_stored[e], 16 * XT // 2)
            for k in range(6):
                add_rest(k)
            dve.wait_ge(S["rope_loaded"], 32)
            rotate_key(0)
            add_rest(6)
            rotate_key(1)
            add_rest(7)

            def convolve(c, e):
                dve.wait_ge(S["xc_centre"], 2 * c + 2)

                def in_order(ins, j):
                    ins.then_inc(S["xc_ready"], 1)
                    dve.wait_ge(S["xc_ready"], 2 * c + (1 if j == 0 else 2))
                taps(lambda a, b: xc[e][:, CTX + a:CTX + b], acc[1][:, :], SEQ,
                     lambda j: colat(pcol, C_LCW + KC * j, c), acc_read[1], in_order)

            def split_conv(c, e):
                slot_read(dve, A_S1, 2, c)
                if not (isinstance(c, int) and c == 0):
                    dve.wait_ge(S["gate_full"], 4 * c)
                v.tensor_copy(xch[:, :], xc[e][:, :]).then_inc(S["xc_hi"], 1)
                dve.wait_ge(S["xc_hi"], c + 1)
                v.tensor_tensor(xcl[:, :], xc[e][:, :], xch[:, :], sub).then_inc(S["xc_lo"], 1)

            def radicands(c):
                for d in range(2):
                    dve.wait_ge(S["sq2_done"], 2 * c + d + 1)
                    dve.wait_ge(S["th_done"], 2 * c + d + 1)
                    v.scalar_tensor_tensor(out=qq[d][:, :], in0=qq[d][:, :], scalar=1.0, in1=sr[d][:, :], op0=add, op1=mult)\
                        .then_inc(S["m_done"], 1)

            def recur(c):
                for d in range(2):
                    dve.wait_ge(S["root_done"], 2 * c + d + 1)
                    dve.wait_ge(S["ix_done"], 2 * c + d + 1)
                    v.tensor_tensor(qq[d][:, :], qq[d][:, :], si[d][:, :], mult).then_inc(S["b_done"], 1)
                    dve.wait_ge(S["b_done"], 2 * c + d + 1)
                    if d == 0:
                        part = (lambda t: t[:, 0:CTX]), (lambda t: t[:, CTX:ALL]), aa[0][:, CTX - 1:CTX]
                    else:
                        part = (lambda t: t[:, CTX - 1::-1]), (lambda t: t[:, ALL - 1:CTX - 1:-1]), aa[1][:, 0:1]
                    v.tensor_tensor_scan(part[0](aa[d]), part[0](aa[d]), part[0](qq[d]), 0.0, mult, add)\
                        .then_inc(S["scan_done"], 1)
                    dve.wait_ge(S["scan_done"], 4 * c + 2 * d + 1)
                    v.tensor_tensor_scan(part[1](aa[d]), part[1](aa[d]), part[1](qq[d]), part[2], mult, add)\
                        .then_inc(S["scan_done"], 1)
                dve.wait_ge(S["scan_done"], 4 * c + 4)
                v.tensor_tensor(aa[0][:, CTX:], aa[0][:, CTX:], aa[1][:, CTX:], add).then_inc(S["y_done"], 1)
                dve.wait_ge(S["y_done"], 2 * c + 1)
                slot_read(dve, A_S1 + 1, 2, c)
                v.tensor_tensor(chunk(Y, c), aa[0][:, CTX:], chunk(Y, c), mult).then_inc(S["y_done"], 1)

            convolve(0, 0)
            dve.wait_ge(S["rest_sum"], 1)
            v.tensor_tensor(rest[:, :, :], gp[:, 0:8 * KC].rearrange("p (j e) -> p j e", e=2)[:, :, 0].rearrange("p (a k) -> p a k", a=4),
                            pcol[:, C_BMOD + 2 * KC:C_BMOD + 6 * KC].rearrange("p (a k) -> p a k", a=4), add).then_inc(S["rest_ready"], 1)
            dve.wait_ge(S["rest_ready"], 1)
            link(v.scalar_tensor_tensor(out=a2col[:, :], in0=rest[:, 2, :], scalar=1.0, in1=pcol[:, C_N2:C_N2 + KC],
                                        op0=add, op1=mult))

            def chunk_step(i, e):
                split_conv(i - 1, 1 - e)
                if not isinstance(i, int):
                    recur(i - 2)
                convolve(i, e)
                radicands(i - 1)

            pairs(dve, chunk_step)
            split_conv(KC - 1, 1)
            recur(KC - 2)
            radicands(KC - 1)
            recur(KC - 1)

            def low(dst, src, hi, hi_sem, lo_sem, c):
                dve.wait_ge(S[hi_sem], c + 1)
                v.tensor_tensor(dst[:, c, :], src[:, c, :], hi[:, c, :], sub).then_inc(S[lo_sem], 1)

            dve.wait_ge(S["y_done"], 2 * KC)
            for c in range(KC):
                if c not in NORM_ON_POOL:
                    low(y_lo, Y, y_hi, "y_hi_s", "y_lo_s", c)

            def gated_branch(s, gate_use, use, per=0, i=0, stored=0):
                slot_read(dve, gate_use, per, i)
                full(dve, use, per, i)
                if not isinstance(stored, int) or stored > 0:
                    dve.wait_ge(t1_stored[s], stored)
                e = use % 2
                v.tensor_tensor(t1[s][:, :], acc[e][:, :], sg[s][:, :], mult).then_inc(acc_read[e], 1)

            for s in range(2):
                gated_branch(s, A_S2 + s, A_S2 + 2 + 2 * s)
            with dve.Fori(1, KC // 2 - 1) as i:
                for s in range(2):
                    gated_branch(s, A_S2 - 1 + 2 * s, A_S2 + 2 + 2 * s, 4, i, 16 * i)
            gated_branch(0, A_S2 + 11, A_S2 + 14, stored=16 * (KC // 2 - 1))
            gated_branch(1, A_S2 + 13, A_S2 + 15, stored=16 * (KC // 2 - 1))

            def rotate_queries(i, meanwhile=None):
                for s in range(2):
                    h = 2 * i + s
                    slot_read(dve, A_Q + s, 2, i)
                    yh = chunk(yq, h)
                    v.tensor_tensor(yh, qf[:, :], cosQ[:, :], mult).then_inc(S["q_cos"], 1)
                    if meanwhile and s == 1:
                        meanwhile()
                    dve.wait_ge(S["q_swap"], 64 * h + 64)
                    v.tensor_tensor(qs[:, :], qs[:, :], sinQ[:, :], mult).then_inc(S["q_sin"], 1)
                    dve.wait_ge(S["q_cos"], h + 1)
                    dve.wait_ge(S["q_sin"], h + 1)
                    v.tensor_tensor(yh, yh, qs[:, :], add).then_inc(S["q_rope"], 1)

            dve.wait_ge(S["rope_loaded"], 64)
            dve.wait_ge(S["y_lo_s"], KC - len(NORM_ON_POOL))
            dve.wait_ge(S["y_lo_pool"], len(NORM_ON_POOL))
            rotate_queries(0)
            with dve.Fori(1, KC // 2 - 1) as i:
                rotate_queries(i)
            dve.wait_ge(S["k_hi_s"], 1)
            v.tensor_tensor(klo[:, :, :], kff[:, :, :], khi[:, :, :], sub).then_inc(S["k_lo_s"], 1)
            v.tensor_copy(ident_b[:, :], ident[:, :]).then_inc(S["mask_b"], 1)
            v.tensor_copy(masks_b[:, :, :], masks[:, :, :]).then_inc(S["mask_b"], 1)
            def maxima(n, kh, u, h):
                pair = gp[:, 1024 * (h % 2):1024 * (h % 2) + 1024]
                dve.wait_ge(S["s_full"], 4 * u + h + 1)
                lo = 256 if is_edge(n) else 128
                v.reduce_max(smax[:, kh, h:h + 1], pair[:, lo:768], AX.X).then_inc(S["s_max"], 1)
                dve.wait_ge(S["s_max"], 4 * u + h + 1)
                hd = Q_PER_KV * kh + h
                v.tensor_scalar(negm[:, kh, h:h + 1], smax[:, kh, h:h + 1], -SCALE, nsink[:, hd:hd + 1], mult, ALU.min)\
                    .then_inc(S["s_neg"], 1)

            rotate_queries(KC // 2 - 1, lambda: [maxima(0, 0, 0, h) for h in range(2)])

            def denominators(n, kh, u):
                dve.wait_ge(S["s_neg"], 4 * u + 4)
                if not (isinstance(u, int) and u < 2):
                    dve.wait_ge(S["n_act"], 2 * u - 2)
                    dve.wait_ge(S["n_pool"], u - 1)
                v.tensor_tensor(esink[:, kh, :], negm[:, kh, :], sink[:, Q_PER_KV * kh:Q_PER_KV * (kh + 1)], add)\
                    .then_inc(S["s_es"], 1)
                dve.wait_ge(S["s_es"], 2 * u + 2)
                dve.wait_ge(S["s_exp"], 4 * u + 4)
                v.tensor_tensor(rden[:, kh, :], rsum[:, kh, :], esink[:, kh, :], add).then_inc(S["s_rden"], 1)
                dve.wait_ge(S["s_rden"], 2 * u + 1)
                v.reciprocal(rden[:, kh, :], rden[:, kh, :]).then_inc(S["s_rden"], 1)
                dve.wait_ge(S["s_rden"], 2 * u + 2)
                pr = prob[kh][:, 3, P if is_edge(n) else 0:]
                v.tensor_scalar(pr, pr, rden[:, kh, 3:4], None, mult).then_inc(S["n_dve"], 1)

            def low_block(n, kh, u, j):
                if j >= (4 if is_edge(n) else 5):
                    return
                kb = j + 1 if is_edge(n) else j
                dve.wait_ge(S["pt_hi_s"], block_base(n, u) + j + 1)
                v.tensor_tensor(pt_lo[:, kb, :], pt_bank(j), pt_hi[:, kb, :], sub)\
                    .then_inc(S["pt_lo_s"], 1)

            def attention(n, kh, u, before):
                if before:
                    maxima(n, kh, u, 0)
                    maxima(n, kh, u, 1)
                if before:
                    for j in range(3):
                        low_block(*before, j)
                maxima(n, kh, u, 2)
                if before:
                    low_block(*before, 3)
                maxima(n, kh, u, 3)
                if before:
                    low_block(*before, 4)
                denominators(n, kh, u)

            units(dve, attention, lambda n, kh, u: [low_block(n, kh, u, j) for j in range(NKB)])

            for c in range(KC):
                low(y_lo, yq, y_hi, "z_hi_s", "z_lo_s", c)

            def merge(m, s, i=0):
                slot_read(dve, A_S4 + 2 * s, 4, i)
                full(dve, A_S4 + 2 * s + 1, 4, i)
                v.tensor_tensor(sg[s][:, :], acc[0][:, :], sg[s][:, :], mult).then_inc(acc_read[0], 1)
                slot_read(dve, A_S4 + 2 * s + 1, 4, i)
                dve.wait_ge(t1_loaded[s], 16 * i + 16)
                v.tensor_tensor(chunk(yq, m), sg[s][:, :], t1[s][:, :], add).then_inc(S["merged"], 1)

            dve.wait_ge(S["z_lo_s"], KC)
            for s in range(2):
                merge(s, s)
            with dve.Fori(1, KC // 2 - 1) as i:
                for s in range(2):
                    merge(2 * i + s, s, i)
            merge(KC - 2, 0, KC // 2 - 1)
            for c in range(KC - 1):
                low(hx_lo, yq, hx_hi, "mg_hi", "mg_lo", c)
            merge(KC - 1, 1, KC // 2 - 1)
            low(hx_lo, yq, hx_hi, "mg_hi", "mg_lo", KC - 1)
            dve.wait_ge(S["mg_lo"], KC)
            for m in range(KC):
                slot, last = (A_S5 + m) % 2, m == KC - 1
                dve.wait_ge(xr_loaded[m % 2], 16 * (m // 2 + 1))
                for h in range(2 if last else 1):
                    if last and h == 0:
                        dve.wait_ge(S["x1_half"], 1)
                    else:
                        full(dve, A_S5 + m)
                    part = slice(HALF * h, HALF * (h + 1)) if last else slice(0, SEQ)
                    v.scalar_tensor_tensor(out=yq[:, m, part], in0=acc[slot][:, part], scalar=rest[:, 0, m:m + 1],
                                           in1=xres[m % 2][:, part], op0=mult, op1=add)\
                        .then_inc(S["x1_part"] if last and h == 0 else acc_read[slot], 1)

            def normed(h, k):
                part = slice(HALF * h, HALF * (h + 1))
                v.scalar_tensor_tensor(out=nrm[:, k, part], in0=yq[:, k, part], scalar=a2col[:, k:k + 1],
                                       in1=rstd[:, part], op0=mult, op1=mult).then_inc(S["n2_a"], 1)

            def normed_low(h, k):
                part = slice(HALF * h, HALF * (h + 1))
                dve.wait_ge(S["n2_hi"], KC * h + k + 1)
                v.scalar_tensor_tensor(out=y_lo[:, k, part], in0=nrm[:, k, part], scalar=rest[:, 1, k:k + 1],
                                       in1=y_hi[:, k, part], op0=add, op1=sub).then_inc(S["n2_lo"], 1)

            mine = [k for k in range(KC) if k not in NORM_ON_POOL]
            for h in range(2):
                part = slice(HALF * h, HALF * (h + 1))
                if h == 0:
                    dve.wait_ge(S["st_root"], 1)
                else:
                    slot_read(dve, A_ST2)
                v.reciprocal(rstd[:, part], rstd[:, part]).then_inc(S["st_rstd"], 1)
                dve.wait_ge(S["st_rstd"], h + 1)
                full(dve, A_S5 + KC - 1)
                normed(h, mine[0])
                for a, b in zip(mine, mine[1:]):
                    normed(h, b)
                    normed_low(h, a)
                normed_low(h, mine[-1])

            def ffn_taps(buf, slot, base, g, j, ct):
                dve.wait_ge(S["f_centre"], ct)
                v.scalar_tensor_tensor(out=buf[:, 1:SEQ], in0=acc[slot][:, 0:SEQ - 1], scalar=colat(pcol, base + j, GRP * g),
                                       in1=buf[:, 1:SEQ], op0=mult, op1=add).then_inc(S["f_conv"], 1)
                dve.wait_ge(S["f_conv"], ct)
                v.scalar_tensor_tensor(out=buf[:, 0:SEQ - 1], in0=acc[slot][:, 1:SEQ],
                                       scalar=colat(pcol, base + 4 * FC + j, GRP * g),
                                       in1=buf[:, 0:SEQ - 1], op0=mult, op1=add).then_inc(acc_read[slot], 1)

            def group(g, e, j0, i=0):
                for j in range(GRP):
                    p = GRP * g + j
                    ffn_taps(ca[j], 0, C_FCW, g, j, 2 * p + 1)
                    ffn_taps(cv[j], 1, C_FCW + FC, g, j, 2 * p + 2)
                    slot_read(dve, A_UP0 + j0 + 2 * j + 1, PER_2, i)
                    dve.wait_ge(S["f_gelu"], p + 1)
                    v.tensor_tensor(ca[j][:, :], ca[j][:, :], cv[j][:, :], mult).then_inc(S["f_prod"], 1)
                    dve.wait_ge(S["f_hi"], p + 1)
                    v.tensor_tensor(g_lo[e][:, j, :], ca[j][:, :], g_hi[e][:, j, :], sub).then_inc(S["f_lo"], 1)

            def add_down(j0, i=0):
                for m in range(KC):
                    full(dve, A_UP0 + j0 + m, PER_2, i)
                    s = (A_UP0 + j0 + m) % 2
                    if not (isinstance(i, int) and j0 == 4 * GRP and i == 0):
                        slot_read(dve, A_UP0 + j0 + m - 2, PER_2, i)
                    v.scalar_tensor_tensor(out=yq[:, m, :], in0=acc[s][:, :], scalar=rest[:, 3, m:m + 1], in1=yq[:, m, :],
                                           op0=mult, op1=add).then_inc(acc_read[s], 1)

            group(0, 0, 0)
            with dve.Fori(0, NG // 2 - 1) as i:
                for e in range(2):
                    group(2 * i + 1 + e, 1 - e, 2 * GRP + e * PER_G, i)
                    add_down(4 * GRP + e * PER_G, i)
            tail = 2 * GRP + PER_2 * (NG // 2 - 1)
            group(NG - 1, 1, tail)
            add_down(tail + 2 * GRP)
            add_down(tail + PER_G)
            dve.wait_ge(S["fn_loaded"], 16)
            for t in range(XT):
                dve.wait_ge(S["o_rms"], t + 1)
                link(v.reciprocal(rstd0[:, t:t + 1], rms[:, t:t + 1]))
                v.scalar_tensor_tensor(out=otile[t][:, :], in0=o_bank(t), scalar=rstd0[:, t:t + 1], in1=fnrow[:, :],
                                       op0=mult, op1=mult).then_inc(S["o_done"], 1)


_INS = ["x", "c", "ctx", "c_ctx", "w_mod", "b_mod", "norm1_w", "w_in", "lru_conv_w", "lru_conv_b", "gate_a_w", "gate_a_b",
        "gate_x_w", "gate_x_b", "lru_lambda", "sink_logit", "w_o_rnn", "w_o_attn", "w_out", "norm2_w", "w_up", "ffn_conv_w",
        "ffn_conv_b", "w_down", "final_norm_w"]


def kernel(**inputs):
    import concourse.bacc as bacc
    from concourse.bass_utils import run_bass_kernel_spmd

    nc = bacc.Bacc("TRN2", target_bir_lowering=False, num_devices=1)
    arrays = {name: np.ascontiguousarray(inputs[name]) for name in _INS}
    cos, sin = rope_tables()
    arrays.update(ident=np.eye(P, dtype=np.float32), masks=window_masks(), rope_cos=cos, rope_sin=sin)
    dram = {n: nc.dram_tensor(f"in_{n}", a.shape, mybir.dt.from_np(a.dtype), kind="ExternalInput").ap() for n, a in arrays.items()}
    out = nc.dram_tensor("out_x", (1, SEQ, D_MODEL), mybir.dt.float32, kind="ExternalOutput").ap()
    build(nc, dram, out)
    r = run_bass_kernel_spmd(nc, [{f"in_{n}": a for n, a in arrays.items()}], core_ids=[0])
    return r.results[0]["out_x"]
```
